# Optimizing a Trainium2 kernel written in Bass

```python
import jax, jax.numpy as jnp
from jax import lax
import numpy as np

D_MODEL = 1024
BATCH = 1
SEQ = 128
DEPTH = 1
DEC_BATCH = 1
DEC_SEQ = 1024
PAST_LEN = 128

GRID_W = 64
EPS = 1e-6
NEG_INF = -1e30
N_BRANCH = 3
MIX_W = D_MODEL // 2
M_HEADS = 4
M_DH = MIX_W // M_HEADS
M_CHUNK = 128
C_GROUPS = 4
C_DG = MIX_W // C_GROUPS
C_CHUNK = 128
A_HEADS = 8
A_KV = 2
A_GROUP = A_HEADS // A_KV
A_DH = MIX_W // A_HEADS
A_KVW = A_KV * A_DH
WINDOW = 128
A_BLOCK = 128
ROPE_BASE = 10000.0
ROPE_AXIS = A_DH // 2
ROPE_FREQS = ROPE_AXIS // 2
N_KEYS = 128
N_EXPERTS = N_KEYS * N_KEYS
PEER_HEADS = 8
PEER_DK = 256
PEER_TOPK = 16
PEER_BLOCK = 128
IN_W = 7 * MIX_W + 4 * M_HEADS + 2 * A_KVW

kernel_name = 'hybrid_mlstm_gmlp_swa_peer_diffusion_step'

def rms_norm(x, g=None):
    xf = x.astype(jnp.float32)
    y = xf * lax.rsqrt(jnp.mean(xf * xf, axis=-1, keepdims=True) + EPS)
    if g is not None:
        y = y * g.astype(jnp.float32)
    return y.astype(x.dtype)

def axial_rope(x):
    n = x.shape[1]
    rows = n // GRID_W
    t_row = jnp.repeat(jnp.arange(rows), GRID_W)
    t_col = jnp.tile(jnp.arange(GRID_W), rows)
    freqs = ROPE_BASE ** (-jnp.arange(ROPE_FREQS, dtype=jnp.float32) / ROPE_FREQS)

    def rot(xh, pos):
        ang = pos.astype(jnp.float32)[:, None] * freqs[None, :]
        cos = jnp.cos(ang)[None, :, None, :]
        sin = jnp.sin(ang)[None, :, None, :]
        x1, x2 = xh[..., :ROPE_FREQS], xh[..., ROPE_FREQS:]
        return jnp.concatenate([x1 * cos - x2 * sin, x2 * cos + x1 * sin], axis=-1)

    xf = x.astype(jnp.float32)
    out = jnp.concatenate([rot(xf[..., :ROPE_AXIS], t_row), rot(xf[..., ROPE_AXIS:], t_col)], axis=-1)
    return out.astype(x.dtype)

def _attend(qb, k_ctx, v_ctx, sink, k_loc=None, v_loc=None, mask=None):
    f32 = jnp.float32
    scale = A_DH ** -0.5
    B, Q = qb.shape[0], qb.shape[1]
    lc = k_ctx.shape[1]
    sink_col = jnp.broadcast_to(sink.astype(f32).reshape(1, A_KV, A_GROUP, 1, 1), (B, A_KV, A_GROUP, Q, 1))
    s_ctx = jnp.einsum('bqkgd,bjkd->bkgqj', qb, k_ctx, preferred_element_type=f32) * scale
    parts = [sink_col, s_ctx]
    if k_loc is not None:
        s_loc = jnp.einsum('bqkgd,bjkd->bkgqj', qb, k_loc, preferred_element_type=f32) * scale
        parts.append(jnp.where(mask[None, None, None], s_loc, NEG_INF))
    p = jax.nn.softmax(jnp.concatenate(parts, axis=-1), axis=-1)
    out = jnp.einsum('bkgqj,bjkd->bqkgd', p[..., 1:1 + lc], v_ctx.astype(f32))
    if k_loc is not None:
        out = out + jnp.einsum('bkgqj,bjkd->bqkgd', p[..., 1 + lc:], v_loc.astype(f32))
    return out.astype(qb.dtype)

def context_attention(q, k, v, sink):
    B, L = q.shape[:2]
    nb = L // A_BLOCK
    qb = q.reshape(B, nb, A_BLOCK, A_KV, A_GROUP, A_DH).swapaxes(0, 1)
    out = lax.map(lambda qi: _attend(qi, k, v, sink), qb)
    return out.swapaxes(0, 1).reshape(B, L, MIX_W)

def latent_attention(q, k, v, k_ctx, v_ctx, sink):
    B, S = q.shape[:2]
    nb = S // A_BLOCK
    qb = q.reshape(B, nb, A_BLOCK, A_KV, A_GROUP, A_DH).swapaxes(0, 1)
    pad = ((0, 0), (A_BLOCK, A_BLOCK), (0, 0), (0, 0))
    kp = jnp.pad(k, pad)
    vp = jnp.pad(v, pad)

    def blk(args):
        i, qi = args
        start = i * A_BLOCK
        kw = lax.dynamic_slice_in_dim(kp, start, 3 * A_BLOCK, axis=1)
        vw = lax.dynamic_slice_in_dim(vp, start, 3 * A_BLOCK, axis=1)
        kpos = start - A_BLOCK + jnp.arange(3 * A_BLOCK)
        qpos = start + jnp.arange(A_BLOCK)
        mask = (jnp.abs(qpos[:, None] - kpos[None, :]) <= WINDOW) & (kpos >= 0)[None, :] & (kpos < S)[None, :]
        return _attend(qi, k_ctx, v_ctx, sink, kw, vw, mask)

    out = lax.map(blk, (jnp.arange(nb), qb))
    return out.swapaxes(0, 1).reshape(B, S, MIX_W)

def mlstm_chunked(q, k, v, li, lf, C0, n0, m0):
    B, S = q.shape[:2]
    nc = S // M_CHUNK

    def seq_chunks(a):
        return a.reshape(B, nc, M_CHUNK, M_HEADS, M_DH).transpose(1, 0, 3, 2, 4)

    def gate_chunks(a):
        return a.reshape(B, nc, M_CHUNK, M_HEADS).transpose(1, 0, 3, 2)

    lower = jnp.tril(jnp.ones((M_CHUNK, M_CHUNK), dtype=bool))

    def step(carry, inp):
        C, n, m = carry
        qc, kc, vc, lic, lfc = inp
        b = jnp.cumsum(lfc, axis=-1)
        a = b + m[..., None]
        dmat = jnp.where(lower, b[..., :, None] - b[..., None, :] + lic[..., None, :], -jnp.inf)
        m_t = jnp.maximum(a, jnp.max(dmat, axis=-1))
        w = jnp.exp(dmat - m_t[..., None])
        w0 = jnp.exp(a - m_t)
        s = w * jnp.einsum('bhtd,bhsd->bhts', qc, kc)
        num = w0[..., None] * jnp.einsum('bhde,bhte->bhtd', C, qc) + jnp.einsum('bhts,bhsd->bhtd', s, vc)
        den = w0 * jnp.einsum('bhe,bhte->bht', n, qc) + jnp.sum(s, axis=-1)
        h = num / jnp.maximum(jnp.abs(den), jnp.exp(-m_t))[..., None]
        m_end = m_t[..., -1]
        w_end = w[..., -1, :]
        w0_end = w0[..., -1]
        C_new = w0_end[..., None, None] * C + jnp.einsum('bhs,bhsd,bhse->bhde', w_end, vc, kc)
        n_new = w0_end[..., None] * n + jnp.einsum('bhs,bhse->bhe', w_end, kc)
        return (C_new, n_new, m_end), h

    (C, n, m), h = lax.scan(step, (C0, n0, m0),
                            (seq_chunks(q), seq_chunks(k), seq_chunks(v), gate_chunks(li), gate_chunks(lf)))
    h = h.transpose(1, 0, 3, 2, 4).reshape(B, S, M_HEADS, M_DH)
    return h, C, n, m

def mlstm_bidir(q, k, v, g, C0, n0, m0):
    li_f, lf_f = g[:, :, 0], jax.nn.log_sigmoid(g[:, :, 1])
    li_b, lf_b = g[:, :, 2], jax.nn.log_sigmoid(g[:, :, 3])
    h_f, C_f, n_f, m_f = mlstm_chunked(q, k, v, li_f, lf_f, C0[:, 0], n0[:, 0], m0[:, 0])
    fl = lambda a: jnp.flip(a, axis=1)
    h_b, C_b, n_b, m_b = mlstm_chunked(fl(q), fl(k), fl(v), fl(li_b), fl(lf_b), C0[:, 1], n0[:, 1], m0[:, 1])
    return (h_f + fl(h_b), jnp.stack([C_f, C_b], axis=1), jnp.stack([n_f, n_b], axis=1),
            jnp.stack([m_f, m_b], axis=1))

def chunk_mlp(u, v, w_s, b_s):
    B, S = u.shape[:2]
    nc = S // C_CHUNK
    vr = rms_norm(v).reshape(B, nc, C_CHUNK, C_GROUPS, C_DG)
    z = jnp.einsum('gpq,bnqgc->bnpgc', w_s, vr) + b_s.T[None, None, :, :, None]
    return u * z.reshape(B, S, MIX_W)

def peer(x, w_q, keys, u_tab, v_tab):
    B, S, D = x.shape
    T = B * S
    xt = x.reshape(T, D)
    q = (xt @ w_q).reshape(T, PEER_HEADS, 2, PEER_DK // 2)
    s = jnp.einsum('thpd,hpkd->thpk', q, keys, preferred_element_type=jnp.float32)
    v1, i1 = lax.top_k(s[:, :, 0], PEER_TOPK)
    v2, i2 = lax.top_k(s[:, :, 1], PEER_TOPK)
    cand = (v1[..., :, None] + v2[..., None, :]).reshape(T, PEER_HEADS, PEER_TOPK * PEER_TOPK)
    vs, ic = lax.top_k(cand, PEER_TOPK)
    e1 = jnp.take_along_axis(i1, ic // PEER_TOPK, axis=-1)
    e2 = jnp.take_along_axis(i2, ic % PEER_TOPK, axis=-1)
    nb = T // PEER_BLOCK
    ids = (e1 * N_KEYS + e2).reshape(nb, PEER_BLOCK, PEER_HEADS * PEER_TOPK)
    gw = jax.nn.softmax(vs, axis=-1).reshape(nb, PEER_BLOCK, PEER_HEADS * PEER_TOPK)
    xb = xt.reshape(nb, PEER_BLOCK, D)

    def blk(args):
        xi, ii, gi = args
        act = jax.nn.gelu(jnp.einsum('tkd,td->tk', u_tab[ii], xi, preferred_element_type=jnp.float32))
        return jnp.einsum('tk,tkd->td', (gi * act).astype(x.dtype), v_tab[ii])

    return lax.map(blk, (xb, ids, gw)).reshape(B, S, D)

def token_mixer(h, P, ctx):
    B, S, _ = h.shape
    f32 = jnp.float32
    z = h @ P['w_in']
    sizes = [MIX_W] * 4 + [4 * M_HEADS] + [MIX_W] * 3 + [A_KVW] * 2
    qm, km, vm, om, gm, uc, vc, qa, ka, va = jnp.split(z, np.cumsum(sizes)[:-1].tolist(), axis=-1)
    hd = (B, S, M_HEADS, M_DH)
    q_m = qm.reshape(hd).astype(f32)
    k_m = km.reshape(hd).astype(f32) * (M_DH ** -0.5)
    v_m = vm.reshape(hd).astype(f32)
    g = gm.reshape(B, S, 4, M_HEADS).astype(f32) + P['b_gates_m'].astype(f32)
    if ctx is None:
        C0 = jnp.zeros((B, 2, M_HEADS, M_DH, M_DH), f32)
        n0 = jnp.zeros((B, 2, M_HEADS, M_DH), f32)
        m0 = jnp.zeros((B, 2, M_HEADS), f32)
    else:
        C0, n0, m0 = ctx[2].astype(f32), ctx[3].astype(f32), ctx[4].astype(f32)
    h_m, C, n, m = mlstm_bidir(q_m, k_m, v_m, g, C0, n0, m0)
    y_m = rms_norm(h_m, P['g_mlstm']).reshape(B, S, MIX_W).astype(h.dtype) * jax.nn.sigmoid(om)
    y_c = chunk_mlp(uc, vc, P['w_spatial'], P['b_spatial'])
    q_a = qa.reshape(B, S, A_HEADS, A_DH)
    k_a = ka.reshape(B, S, A_KV, A_DH)
    v_a = va.reshape(B, S, A_KV, A_DH)
    if ctx is None:
        y_a = context_attention(q_a, k_a, v_a, P['sink'])
        new = (k_a, v_a, C, n, m)
    else:
        y_a = latent_attention(axial_rope(q_a), axial_rope(k_a), v_a, ctx[0], ctx[1], P['sink'])
        new = None
    gate = jax.nn.sigmoid(h @ P['w_merge'] + P['b_merge']).reshape(B, S, N_BRANCH, D_MODEL)
    br = jnp.stack([y_m, y_c.astype(h.dtype), y_a.astype(h.dtype)], axis=2)
    proj = jnp.einsum('bsnm,nmd->bsnd', br, P['w_branch'])
    out = jnp.sum(gate * proj, axis=2) @ P['w_out']
    return out, new

def layer(x, cond, P, ctx):
    mod = jax.nn.silu(cond) @ P['w_ada'] + P['b_ada']
    sh1, sc1, g1, sh2, sc2, g2 = jnp.split(mod, 6, axis=-1)
    h = rms_norm(x, P['g_norm1']) * (1 + sc1) + sh1
    y, new = token_mixer(h, P, ctx)
    x = x + g1 * y
    h2 = rms_norm(x, P['g_norm2']) * (1 + sc2) + sh2
    x = x + g2 * peer(h2, P['w_peer_q'], P['peer_keys'], P['peer_u'], P['peer_v'])
    return x, new

def setup_inputs(seed: int = 0) -> dict:
    key = jax.random.key(seed)
    ks = jax.random.split(key, 32)
    f32 = jnp.float32
    D = D_MODEL

    def nrm(k, shape, scale):
        return jax.random.normal(k, shape, f32) * scale

    f_bias = jnp.linspace(3.0, 6.0, M_HEADS, dtype=f32)
    gate_offsets = jnp.stack([jnp.zeros_like(f_bias), f_bias, jnp.zeros_like(f_bias), f_bias], axis=0)
    return {
        'x_prompt': nrm(ks[0], (BATCH, SEQ, D), 1.0),
        'x_sample': nrm(ks[1], (DEC_BATCH, DEC_SEQ, D), 1.0),
        'cache_k': nrm(ks[2], (DEC_BATCH, DEPTH, PAST_LEN, A_KV, A_DH), 1.0),
        'cache_v': nrm(ks[3], (DEC_BATCH, DEPTH, PAST_LEN, A_KV, A_DH), 1.0),
        'state_C': nrm(ks[4], (DEC_BATCH, DEPTH, 2, M_HEADS, M_DH, M_DH), 0.05),
        'state_n': nrm(ks[5], (DEC_BATCH, DEPTH, 2, M_HEADS, M_DH), 0.5),
        'state_m': nrm(ks[6], (DEC_BATCH, DEPTH, 2, M_HEADS), 1.0),
        'c': nrm(ks[7], (DEC_BATCH, D), 1.0),
        'c_ctx': nrm(ks[8], (D,), 1.0),
        'w_ada': nrm(ks[9], (DEPTH, D, 6 * D), D ** -0.5),
        'b_ada': nrm(ks[10], (DEPTH, 6 * D), 0.02),
        'g_norm1': 1.0 + nrm(ks[11], (DEPTH, D), 0.05),
        'g_norm2': 1.0 + nrm(ks[12], (DEPTH, D), 0.05),
        'w_in': nrm(ks[13], (DEPTH, D, IN_W), D ** -0.5),
        'b_gates_m': gate_offsets[None] + nrm(ks[14], (DEPTH, 4, M_HEADS), 0.1),
        'g_mlstm': 1.0 + nrm(ks[15], (DEPTH, M_HEADS, M_DH), 0.05),
        'w_spatial': nrm(ks[16], (DEPTH, C_GROUPS, C_CHUNK, C_CHUNK), C_CHUNK ** -0.5),
        'b_spatial': 1.0 + nrm(ks[17], (DEPTH, C_GROUPS, C_CHUNK), 0.05),
        'sink': nrm(ks[18], (DEPTH, A_HEADS), 0.5),
        'w_branch': nrm(ks[19], (DEPTH, N_BRANCH, MIX_W, D), MIX_W ** -0.5),
        'w_merge': nrm(ks[20], (DEPTH, D, N_BRANCH * D), D ** -0.5),
        'b_merge': nrm(ks[21], (DEPTH, N_BRANCH * D), 0.02),
        'w_out': nrm(ks[22], (DEPTH, D, D), D ** -0.5),
        'w_peer_q': nrm(ks[23], (DEPTH, D, PEER_HEADS * PEER_DK), D ** -0.5),
        'peer_keys': nrm(ks[24], (DEPTH, PEER_HEADS, 2, N_KEYS, PEER_DK // 2), (PEER_DK // 2) ** -0.5),
        'peer_u': nrm(ks[25], (DEPTH, N_EXPERTS, D), D ** -0.5),
        'peer_v': nrm(ks[26], (DEPTH, N_EXPERTS, D), 0.5),
        'g_final': 1.0 + nrm(ks[27], (D,), 0.05),
    }

def reference(x_prompt, x_sample, cache_k, cache_v, state_C, state_n, state_m, c, c_ctx,
              w_ada, b_ada, g_norm1, g_norm2, w_in, b_gates_m, g_mlstm, w_spatial, b_spatial, sink,
              w_branch, w_merge, b_merge, w_out, w_peer_q, peer_keys, peer_u, peer_v, g_final):
    cond_ctx = c_ctx[None, None, :]
    cond_lat = c[:, None, :]
    xp = x_prompt
    xs = x_sample
    ks_, vs_, Cs_, ns_, ms_ = [], [], [], [], []
    for l in range(DEPTH):
        P = {'w_ada': w_ada[l], 'b_ada': b_ada[l], 'g_norm1': g_norm1[l], 'g_norm2': g_norm2[l],
             'w_in': w_in[l], 'b_gates_m': b_gates_m[l], 'g_mlstm': g_mlstm[l],
             'w_spatial': w_spatial[l], 'b_spatial': b_spatial[l], 'sink': sink[l],
             'w_branch': w_branch[l], 'w_merge': w_merge[l], 'b_merge': b_merge[l], 'w_out': w_out[l],
             'w_peer_q': w_peer_q[l], 'peer_keys': peer_keys[l], 'peer_u': peer_u[l], 'peer_v': peer_v[l]}
        xp, (k_l, v_l, C_l, n_l, m_l) = layer(xp, cond_ctx, P, None)
        ks_.append(k_l)
        vs_.append(v_l)
        Cs_.append(C_l)
        ns_.append(n_l)
        ms_.append(m_l)
        ctx = (cache_k[:, l], cache_v[:, l], state_C[:, l], state_n[:, l], state_m[:, l])
        xs, _ = layer(xs, cond_lat, P, ctx)
    y_prompt = rms_norm(xp, g_final)
    y_sample = rms_norm(xs, g_final)
    new_cache_k = jnp.stack(ks_, axis=1)
    new_cache_v = jnp.stack(vs_, axis=1)
    new_state_C = jnp.stack(Cs_, axis=1)
    new_state_n = jnp.stack(ns_, axis=1)
    new_state_m = jnp.stack(ms_, axis=1)
    return (y_prompt, y_sample, new_cache_k, new_cache_v, new_state_C, new_state_n, new_state_m)


_drawn_inputs = setup_inputs


def setup_inputs(seed=0):
    import zlib

    import numpy as np

    out = dict(_drawn_inputs(seed))
    spreads = {}
    factors = {'state_C': 8.0,
     'state_n': 4.833,
     'state_m': 5.424,
     'g_mlstm': 3.543,
     'sink': 8.0,
     'b_merge': 5.276,
     'cache_k': 2.677}
    for name, (base, spread) in spreads.items():
        noise = np.random.default_rng([zlib.crc32(name.encode()), seed]).standard_normal(out[name].shape)
        drawn = base * np.exp(spread * noise) if base else spread * noise
        out[name] = __import__('jax').numpy.asarray(drawn.astype(out[name].dtype))
    for name, factor in factors.items():
        out[name] = (out[name] * factor).astype(out[name].dtype)
    return out
```

```python
from contextlib import ExitStack

import numpy as np

import concourse.bass as bass
from concourse import mybir

F32 = mybir.dt.float32
U32 = mybir.dt.uint32
ALU = mybir.AluOpType
ACT = mybir.ActivationFunctionType
AX_X = mybir.AxisListType.X

P = 128
D = 1024
DC = D // P
LAT = 8
TILES = 1 + LAT
EPS = 1e-6
MIX = D // 2
MH, MD = 4, 128
AH, AKV, AD = 8, 2, 64
IN_W = 7 * MIX + 4 * MH + 2 * AKV * AD
NEXP = 16384
PH, TOPK = 8, 16
PICKS = PH * TOPK
GRID_W = 64
NEG = -1e30
BIG = -3.0e38


class Steps:

    def __init__(self, eng, sem):
        self.eng, self.sem, self.base, self.n, self.i, self.per = eng, sem, 0, 0, None, 0

    def enter(self, i, per):
        self.base, self.n, self.i, self.per = self.base + self.n, 0, i, per

    def leave(self, turns):
        assert self.n == self.per, f"{self.sem}: {self.n} steps a turn, {self.per} said"
        self.base, self.n, self.i = self.base + self.per * turns, 0, None

    def value(self):
        flat = self.base + self.n
        return flat if self.i is None else self.i * self.per + flat

    def link(self, ins):
        ins.then_inc(self.sem, 1)
        self.n += 1
        self.eng.wait_ge(self.sem, self.value())


def is_first(t):
    return isinstance(t, int) and t == 0


def cols(ap, a, n):
    return ap[:, bass.ds(a, n)]


def row(ap, t):
    return ap[bass.ds(t, 1)].rearrange("a p n -> (a p) n")


def host_constants():
    n = LAT * P
    pos = np.arange(n)
    freqs = 10000.0 ** (-np.arange(16, dtype=np.float32) / 16)
    tabs = []
    for axis in (pos // GRID_W, pos % GRID_W):
        ang = axis.astype(np.float32)[:, None] * freqs[None, :].astype(np.float32)
        tabs.append((np.cos(ang), np.sin(ang)))
    cos = np.concatenate([tabs[0][0], tabs[0][0], tabs[1][0], tabs[1][0]], 1).astype(np.float32)
    sin = np.concatenate([-tabs[0][1], tabs[0][1], -tabs[1][1], tabs[1][1]], 1).astype(np.float32)
    rope = np.concatenate([cos, sin], 1).reshape(LAT, P, 2 * AD)
    q, k = np.arange(P)[:, None], np.arange(3 * P)[None, :] - P
    band = np.where(np.abs(q - k) <= P, 0.0, NEG * 8)
    win = np.zeros((LAT, P, 4 * P), np.float32)
    for t in range(LAT):
        win[t, :, P:] = band
        if t == 0:
            win[t, :, P:2 * P] = NEG * 8
        if t == LAT - 1:
            win[t, :, 3 * P:] = NEG * 8
    s, tt = np.arange(P)[:, None], np.arange(P)[None, :]
    causal = np.stack([np.where(s <= tt, 0.0, NEG), np.where(s >= tt, 0.0, NEG)]).astype(np.float32)
    restart = np.ones((MH, 2, TILES, P), np.float32)
    restart[:, 0, :, 0] = 0.0
    restart[:, 1, :, P - 1] = 0.0
    head_row = np.zeros((MH, MH, P), np.float32)
    for h in range(MH):
        head_row[h, h] = 1.0
    return {
        "const_ident": np.eye(P, dtype=np.float32), "const_rope": rope, "const_window": win,
        "const_causal": causal, "const_restart": restart.reshape(MH, -1),
        "const_head_row": head_row.reshape(MH, -1),
        "const_iota": np.tile(np.arange(TOPK, dtype=np.float32), (P, 1)),
    }


def modulate(nc, T):
    NB = 6 * D // 512
    with nc.cleanup_on_exit(), ExitStack() as ctx:
        sb = lambda n, s, d=F32: ctx.enter_context(nc.sbuf_tensor(n, s, d))
        sem = nc.alloc_semaphore
        cond = sb("mo_cond", [P, 2, DC])
        act = sb("mo_silu", [P, DC, 2])
        wa = [sb(f"mo_w{u}", [P, DC, 512]) for u in range(2)]
        bias = sb("mo_bias", [2, 6 * D])
        mod = sb("mo_mod", [2, 6 * D])
        ps = [ctx.enter_context(nc.psum_tensor(f"mo_ps{u}", [P, 512], F32)) for u in range(2)]
        cond_in, bias_in, silu_done = sem("mo_cond_in"), sem("mo_bias_in"), sem("mo_silu_done")
        w_in_ = [sem(f"mo_w_in{u}") for u in range(2)]
        prod, mod_done, stored = sem("mo_prod"), sem("mo_mod_done"), sem("mo_stored")
        w_view = T["w_ada"][0].rearrange("(k p) n -> p k n", p=P)
        block = ctx.enter_context(nc.Block())

        @block.sync
        def _(sp):
            sp.dma_start(cond[:, 0, :], T["c_ctx"].rearrange("(k p) -> p k", p=P), allow_slow_non_contiguous=True).then_inc(cond_in, 16)
            sp.dma_start(cond[:, 1, :], T["c"][0].rearrange("(k p) -> p k", p=P), allow_slow_non_contiguous=True).then_inc(cond_in, 16)
            sp.dma_start(bias[:], T["b_ada"].to_broadcast([2, 6 * D])).then_inc(bias_in, 16)
            for u in range(2):
                sp.dma_start(wa[u][:], w_view[:, :, u * 512:u * 512 + 512]).then_inc(w_in_[u], 16)
            with sp.Fori(1, NB // 2) as i:
                for u in range(2):
                    sp.wait_ge(prod, 2 * i + u - 1)
                    sp.dma_start(wa[u][:], w_view[:, :, bass.ds((2 * i + u) * 512, 512)]).then_inc(w_in_[u], 16)
            sp.wait_ge(mod_done, NB)
            sp.dma_start(T["mod"], mod[:]).then_inc(stored, 16)
            sp.wait_ge(stored, 16)

        @block.scalar
        def _(act_eng):
            act_eng.wait_ge(cond_in, 32)
            nc.scalar.activation(act[:].rearrange("p k c -> p c k"), cond[:], ACT.Silu).then_inc(silu_done, 1)

        @block.tensor
        def _(pe):
            pe.wait_ge(silu_done, 1)

            def column_block(i, u, first):
                pe.wait_ge(w_in_[u], 16 * i + 16)
                if not first:
                    pe.wait_ge(mod_done, 2 * i + u - 1)
                for k in range(DC):
                    mm = nc.tensor.matmul(ps[u][0:2, :], act[:, k, :], wa[u][:, k, :], start=(k == 0), stop=(k == DC - 1))
                mm.then_inc(prod, 1)

            column_block(0, 0, True)
            column_block(0, 1, True)
            with pe.Fori(1, NB // 2) as i:
                for u in range(2):
                    column_block(i, u, False)

        @block.vector
        def _(dve):
            dve.wait_ge(bias_in, 16)
            with dve.Fori(0, NB // 2) as i:
                for u in range(2):
                    dve.wait_ge(prod, 2 * i + u + 1)
                    at = (2 * i + u) * 512
                    nc.vector.tensor_tensor(cols(mod, at, 512), ps[u][0:2, :], cols(bias, at, 512),
                                            ALU.add).then_inc(mod_done, 1)


def load_norm_rows(sp, T, scale_t, shift_t, gain_t, row, sc_col, sh_col, gain, done):
    sp.dma_start(scale_t, T["mod"][row:row + 1, sc_col * D:(sc_col + 1) * D].to_broadcast([P, D])).then_inc(done, 16)
    sp.dma_start(shift_t, T["mod"][row:row + 1, sh_col * D:(sh_col + 1) * D].to_broadcast([P, D])).then_inc(done, 16)
    sp.dma_start(gain_t, gain.to_broadcast([P, D])).then_inc(done, 16)


Q0, K0, V0, O0, G0, U0, S0, A0 = 0, MIX, 2 * MIX, 3 * MIX, 4 * MIX, 4 * MIX + 16, 5 * MIX + 16, 6 * MIX + 16


def project(nc, T, keep):
    with nc.cleanup_on_exit(), ExitStack() as ctx:
        sb = lambda n, s, d=F32: ctx.enter_context(nc.sbuf_tensor(n, s, d))
        sem = nc.alloc_semaphore
        bank = lambda n: ctx.enter_context(nc.psum_tensor(n, [P, 512], F32))
        ident, gates, kat, va = keep.ident, keep.gates, keep.kat, keep.va
        w = sb("pj_w", [P, DC, IN_W])
        x = sb("pj_x", [P, D])
        h = sb("pj_h", [P, D])
        scale1, shift1 = sb("pj_scale1", [P, D]), sb("pj_shift1", [P, D])
        ht = sb("pj_ht", [P, DC, P])
        qkv = sb("pj_qkv", [P, 3 * MIX])
        og = sb("pj_og", [P, MIX])
        u = sb("pj_u", [P, MIX])
        sv = sb("pj_sv", [P, MIX])
        vr = sb("pj_vr", [P, MIX])
        yc = sb("pj_yc", [P, MIX])
        qka = sb("pj_qka", [P, MIX + 2 * AKV * AD])
        rot_c = sb("pj_rot_c", [P, 10, AD])
        rot_s = sb("pj_rot_s", [P, 10, 2, 2, 16])
        qr = sb("pj_qr", [P, 10, AD])
        qkt = sb("pj_qkt", [P, 2 * MIX])
        qat = sb("pj_qat", [AD, AH * P])
        yct = sb("pj_yct", [P, MIX])
        rope = sb("pj_rope", [P, 2 * AD])
        ws = sb("pj_ws", [P, 4, P])
        wst = sb("pj_wst", [P, 4, P])
        bs = sb("pj_bs", [P, 4])
        gb = sb("pj_gb", [P, 16])
        ss = sb("pj_ss", [P, 8])
        half = sb("pj_half", [P, 1])
        gain1 = sb("pj_gain1", [P, D])
        ps_x = ctx.enter_context(nc.psum_tensor("pj_ps_x", [P, 2, 512], F32))
        ps_z = [bank(f"pj_ps_z{b}") for b in range(3)]
        ps_t = [bank(f"pj_ps_t{b}") for b in range(2)]
        ps_m = bank("pj_ps_m")

        w_in_ = [sem(f"pj_w_in{k}") for k in range(DC)]
        rows_in, small_in, rope_in, x_in = sem("pj_rows_in"), sem("pj_small_in"), sem("pj_rope_in"), sem("pj_x_in")
        rows2_in, half_set = sem("pj_rows2_in"), sem("pj_half_set")
        ws_t, ws_done = sem("pj_ws_t"), sem("pj_ws_done")
        ss_done, ms_done, rstd_done = sem("pj_ss_done"), sem("pj_ms_done"), sem("pj_rstd_done")
        h_done, x_t, ht_done = sem("pj_h_done"), sem("pj_x_t"), sem("pj_ht_done")
        z_done, z_act, z_dve = sem("pj_z_done"), sem("pj_z_act"), sem("pj_z_dve")
        ssv_done, msv_done, rstdv_done, vr_done = sem("pj_ssv"), sem("pj_msv"), sem("pj_rstdv"), sem("pj_vr_done")
        qr_done, gm_done, yc_done = sem("pj_qr_done"), sem("pj_gm_done"), sem("pj_yc_done")
        t_done, t_out = sem("pj_t_done"), sem("pj_t_out")
        st_h, st_qa, st_qk, st_kv, st_o, st_yc, st_new = (sem(f"pj_st_{n}") for n in ("h", "qa", "qk", "kv", "o", "yc", "new"))
        step = sem("pj_dve_step")
        block = ctx.enter_context(nc.Block())

        ZB = [(A0, 512, "d"), (A0 + 512, 256, "d"), (S0, 512, "a"), (U0, 512, "a"), (Q0, 512, "d"),
              (K0, 512, "a"), (V0, 512, "d"), (O0, 512, "a"), (G0, 16, "d")]
        NZ = len(ZB)
        NT = 6
        per = {"d": sum(b[2] == "d" for b in ZB), "a": sum(b[2] == "a" for b in ZB)}
        rank = [sum(c[2] == b[2] for c in ZB[:j + 1]) for j, b in enumerate(ZB)]
        zsem = {"d": z_dve, "a": z_act}

        @block.sync
        def _(sp):
            sp.dma_start(ident[:], T["const_ident"]).then_inc(small_in, 16)
            load_norm_rows(sp, T, scale1[:], shift1[:], gain1[:], 0, 1, 0, T["g_norm1"], rows_in)
            sp.dma_start(ws[:], T["w_spatial"][0].rearrange("g p q -> p g q")).then_inc(small_in, 16)
            sp.dma_start(bs[:], T["b_spatial"][0].rearrange("g p -> p g"), allow_slow_non_contiguous=True).then_inc(small_in, 16)
            sp.dma_start(gb[:], T["b_gates_m"].rearrange("a g h -> a (g h)").to_broadcast([P, 16])).then_inc(small_in, 16)
            for k in range(DC):
                sp.dma_start(w[:, k, :], T["w_in"][0, k * P:(k + 1) * P, :]).then_inc(w_in_[k], 16)

            def stores(t):
                sp.wait_ge(ht_done, 2 * t + 2)
                sp.dma_start(row(T["ht"], t), ht[:].rearrange("p k n -> p (k n)")).then_inc(st_h, 16)
                if is_first(t):
                    sp.wait_ge(z_dve, 2)
                    sp.dma_start(T["new_k"][0, 0].rearrange("s k d -> s (k d)"), qka[:, 512:640]).then_inc(st_new, 16)
                    sp.dma_start(T["new_v"][0, 0].rearrange("s k d -> s (k d)"), qka[:, 640:768]).then_inc(st_new, 16)
                sp.wait_ge(z_act, t * per["a"] + rank[5])
                sp.wait_ge(z_dve, t * per["d"] + rank[6])
                sp.dma_start(row(T["kv"], t), qkv[:, MIX:]).then_inc(st_kv, 16)
                sp.wait_ge(z_act, t * per["a"] + rank[7])
                sp.dma_start(row(T["og"], t), og[:]).then_inc(st_o, 16)
                sp.wait_ge(t_out, t * NT + 2)
                sp.dma_start(row(T["qat"], t), qat[:]).then_inc(st_qa, 16)
                sp.wait_ge(t_out, t * NT + 5)
                sp.dma_start(row(T["qkt"], t), qkt[:]).then_inc(st_qk, 16)
                sp.wait_ge(t_out, t * NT + 6)
                sp.dma_start(row(T["yct"], t), yct[:]).then_inc(st_yc, 16)

            stores(0)
            with sp.Fori(0, LAT) as i:
                stores(i + 1)
            for s in (st_h, st_qa, st_qk, st_kv, st_o, st_yc):
                sp.wait_ge(s, 16 * TILES)

        @block.gpsimd
        def _(pool):
            nc.gpsimd.memset(half[:], -0.5).then_inc(half_set, 1)
            nc.gpsimd.memset(kat[:, :, TILES * P:], 0.0).then_inc(half_set, 1)
            nc.gpsimd.memset(va[:, TILES, :], 0.0).then_inc(half_set, 1)
            pool.wait_ge(half_set, 3)

            def rsqrt(t, ready, a, b, done):
                pool.wait_ge(ready, t + 1)
                nc.gpsimd.tensor_tensor(ss[:, b:b + 1], ss[:, a:a + 1], half[:], ALU.pow).then_inc(done, 1)

            pool.dma_start(x[:], T["x_prompt"][0]).then_inc(x_in, 16)
            rsqrt(0, ms_done, 1, 2, rstd_done)
            pool.wait_ge(h_done, 1)
            for tile_, col in ((scale1, 1), (shift1, 0)):
                pool.dma_start(tile_[:], T["mod"][1:2, col * D:(col + 1) * D].to_broadcast([P, D])).then_inc(rows2_in, 16)
            rsqrt(0, msv_done, 4, 5, rstdv_done)
            with pool.Fori(0, LAT) as i:
                pool.wait_ge(h_done, i + 1)
                pool.wait_ge(half_set, 1)
                pool.dma_start(x[:], T["x_sample"][0].rearrange("(t p) d -> t p d", p=P)[bass.ds(i, 1)].rearrange(
                    "a p d -> (a p) d")).then_inc(x_in, 16)
                rsqrt(i + 1, ms_done, 1, 2, rstd_done)
                pool.wait_ge(qr_done, i + 1)
                pool.wait_ge(half_set, 1)
                pool.dma_start(rope[:], row(T["const_rope"], i)).then_inc(rope_in, 16)
                rsqrt(i + 1, msv_done, 4, 5, rstdv_done)

        @block.tensor
        def _(pe):
            pe.wait_ge(small_in, 64)
            for g in range(4):
                tr = nc.tensor.transpose(ps_m[:, g * P:(g + 1) * P], ws[:, g, :], ident[:])
            tr.then_inc(ws_t, 1)

            def tile(t):
                pe.wait_ge(h_done, t + 1)
                if not is_first(t):
                    pe.wait_ge(ht_done, 2 * t)
                for k in range(DC):
                    tr = nc.tensor.transpose(ps_x[:, k // 4, (k % 4) * P:(k % 4 + 1) * P], h[:, k * P:(k + 1) * P], ident[:])
                    if k % 4 == 3:
                        tr.then_inc(x_t, 1)
                pe.wait_ge(ht_done, 2 * t + 2)
                for j, (c0, n, _) in enumerate(ZB):
                    if not is_first(t) or j >= 3:
                        prev = j - 3 if j >= 3 else j - 3 + NZ
                        eng = ZB[prev][2]
                        back = t if j >= 3 else t - 1
                        pe.wait_ge(zsem[eng], back * per[eng] + rank[prev])
                    for k in range(DC):
                        if is_first(t) and j == 0:
                            pe.wait_ge(w_in_[k], 16)
                        mm = nc.tensor.matmul(ps_z[j % 3][:, 0:n], ht[:, k, :], w[:, k, c0:c0 + n], start=(k == 0), stop=(k == DC - 1))
                    mm.then_inc(z_done, 1)

                def group(g, n, src, ready, value, rows=P):
                    pe.wait_ge(ready, value)
                    if not is_first(t) or g >= 2:
                        pe.wait_ge(t_out, t * NT + g - 1)
                    for a in range(n):
                        dst = ps_t[g % 2][0:rows, a * P:(a + 1) * P]
                        if rows < P:
                            tr = nc.tensor.matmul(dst, src(a), ident[:], start=True, stop=True)
                        else:
                            tr = nc.tensor.transpose(dst, src(a), ident[:])
                    tr.then_inc(t_done, 1)

                group(0, 4, lambda a: qr[:, a, :], qr_done, t + 1, AD)
                group(1, 4, lambda a: qr[:, 4 + a, :], qr_done, t + 1, AD)
                group(2, 2, lambda a: qr[:, 8 + a, :], qr_done, t + 1, AD)
                group(3, 4, lambda a: qkv[:, a * P:(a + 1) * P], z_dve, t * per["d"] + rank[4])
                group(4, 4, lambda a: qkv[:, MIX + a * P:MIX + (a + 1) * P], z_act, t * per["a"] + rank[5])
                pe.wait_ge(vr_done, t + 1)
                if is_first(t):
                    pe.wait_ge(ws_done, 1)
                else:
                    pe.wait_ge(yc_done, t)
                for g in range(4):
                    mm = nc.tensor.matmul(ps_m[:, g * P:(g + 1) * P], wst[:, g, :], vr[:, g * P:(g + 1) * P], start=True, stop=True)
                mm.then_inc(gm_done, 1)
                group(5, 4, lambda a: yc[:, a * P:(a + 1) * P], yc_done, t + 1)

            tile(0)
            with pe.Fori(0, LAT) as i:
                tile(i + 1)

        @block.scalar
        def _(act):
            act.wait_ge(ws_t, 1)
            nc.scalar.copy(wst[:].rearrange("p g q -> p (g q)"), ps_m[:]).then_inc(ws_done, 1)

            def tile(t):
                act.wait_ge(x_in, 16 * t + 16)
                if not is_first(t):
                    act.wait_ge(x_t, 2 * t)
                nc.scalar.activation(h[:], x[:], ACT.Square, accum_out=ss[:, 0:1]).then_inc(ss_done, 1)
                for b in range(2):
                    act.wait_ge(x_t, 2 * t + b + 1)
                    if not is_first(t) and b == 0:
                        act.wait_ge(z_done, NZ * t)
                        act.wait_ge(st_h, 16 * t)
                    nc.scalar.copy(ht[:].rearrange("p k n -> p (k n)")[:, b * 512:(b + 1) * 512], ps_x[:, b, :]).then_inc(ht_done, 1)
                act.wait_ge(z_done, t * NZ + 3)
                if not is_first(t):
                    act.wait_ge(vr_done, t)
                nc.scalar.copy(sv[:], ps_z[2][:]).then_inc(z_act, 1)
                if not is_first(t):
                    act.wait_ge(gm_done, t)
                act.wait_ge(z_act, t * per["a"] + 1)
                nc.scalar.activation(vr[:], sv[:], ACT.Square, accum_out=ss[:, 3:4]).then_inc(ssv_done, 1)
                act.wait_ge(z_done, t * NZ + 4)
                if not is_first(t):
                    act.wait_ge(yc_done, t)
                nc.scalar.copy(u[:], ps_z[0][:]).then_inc(z_act, 1)
                act.wait_ge(z_done, t * NZ + 6)
                if not is_first(t):
                    act.wait_ge(st_kv, 16 * t)
                nc.scalar.mul(qkv[:, MIX:2 * MIX], ps_z[2][:], MD ** -0.5).then_inc(z_act, 1)
                act.wait_ge(z_done, t * NZ + 8)
                if not is_first(t):
                    act.wait_ge(st_o, 16 * t)
                nc.scalar.activation(og[:], ps_z[1][:], ACT.Sigmoid).then_inc(z_act, 1)
                outs = [(qat[:, 0:512], ps_t[0][0:AD, :], st_qa), (qat[:, 512:1024], ps_t[1][0:AD, :], None),
                        (kat[:, :, bass.ds(t * P, P)], ps_t[0][0:AD, 0:256].rearrange("p (k n) -> p k n", k=2), None),
                        (qkt[:, 0:512], ps_t[1][:], st_qk), (qkt[:, 512:1024], ps_t[0][:], None),
                        (yct[:], ps_t[1][:], st_yc)]
                for g, (dst, src, stored) in enumerate(outs):
                    act.wait_ge(t_done, t * NT + g + 1)
                    if stored is not None and not is_first(t):
                        act.wait_ge(stored, 16 * t)
                    nc.scalar.copy(dst, src).then_inc(t_out, 1)

            tile(0)
            with act.Fori(0, LAT) as i:
                tile(i + 1)

        @block.vector
        def _(dve):
            s = Steps(dve, step)
            dve.wait_ge(rows_in, 48)
            s.link(nc.vector.scalar_tensor_tensor(out=scale1[:], in0=scale1[:], scalar=1.0, in1=gain1[:], op0=ALU.add, op1=ALU.mult))

            def tile(t):
                dve.wait_ge(ss_done, t + 1)
                nc.vector.tensor_scalar(ss[:, 1:2], ss[:, 0:1], 1.0 / D, EPS, ALU.mult, ALU.add).then_inc(ms_done, 1)
                dve.wait_ge(rstd_done, t + 1)
                s.link(nc.vector.scalar_tensor_tensor(out=h[:], in0=x[:], scalar=ss[:, 2:3], in1=scale1[:], op0=ALU.mult, op1=ALU.mult))
                nc.vector.tensor_tensor(h[:], h[:], shift1[:], ALU.add).then_inc(h_done, 1)
                dve.wait_ge(z_done, t * NZ + 1)
                nc.vector.tensor_copy(qka[:, 0:512], ps_z[0][:]).then_inc(z_dve, 1)
                dve.wait_ge(z_done, t * NZ + 2)
                nc.vector.tensor_copy(cols(va[:].rearrange("p t n -> p (t n)"), t * P, P), ps_z[1][:, P:2 * P])
                if not is_first(t):
                    dve.wait_ge(st_new, 32)
                nc.vector.tensor_copy(qka[:, 512:768], ps_z[1][:, 0:256]).then_inc(z_dve, 1)
                dve.wait_ge(z_dve, t * per["d"] + 2)
                heads = qka[:, 0:640].rearrange("p (h d) -> p h d", h=10)
                if is_first(t):
                    nc.vector.tensor_copy(qr[:], heads).then_inc(qr_done, 1)
                else:
                    dve.wait_ge(rope_in, 16 * t)
                    nc.vector.tensor_tensor(rot_c[:], heads, rope[:, 0:AD].unsqueeze(1).to_broadcast([P, 10, AD]), ALU.mult)
                    split = qka[:, 0:640].rearrange("p (h a b c) -> p h a b c", h=10, a=2, b=2)
                    sine = rope[:, AD:].rearrange("p (a b c) -> p a b c", a=2, b=2)
                    for b in range(2):
                        for a in range(2):
                            last = nc.vector.tensor_tensor(rot_s[:, :, a, b, :], split[:, :, a, 1 - b, :],
                                                           sine[:, a, b, :].unsqueeze(1).to_broadcast([P, 10, 16]), ALU.mult)
                    s.link(last)
                    nc.vector.tensor_tensor(qr[:], rot_c[:], rot_s[:].rearrange("p h a b c -> p h (a b c)"), ALU.add).then_inc(qr_done, 1)
                dve.wait_ge(ssv_done, t + 1)
                nc.vector.tensor_scalar(ss[:, 4:5], ss[:, 3:4], 1.0 / MIX, EPS, ALU.mult, ALU.add).then_inc(msv_done, 1)
                dve.wait_ge(z_done, t * NZ + 5)
                nc.vector.tensor_copy(qkv[:, 0:MIX], ps_z[1][:]).then_inc(z_dve, 1)
                dve.wait_ge(rstdv_done, t + 1)
                nc.vector.tensor_scalar(vr[:], sv[:], ss[:, 5:6], None, ALU.mult).then_inc(vr_done, 1)
                dve.wait_ge(z_done, t * NZ + 7)
                if not is_first(t):
                    dve.wait_ge(st_kv, 16 * t)
                nc.vector.tensor_copy(qkv[:, 2 * MIX:], ps_z[0][:]).then_inc(z_dve, 1)
                dve.wait_ge(z_done, t * NZ + 9)
                nc.vector.tensor_tensor(cols(gates[:].rearrange("p t g -> p (t g)"), t * 16, 16), ps_z[2][:, 0:16], gb[:], ALU.add).then_inc(z_dve, 1)
                dve.wait_ge(gm_done, t + 1)
                dve.wait_ge(z_act, t * per["a"] + 2)
                for g in range(4):
                    last = nc.vector.scalar_tensor_tensor(out=yc[:, g * P:(g + 1) * P], in0=ps_m[:, g * P:(g + 1) * P],
                                                          scalar=bs[:, g:g + 1], in1=u[:, g * P:(g + 1) * P], op0=ALU.add, op1=ALU.mult)
                last.then_inc(yc_done, 1)

            dve.wait_ge(small_in, 64)
            tile(0)
            dve.wait_ge(rows2_in, 32)
            s.link(nc.vector.scalar_tensor_tensor(out=scale1[:], in0=scale1[:], scalar=1.0, in1=gain1[:], op0=ALU.add, op1=ALU.mult))
            with dve.Fori(0, LAT) as i:
                s.enter(i, 2)
                tile(i + 1)
            s.leave(LAT)


def mlstm(nc, T, keep):
    W = MD + 1
    NCOL = TILES + 2
    PREV0 = (0, TILES)
    END0 = TILES + 1
    with nc.cleanup_on_exit(), ExitStack() as ctx:
        sb = lambda n, s, d=F32: ctx.enter_context(nc.sbuf_tensor(n, s, d))
        sem = nc.alloc_semaphore
        ident, gates, hd = keep.ident, keep.gates, keep.hd
        log_f = sb("ml_log_f", [P, TILES, 16])
        tmp = sb("ml_tmp", [P, TILES, 16])
        causal = sb("ml_causal", [P, 2, P])
        restart = sb("ml_restart", [MH, 2, TILES * P])
        head_row = sb("ml_head_row", [MH, MH, P])
        li = sb("ml_li", [MH, 2, TILES * P])
        lf = sb("ml_lf", [MH, 2, TILES * P])
        b = sb("ml_b", [MH, 2, TILES * P])
        g = sb("ml_g", [MH, 2, TILES * P])
        mx = sb("ml_mx", [MH, 2, TILES * P])
        m = sb("ml_m", [MH, 2, TILES * P])
        prev = sb("ml_prev", [MH, 2, NCOL])
        end = sb("ml_end", [MH, 2, TILES])
        col = sb("ml_col", [P, 3, 2, TILES, MH])
        prevb = sb("ml_prevb", [P, 2, MH, NCOL])
        endb = sb("ml_endb", [P, 2, MH, TILES])
        w0 = sb("ml_w0", [P, 2, TILES, MH])
        em = sb("ml_em", [P, 2, TILES, MH])
        we0 = sb("ml_we0", [P, 2, TILES, MH])
        qkt = [sb(f"ml_qkt{d}", [P, 2 * MIX]) for d in range(2)]
        kk = [sb(f"ml_k{d}", [P, MIX]) for d in range(2)]
        v1 = [sb(f"ml_v{d}", [P, MH, W]) for d in range(2)]
        cn = [sb(f"ml_cn{d}", [P, MH, W]) for d in range(2)]
        arg = sb("ml_arg", [P, MIX])
        wt = sb("ml_wt", [P, MH, P])
        pw = sb("ml_pw", [P, MIX])
        vw = sb("ml_vw", [P, MH, W])
        ic = sb("ml_ic", [P, MH, W])
        tot = sb("ml_tot", [P, MH, W])
        den = sb("ml_den", [P, MH])
        cs = sb("ml_cs", [P, 2 * MH, P])
        ps = [ctx.enter_context(nc.psum_tensor(f"ml_ps{i}", [P, 512], F32)) for i in range(2)]
        ps_i, ps_l, ps_u = (ctx.enter_context(nc.psum_tensor(f"ml_ps_{n}", [P, 2, 512], F32)) for n in "ilu")
        banks = [ps_i[:, 0, :], ps_i[:, 1, :], ps_l[:, 0, :], ps_l[:, 1, :], ps_u[:, 0, :], ps_u[:, 1, :]]

        small_in, m0_in = sem("ml_small_in"), sem("ml_m0_in")
        cell_in = [sem(f"ml_cell_in{d}") for d in range(2)]
        c0_in, n0_in, c_stored = sem("ml_c0_in"), sem("ml_n0_in"), sem("ml_c_stored")
        abs_done, exp_done, ln_done, f_done = sem("ml_abs"), sem("ml_exp"), sem("ml_ln"), sem("ml_f_done")
        rows_t, rows_out, ones_set, zero_set = sem("ml_rows_t"), sem("ml_rows_out"), sem("ml_ones"), sem("ml_zero")
        scan_done, col_t, col_out, diff_done, w_cols = (sem(f"ml_{n}") for n in ("scan", "col_t", "col_out", "diff", "w_cols"))
        mb_done, arg_done, wt_done, st_done, p_done = (sem(f"ml_{n}") for n in ("mb", "arg", "wt", "st", "p"))
        inter_done, ic_done, local_done, tot_done = (sem(f"ml_{n}") for n in ("inter", "ic", "local", "tot"))
        vw_done, upd_done, cn_done = (sem(f"ml_{n}") for n in ("vw", "upd", "cn"))
        cs_t, cs_out, c0_t, c0_out = (sem(f"ml_{n}") for n in ("cs_t", "cs_out", "c0_t", "c0_out"))
        step = sem("ml_dve_step")
        block = ctx.enter_context(nc.Block())

        def order(eng, cell, between=None):
            for d in range(2):
                cell(d, 0, d, 0)
            if between is not None:
                between()
            with eng.Fori(0, LAT) as i:
                tiles = (i + 1, LAT - i)
                eng.to_reg(tiles[1])
                for d in range(2):
                    cell(2 * i + (2 + d), i + 1, d, tiles[d])

        @block.sync
        def _(sp):
            sp.dma_start(causal[:], T["const_causal"].rearrange("d s t -> s d t")).then_inc(small_in, 16)
            sp.dma_start(restart[:].rearrange("h d n -> h (d n)"), T["const_restart"]).then_inc(small_in, 16)
            sp.dma_start(head_row[:].rearrange("h r n -> h (r n)"), T["const_head_row"]).then_inc(small_in, 16)
            sp.wait_ge(zero_set, 3)
            for d, c in ((0, 1), (1, LAT)):
                sp.dma_start(prev[:, d, c:c + 1], T["state_m"][0, 0, d].rearrange("(h a) -> h a", a=1)).then_inc(m0_in, 16)
            sp.wait_ge(ones_set, 2)

            def cell(s, n, d, t):
                if not isinstance(s, int):
                    sp.wait_ge(upd_done, s - 1)
                sp.dma_start(qkt[d][:], row(T["qkt"], t)).then_inc(cell_in[d], 16)
                sp.dma_start(kk[d][:], row(T["kv"], t)[:, 0:MIX]).then_inc(cell_in[d], 16)
                sp.dma_start(v1[d][:, :, 0:MD], row(T["kv"], t)[:, MIX:].rearrange("p (h n) -> p h n", h=MH)).then_inc(cell_in[d], 16)

            def states():
                sp.wait_ge(cn_done, 2)
                for d in range(2):
                    sp.dma_start(T["new_n"][0, 0, d].rearrange("h e -> e h"), cn[d][:, :, MD:W].rearrange("p h a -> p (h a)"),
                                 allow_slow_non_contiguous=True).then_inc(c_stored, 16)
                    sp.dma_start(T["new_m"][0, 0, d].rearrange("(h a) -> h a", a=1), prev[:, d, END0:END0 + 1]).then_inc(c_stored, 16)
                sp.wait_ge(cs_out, 2)
                sp.dma_start(T["new_C"][0, 0].rearrange("d h r e -> r (d h) e"), cs[:]).then_inc(c_stored, 16)
                sp.wait_ge(c_stored, 80)
                sp.dma_start(cs[:], T["state_C"][0, 0].rearrange("d h r e -> r (d h) e")).then_inc(c0_in, 16)
                for d in range(2):
                    sp.dma_start(cn[d][:, :, MD:W].rearrange("p h a -> p (h a)"), T["state_n"][0, 0, d].rearrange("h e -> e h"),
                                 allow_slow_non_contiguous=True).then_inc(n0_in, 16)

            order(sp, cell, states)

        @block.gpsimd
        def _(pool):
            nc.gpsimd.memset(prev[:], 0.0).then_inc(zero_set, 1)
            for d in range(2):
                nc.gpsimd.memset(cn[d][:], 0.0).then_inc(zero_set, 1)
            for d in range(2):
                nc.gpsimd.memset(v1[d][:, :, MD:W], 1.0).then_inc(ones_set, 1)

        @block.tensor
        def _(pe):
            pe.wait_ge(f_done, 1)
            k = 0
            for kind in range(2):
                for d in range(2):
                    src = gates if kind == 0 else log_f
                    if k >= 2:
                        pe.wait_ge(rows_out, k - 1)
                    for t in range(TILES):
                        c = 8 * d + 4 * kind
                        mm = nc.tensor.matmul(banks[3 * (k % 2) + t // 3][0:MH, (t % 3) * P:(t % 3 + 1) * P],
                                              src[:, t, c:c + MH], ident[:], start=True, stop=True)
                    mm.then_inc(rows_t, 1)
                    k += 1
            pe.wait_ge(scan_done, 1)
            for j, src in enumerate((g, mx, m)):
                for d in range(2):
                    for t in range(TILES):
                        c = ((j * 2 + d) * TILES + t) * MH
                        nc.tensor.matmul(ps[0][:, c:c + MH], src[:, d, t * P:(t + 1) * P], ident[0:MH, 0:MH], start=True, stop=True)
            pe.wait_ge(small_in, 48)
            for d in range(2):
                for h in range(MH):
                    c = (d * MH + h) * NCOL
                    nc.tensor.matmul(ps[1][:, c:c + NCOL], head_row[:, h, :], prev[:, d, :], start=True, stop=True)
                    c = 2 * MH * NCOL + (d * MH + h) * TILES
                    mm = nc.tensor.matmul(ps[1][:, c:c + TILES], head_row[:, h, :], end[:, d, :], start=True, stop=True)
            mm.then_inc(col_t, 1)
            pe.wait_ge(col_out, 3)

            def cell(s, n, d, t):
                first = isinstance(s, int) and s == 0
                if not first:
                    pe.wait_ge(arg_done, s)
                row = mx[:, d, :]
                for h in range(MH):
                    mm = nc.tensor.matmul(ps[0][:, h * P:(h + 1) * P], head_row[:, h, :], cols(row, t * P, P), start=True, stop=True)
                mm.then_inc(mb_done, 1)
                pe.wait_ge(cell_in[d], 48 * n + 48)
                if not first:
                    pe.wait_ge(p_done, s)
                for h in range(MH):
                    mm = nc.tensor.matmul(ps[1][:, h * P:(h + 1) * P], qkt[d][:, MIX + h * P:MIX + (h + 1) * P],
                                          qkt[d][:, h * P:(h + 1) * P], start=True, stop=True)
                mm.then_inc(st_done, 1)
                if isinstance(s, int):
                    pe.wait_ge(zero_set, 3)
                else:
                    pe.wait_ge(cn_done, s - 1)
                    pe.wait_ge(c0_out, 4)
                    pe.wait_ge(n0_in, 32)
                if not first:
                    pe.wait_ge(ic_done, s)
                for h in range(MH):
                    mm = nc.tensor.matmul(ps_i[:, h // 2, (h % 2) * W:(h % 2 + 1) * W], qkt[d][:, h * P:(h + 1) * P],
                                          cn[d][:, h, :], start=True, stop=True)
                mm.then_inc(inter_done, 1)
                pe.wait_ge(p_done, s + 1)
                if not first:
                    pe.wait_ge(tot_done, s)
                for h in range(MH):
                    mm = nc.tensor.matmul(ps_l[:, h // 2, (h % 2) * W:(h % 2 + 1) * W], pw[:, h * P:(h + 1) * P],
                                          v1[d][:, h, :], start=True, stop=True)
                mm.then_inc(local_done, 1)
                pe.wait_ge(vw_done, s + 1)
                if not first:
                    pe.wait_ge(cn_done, s)
                for h in range(MH):
                    mm = nc.tensor.matmul(ps_u[:, h // 2, (h % 2) * W:(h % 2 + 1) * W], kk[d][:, h * P:(h + 1) * P],
                                          vw[:, h, :], start=True, stop=True)
                mm.then_inc(upd_done, 1)

            def states():
                for d in range(2):
                    pe.wait_ge(cn_done, 2)
                    for h in range(MH):
                        tr = nc.tensor.transpose(banks[d][:, h * P:(h + 1) * P], cn[d][:, h, 0:MD], ident[:])
                    tr.then_inc(cs_t, 1)
                pe.wait_ge(c0_in, 16)
                pe.wait_ge(cs_out, 2)
                for d in range(2):
                    for h in range(MH):
                        tr = nc.tensor.transpose(banks[d][:, h * P:(h + 1) * P], cs[:, d * MH + h, :], ident[:])
                    tr.then_inc(c0_t, 1)
                pe.wait_ge(c0_out, 4)

            order(pe, cell, states)

        @block.scalar
        def _(act):
            act.wait_ge(abs_done, 1)
            nc.scalar.activation(tmp[:], log_f[:], ACT.Exp, scale=-1.0).then_inc(exp_done, 1)
            act.wait_ge(exp_done, 1)
            nc.scalar.activation(tmp[:], tmp[:], ACT.Ln, bias=1.0).then_inc(ln_done, 1)
            act.wait_ge(col_out, 3)
            act.wait_ge(diff_done, 1)
            for x in (w0, we0):
                nc.scalar.activation(x[:], x[:], ACT.Exp).then_inc(w_cols, 1)
            nc.scalar.activation(em[:], col[:, 2], ACT.Exp, scale=-1.0).then_inc(w_cols, 1)

            def cell(s, n, d, t):
                first = isinstance(s, int) and s == 0
                act.wait_ge(arg_done, s + 1)
                if not first:
                    act.wait_ge(vw_done, s)
                for h in range(MH):
                    bias = cols(col[:, 0, d].rearrange("p t h -> p (t h)"), t * MH + h, 1)
                    a = nc.scalar.activation(wt[:, h, :], arg[:, h * P:(h + 1) * P], ACT.Exp, bias=bias)
                a.then_inc(wt_done, 1)
                act.wait_ge(inter_done, s + 1)
                act.wait_ge(w_cols, 3)
                if not first:
                    act.wait_ge(tot_done, s)
                for h in range(MH):
                    scale = cols(w0[:, d].rearrange("p t h -> p (t h)"), t * MH + h, 1)
                    a = nc.scalar.activation(ic[:, h, :], ps_i[:, h // 2, (h % 2) * W:(h % 2 + 1) * W], ACT.Copy, scale=scale)
                a.then_inc(ic_done, 1)

            def states():
                for d in range(2):
                    act.wait_ge(cs_t, d + 1)
                    nc.scalar.copy(cs[:, d * MH:(d + 1) * MH, :].rearrange("p h n -> p (h n)"), banks[d]).then_inc(cs_out, 1)

            order(act, cell, states)

        @block.vector
        def _(dve):
            s_ = Steps(dve, step)
            nc.vector.scalar_tensor_tensor(out=log_f[:], in0=gates[:], scalar=-1.0, in1=gates[:], op0=ALU.mult, op1=ALU.max).then_inc(abs_done, 1)
            dve.wait_ge(ln_done, 1)
            s_.link(nc.vector.tensor_scalar(log_f[:], gates[:], 0.0, None, ALU.min))
            nc.vector.tensor_tensor(log_f[:], log_f[:], tmp[:], ALU.subtract).then_inc(f_done, 1)
            k = 0
            for kind in range(2):
                for d in range(2):
                    dve.wait_ge(rows_t, k + 1)
                    for j in range(3):
                        dst = (li if kind == 0 else lf)[:, d, j * 3 * P:(j + 1) * 3 * P]
                        c = nc.vector.tensor_copy(dst, banks[3 * (k % 2) + j][0:MH, 0:3 * P])
                    c.then_inc(rows_out, 1)
                    k += 1
            dve.wait_ge(rows_out, 4)
            dve.wait_ge(small_in, 48)
            flip = lambda ap: ap[:, ::-1]
            for d in range(2):
                way = (lambda ap: ap) if d == 0 else flip
                last = nc.vector.tensor_tensor_scan(way(b[:, d, :]), way(restart[:, d, :]), way(lf[:, d, :]), 0.0, ALU.mult, ALU.add)
            s_.link(last)
            s_.link(nc.vector.tensor_tensor(g[:], li[:], b[:], ALU.subtract))
            dve.wait_ge(zero_set, 1)
            dve.wait_ge(m0_in, 32)

            def scan(tiles, c_prev, c_next):
                for d in range(2):
                    way = (lambda ap: ap) if d == 0 else flip
                    row = cols(g[:, d, :], tiles[d] * P, P)
                    last = nc.vector.tensor_tensor_scan(way(cols(mx[:, d, :], tiles[d] * P, P)), way(row), way(row),
                                                        cols(prev[:, d, :], c_prev[d], 1), ALU.max, ALU.max)
                s_.link(last)
                for d in range(2):
                    e = tiles[d] * P + (P - 1 if d == 0 else 0)
                    last = nc.vector.tensor_tensor(cols(prev[:, d, :], c_next[d], 1), cols(mx[:, d, :], e, 1), cols(b[:, d, :], e, 1), ALU.add)
                s_.link(last)

            scan((0, 0), PREV0, (END0, END0))
            for i in range(LAT):
                scan((i + 1, LAT - i), (i + 1, LAT - i), (i + 2, LAT - i - 1))
            nc.vector.tensor_tensor(m[:], mx[:], b[:], ALU.add)
            for d in range(2):
                e = P - 1 if d == 0 else 0
                last = nc.vector.tensor_copy(end[:, d, :], mx[:, d, :].rearrange("h (t n) -> h t n", t=TILES)[:, :, e])
            s_.link(last)
            nc.vector.memset(prev[:, 1, 0:1], 0.0).then_inc(scan_done, 1)
            dve.wait_ge(col_t, 1)
            nc.vector.tensor_copy(col[:].rearrange("p k d t h -> p (k d t h)"), ps[0][:, 0:3 * 2 * TILES * MH]).then_inc(col_out, 1)
            nc.vector.tensor_copy(prevb[:].rearrange("p d h t -> p (d h t)"), ps[1][:, 0:2 * MH * NCOL]).then_inc(col_out, 1)
            nc.vector.tensor_copy(endb[:].rearrange("p d h t -> p (d h t)"), ps[1][:, 2 * MH * NCOL:2 * MH * (NCOL + TILES)]).then_inc(col_out, 1)
            dve.wait_ge(col_out, 3)
            for d in range(2):
                before = prevb[:, d, :, 0:TILES].rearrange("p h t -> p t h")
                nc.vector.tensor_tensor(w0[:, d], before, col[:, 1, d], ALU.subtract)
                last = nc.vector.tensor_tensor(we0[:, d], before, endb[:, d].rearrange("p h t -> p t h"), ALU.subtract)
            last.then_inc(diff_done, 1)
            dve.wait_ge(w_cols, 3)

            def cell(s, n, d, t):
                first = isinstance(s, int) and s == 0
                dve.wait_ge(mb_done, s + 1)
                if not first:
                    dve.wait_ge(wt_done, s)
                nc.vector.scalar_tensor_tensor(out=arg[:].rearrange("p (h n) -> p h n", h=MH), in0=ps[0][:].rearrange("p (h n) -> p h n", h=MH),
                                               scalar=-1.0, in1=causal[:, d, :].unsqueeze(1).to_broadcast([P, MH, P]),
                                               op0=ALU.mult, op1=ALU.add).then_inc(arg_done, 1)
                dve.wait_ge(wt_done, s + 1)
                dve.wait_ge(st_done, s + 1)
                if not first:
                    dve.wait_ge(local_done, s)
                nc.vector.tensor_tensor(pw[:], ps[1][:], wt[:].rearrange("p h n -> p (h n)"), ALU.mult).then_inc(p_done, 1)
                dve.wait_ge(cell_in[d], 48 * n + 48)
                if not first:
                    dve.wait_ge(upd_done, s)
                e = P - 1 if d == 0 else 0
                nc.vector.tensor_tensor(vw[:], v1[d][:], wt[:, :, e:e + 1].to_broadcast([P, MH, W]), ALU.mult).then_inc(vw_done, 1)
                dve.wait_ge(ic_done, s + 1)
                dve.wait_ge(local_done, s + 1)
                for a in range(2):
                    last = nc.vector.tensor_tensor(tot[:, 2 * a:2 * a + 2, :].rearrange("p h n -> p (h n)"),
                                                   ic[:, 2 * a:2 * a + 2, :].rearrange("p h n -> p (h n)"), ps_l[:, a, 0:2 * W], ALU.add)
                last.then_inc(tot_done, 1)
                dve.wait_ge(tot_done, s + 1)
                raw = tot[:, :, MD:W].rearrange("p h a -> p (h a)")
                s_.link(nc.vector.scalar_tensor_tensor(out=den[:], in0=raw, scalar=-1.0, in1=raw, op0=ALU.mult, op1=ALU.max))
                s_.link(nc.vector.tensor_tensor(den[:], den[:], cols(em[:, d].rearrange("p t h -> p (t h)"), t * MH, MH), ALU.max))
                s_.link(nc.vector.reciprocal(den[:], den[:]))
                nc.vector.tensor_tensor(cols(hd[:, d], t * MIX, MIX).rearrange("p (h n) -> p h n", h=MH), tot[:, :, 0:MD],
                                        den[:].unsqueeze(2).to_broadcast([P, MH, MD]), ALU.mult)
                dve.wait_ge(upd_done, s + 1)
                for h in range(MH):
                    carry = cols(we0[:, d].rearrange("p t h -> p (t h)"), t * MH + h, 1)
                    last = nc.vector.scalar_tensor_tensor(out=cn[d][:, h, :], in0=cn[d][:, h, :], scalar=carry,
                                                          in1=ps_u[:, h // 2, (h % 2) * W:(h % 2 + 1) * W], op0=ALU.mult, op1=ALU.add)
                last.then_inc(cn_done, 1)

            for d in range(2):
                cell(d, 0, d, 0)
            dve.wait_ge(n0_in, 32)
            for d in range(2):
                dve.wait_ge(c0_t, d + 1)
                for a in range(2):
                    nc.vector.tensor_copy(cn[d][:, 2 * a:2 * a + 2, 0:MD], banks[d][:, a * 256:(a + 1) * 256].rearrange(
                        "p (h n) -> p h n", h=2)).then_inc(c0_out, 1)
            dve.wait_ge(c0_out, 4)
            with dve.Fori(0, LAT) as i:
                s_.enter(i, 6)
                tiles = (i + 1, LAT - i)
                dve.to_reg(tiles[1])
                for d in range(2):
                    cell(2 * i + (2 + d), i + 1, d, tiles[d])
            s_.leave(LAT)


def attend(nc, T, keep):
    with nc.cleanup_on_exit(), ExitStack() as ctx:
        sb = lambda n, s, d=F32: ctx.enter_context(nc.sbuf_tensor(n, s, d))
        sem = nc.alloc_semaphore
        bank = lambda n: ctx.enter_context(nc.psum_tensor(n, [P, 512], F32))
        ident, kat, va, hd = keep.ident, keep.kat, keep.va, keep.hd
        ck = sb("at_ck", [P, AKV * AD])
        ckt = sb("at_ckt", [AD, AKV, P])
        cv = sb("at_cv", [P, AKV * AD])
        sink = sb("at_sink", [P, AH])
        gm = sb("at_gm", [P, MIX])
        half = sb("at_half", [P, MH])
        qat = [sb(f"at_qat{u}", [AD, AH * P]) for u in range(2)]
        win = [sb(f"at_win{u}", [P, 4 * P]) for u in range(2)]
        og = [sb(f"at_og{u}", [P, MIX]) for u in range(2)]
        sm = [sb(f"at_sm{u}", [P, 512]) for u in range(2)]
        pr = [sb(f"at_pr{u}", [P, 512]) for u in range(2)]
        pt = [sb(f"at_pt{u}", [P, 512]) for u in range(2)]
        top = sb("at_top", [P, AH])
        ntop = sb("at_ntop", [P, AH])
        total = sb("at_total", [P, AH])
        es = sb("at_es", [P, AH])
        rec = sb("at_rec", [P, AH])
        ya = sb("at_ya", [P, MIX])
        hs = sb("at_hs", [P, MIX])
        sq = sb("at_sq", [P, MIX])
        ms = sb("at_ms", [P, MH])
        rstd = sb("at_rstd", [P, MH])
        ym = sb("at_ym", [P, MIX])
        yt = sb("at_yt", [P, 2 * MIX])
        ps_s = [bank(f"at_ps_s{b}") for b in range(3)]
        ps_t = [bank(f"at_ps_t{b}") for b in range(2)]
        ps_o = bank("at_ps_o")
        ps_y = [bank(f"at_ps_y{b}") for b in range(2)]

        small_in, ckt_t, ckt_out, half_set = (sem(f"at_{n}") for n in ("small_in", "ckt_t", "ckt_out", "half_set"))
        tile_in = [sem(f"at_tile_in{u}") for u in range(2)]
        s_done, top_done, pr_done, pt_t, pt_done, o_done = (sem(f"at_{n}") for n in ("s", "top", "pr", "pt_t", "pt", "o"))
        diff_done, es_done, ya_done, ym_done = (sem(f"at_{n}") for n in ("diff", "es", "ya", "ym"))
        ms_done, rstd_done, y_t, y_out, stored = (sem(f"at_{n}") for n in ("ms", "rstd", "y_t", "y_out", "stored"))
        step = sem("at_dve_step")
        block = ctx.enter_context(nc.Block())
        SCALE = AD ** -0.5

        def order(eng, tile):
            tile(0, 1, 0)
            with eng.Fori(0, LAT // 2) as i:
                for u in range(2):
                    tile(2 * i + (1 + u), u, i + u)

        @block.sync
        def _(sp):
            sp.dma_start(ck[:], T["cache_k"][0, 0].rearrange("s k d -> s (k d)")).then_inc(small_in, 16)
            sp.dma_start(cv[:], T["cache_v"][0, 0].rearrange("s k d -> s (k d)")).then_inc(small_in, 16)
            sp.dma_start(sink[:], T["sink"].to_broadcast([P, AH])).then_inc(small_in, 16)
            sp.dma_start(gm[:], T["g_mlstm"].rearrange("a h n -> a (h n)").to_broadcast([P, MIX])).then_inc(small_in, 16)

            def load(t, u, n):
                if not isinstance(t, int) or t >= 2:
                    sp.wait_ge(ya_done, t - 1)
                    sp.wait_ge(ym_done, t - 1)
                sp.dma_start(qat[u][:], row(T["qat"], t)).then_inc(tile_in[u], 16)
                sp.dma_start(og[u][:], row(T["og"], t)).then_inc(tile_in[u], 16)
                if is_first(t):
                    sp.dma_start(win[u][:, 0:P], row(T["const_window"], 3)[:, 2 * P:3 * P]).then_inc(tile_in[u], 16)
                else:
                    sp.dma_start(win[u][:], row(T["const_window"], t - 1)).then_inc(tile_in[u], 16)

            def store(t):
                sp.wait_ge(y_out, 2 * t + 2)
                sp.dma_start(row(T["yt"], t), yt[:]).then_inc(stored, 16)

            load(0, 1, 0)
            load(1, 0, 0)
            store(0)
            load(2, 1, 1)
            store(1)
            with sp.Fori(0, LAT // 2 - 1) as i:
                for u in range(2):
                    load(2 * i + (3 + u), u, i + 1 + u)
                    store(2 * i + (2 + u))
            store(LAT)
            sp.wait_ge(stored, 16 * TILES)

        @block.gpsimd
        def _(pool):
            nc.gpsimd.memset(half[:], -0.5).then_inc(half_set, 1)
            pool.wait_ge(half_set, 1)

            def tile(t, u, n):
                pool.wait_ge(ms_done, t + 1)
                nc.gpsimd.tensor_tensor(rstd[:], ms[:], half[:], ALU.pow).then_inc(rstd_done, 1)

            order(pool, tile)

        @block.tensor
        def _(pe):
            pe.wait_ge(small_in, 64)
            for k in range(AKV):
                tr = nc.tensor.transpose(ps_t[0][0:AD, k * P:(k + 1) * P], ck[:, k * AD:(k + 1) * AD], ident[:])
            tr.then_inc(ckt_t, 1)
            pe.wait_ge(ckt_out, 1)

            def tile(t, u, n):
                nb = 1 if is_first(t) else 4

                def scores(h):
                    if not is_first(t) or h >= 3:
                        pe.wait_ge(top_done, AH * t + h - 2)
                    q, kv = qat[u][:, h * P:(h + 1) * P], h // (AH // AKV)
                    if is_first(t):
                        mm = nc.tensor.matmul(ps_s[h % 3][:, 0:P], q, kat[:, kv, 0:P], start=True, stop=True)
                    else:
                        nc.tensor.matmul(ps_s[h % 3][:, 0:P], q, ckt[:, kv, :], start=True, stop=True)
                        mm = nc.tensor.matmul(ps_s[h % 3][:, P:4 * P], q, cols(kat[:, kv, :], (t - 1) * P, 3 * P), start=True, stop=True)
                    mm.then_inc(s_done, 1)

                def turn(h):
                    pe.wait_ge(pr_done, AH * t + h + 1)
                    if not is_first(t) or h >= 2:
                        pe.wait_ge(pt_done, AH * t + h - 1)
                    for b in range(nb):
                        tr = nc.tensor.transpose(ps_t[h % 2][:, b * P:(b + 1) * P], pr[h % 2][:, b * P:(b + 1) * P], ident[:])
                    tr.then_inc(pt_t, 1)

                def values(h):
                    pe.wait_ge(pt_done, AH * t + h + 1)
                    if h == 0 and not is_first(t):
                        pe.wait_ge(ya_done, t)
                    kv = h // (AH // AKV)
                    for b in range(nb):
                        if is_first(t):
                            v = va[:, 0, kv * AD:(kv + 1) * AD]
                        elif b == 0:
                            v = cv[:, kv * AD:(kv + 1) * AD]
                        else:
                            v = cols(va[:].rearrange("p t n -> p (t n)"), (t + (b - 2)) * P + kv * AD, AD)
                        mm = nc.tensor.matmul(ps_o[:, h * AD:(h + 1) * AD], pt[h % 2][:, b * P:(b + 1) * P], v, start=(b == 0), stop=(b == nb - 1))
                    mm.then_inc(o_done, 1)

                pe.wait_ge(tile_in[u], 48 * n + 48)
                scores(0)
                scores(1)
                for h in range(AH):
                    if h + 2 < AH:
                        scores(h + 2)
                    turn(h)
                    if h >= 1:
                        values(h - 1)
                values(AH - 1)
                for k, (y, ready) in enumerate(((ym, ym_done), (ya, ya_done))):
                    pe.wait_ge(ready, t + 1)
                    if not is_first(t):
                        pe.wait_ge(y_out, 2 * t - 1 + k)
                    for a in range(4):
                        tr = nc.tensor.transpose(ps_y[k][:, a * P:(a + 1) * P], y[:, a * P:(a + 1) * P], ident[:])
                    tr.then_inc(y_t, 1)

            order(pe, tile)

        @block.scalar
        def _(act):
            act.wait_ge(ckt_t, 1)
            nc.scalar.copy(ckt[:].rearrange("p k n -> p (k n)"), ps_t[0][0:AD, 0:2 * P]).then_inc(ckt_out, 1)

            def tile(t, u, n):
                w = P if is_first(t) else 4 * P
                for h in range(AH):
                    act.wait_ge(top_done, AH * t + h + 1)
                    if not is_first(t) or h >= 2:
                        act.wait_ge(pt_t, AH * t + h - 1)
                    nc.scalar.activation(pr[h % 2][:, 0:w], sm[h % 2][:, 0:w], ACT.Exp, bias=ntop[:, h:h + 1],
                                         accum_out=total[:, h:h + 1]).then_inc(pr_done, 1)
                    if h % 2 == 1:
                        act.wait_ge(pt_t, AH * t + h)
                        if not is_first(t) or h >= 2:
                            act.wait_ge(o_done, AH * t + h - 2)
                        nc.scalar.copy(pt[0][:, 0:w], ps_t[0][:, 0:w]).then_inc(pt_done, 1)
                        act.wait_ge(pt_t, AH * t + h + 1)
                        if not is_first(t) or h >= 2:
                            act.wait_ge(o_done, AH * t + h - 1)
                        nc.scalar.copy(pt[1][:, 0:w], ps_t[1][:, 0:w]).then_inc(pt_done, 1)
                act.wait_ge(diff_done, t + 1)
                nc.scalar.activation(es[:], es[:], ACT.Exp).then_inc(es_done, 1)
                for k in range(2):
                    act.wait_ge(y_t, 2 * t + k + 1)
                    if not is_first(t):
                        act.wait_ge(stored, 16 * t)
                    nc.scalar.copy(yt[:, k * MIX:(k + 1) * MIX], ps_y[k][:]).then_inc(y_out, 1)

            order(act, tile)

        @block.vector
        def _(dve):
            s_ = Steps(dve, step)
            dve.wait_ge(small_in, 64)

            def tile(t, u, n):
                w = P if is_first(t) else 4 * P
                dve.wait_ge(tile_in[u], 48 * n + 48)
                hf, hb = (cols(hd[:, d], t * MIX, MIX) for d in range(2))
                if not is_first(t):
                    dve.wait_ge(y_t, 2 * t)
                s_.link(nc.vector.tensor_tensor(hs[:], hf, hb, ALU.add))
                s_.link(nc.vector.tensor_tensor(sq[:], hs[:], hs[:], ALU.mult))
                s_.link(nc.vector.tensor_reduce(ms[:], sq[:].rearrange("p (h n) -> p h n", h=MH), AX_X, ALU.add))
                nc.vector.tensor_scalar(ms[:], ms[:], 1.0 / MD, EPS, ALU.mult, ALU.add).then_inc(ms_done, 1)
                nc.vector.tensor_tensor(sq[:], gm[:], og[u][:], ALU.mult)
                dve.wait_ge(rstd_done, t + 1)
                s_.link(nc.vector.tensor_tensor(hs[:].rearrange("p (h n) -> p h n", h=MH), hs[:].rearrange("p (h n) -> p h n", h=MH),
                                                rstd[:].unsqueeze(2).to_broadcast([P, MH, MD]), ALU.mult))
                nc.vector.tensor_tensor(ym[:], hs[:], sq[:], ALU.mult).then_inc(ym_done, 1)
                for h in range(AH):
                    if not is_first(t) or h >= 2:
                        dve.wait_ge(pr_done, AH * t + h - 1)
                    dve.wait_ge(s_done, AH * t + h + 1)
                    s_.link(nc.vector.tensor_tensor(sm[h % 2][:, 0:w], ps_s[h % 3][:, 0:w], win[u][:, 0:w], ALU.add))
                    s_.link(nc.vector.tensor_reduce(top[:, h:h + 1], sm[h % 2][:, 0:w], AX_X, ALU.max))
                    nc.vector.tensor_scalar(sm[h % 2][:, 0:w], sm[h % 2][:, 0:w], SCALE, None, ALU.mult)
                    s_.link(nc.vector.scalar_tensor_tensor(out=top[:, h:h + 1], in0=top[:, h:h + 1], scalar=SCALE, in1=sink[:, h:h + 1],
                                                           op0=ALU.mult, op1=ALU.max))
                    nc.vector.tensor_scalar(ntop[:, h:h + 1], top[:, h:h + 1], -1.0, None, ALU.mult).then_inc(top_done, 1)
                nc.vector.tensor_tensor(es[:], sink[:], top[:], ALU.subtract).then_inc(diff_done, 1)
                dve.wait_ge(es_done, t + 1)
                s_.link(nc.vector.tensor_tensor(rec[:], es[:], total[:], ALU.add))
                s_.link(nc.vector.reciprocal(rec[:], rec[:]))
                dve.wait_ge(o_done, AH * t + AH)
                nc.vector.tensor_tensor(ya[:].rearrange("p (h n) -> p h n", h=AH), ps_o[:].rearrange("p (h n) -> p h n", h=AH),
                                        rec[:].unsqueeze(2).to_broadcast([P, AH, AD]), ALU.mult).then_inc(ya_done, 1)

            tile(0, 1, 0)
            PER = 4 + 3 * AH + 2
            with dve.Fori(0, LAT // 2) as i:
                s_.enter(i, 2 * PER)
                for u in range(2):
                    tile(2 * i + (1 + u), u, i + u)
            s_.leave(LAT // 2)


def pairs(eng, tile):
    tile(0, 1, 0)
    with eng.Fori(0, LAT // 2) as i:
        for u in range(2):
            tile(2 * i + (1 + u), u, i + u)


def merge(nc, T, keep):
    NBR = 3
    NJ = 2 * NBR
    with nc.cleanup_on_exit(), ExitStack() as ctx:
        sb = lambda n, s, d=F32: ctx.enter_context(nc.sbuf_tensor(n, s, d))
        sem = nc.alloc_semaphore
        bank = lambda n: ctx.enter_context(nc.psum_tensor(n, [P, 512], F32))
        ident = keep.ident
        wm = sb("mg_wm", [P, DC, NBR * D])
        wb = sb("mg_wb", [P, NBR, 4, D])
        bm = sb("mg_bm", [P, NBR * D])
        ht = [sb(f"mg_ht{u}", [P, DC, P]) for u in range(2)]
        yt = [sb(f"mg_yt{u}", [P, 3, 4, P]) for u in range(2)]
        gsum = [sb(f"mg_gsum{u}", [P, 512]) for u in range(2)]
        gate = [sb(f"mg_gate{u}", [P, 512]) for u in range(2)]
        merged = sb("mg_merged", [P, D])
        mt = sb("mg_mt", [P, D])
        ps_g = [bank(f"mg_ps_g{b}") for b in range(3)]
        ps_p = [bank(f"mg_ps_p{b}") for b in range(2)]
        ps_t = [bank(f"mg_ps_t{b}") for b in range(2)]
        wm_in, wb_in = [sem(f"mg_wm_in{k}") for k in range(DC)], [sem(f"mg_wb_in{n}") for n in range(NBR)]
        bm_in = sem("mg_bm_in")
        tile_in = [sem(f"mg_tile_in{u}") for u in range(2)]
        g_done, p_done, sum_done, gate_done, prod_done = (sem(f"mg_{n}") for n in ("g", "p", "sum", "gate", "prod"))
        m_t, m_out, stored = (sem(f"mg_{n}") for n in ("m_t", "m_out", "stored"))
        step = sem("mg_dve_step")
        block = ctx.enter_context(nc.Block())

        @block.sync
        def _(sp):
            def load(t, u, n):
                if not isinstance(t, int) or t >= 2:
                    sp.wait_ge(p_done, NJ * (t - 1))
                sp.dma_start(ht[u][:].rearrange("p k n -> p (k n)"), row(T["ht"], t)).then_inc(tile_in[u], 16)
                flat = yt[u][:].rearrange("p b k n -> p b (k n)")
                sp.dma_start(flat[:, 0, :], row(T["yt"], t)[:, 0:MIX]).then_inc(tile_in[u], 16)
                sp.dma_start(flat[:, 1, :], row(T["yct"], t)).then_inc(tile_in[u], 16)
                sp.dma_start(flat[:, 2, :], row(T["yt"], t)[:, MIX:]).then_inc(tile_in[u], 16)

            def store(t):
                sp.wait_ge(m_out, 2 * t + 2)
                sp.dma_start(row(T["mt"], t), mt[:]).then_inc(stored, 16)

            load(0, 1, 0)
            for k in range(DC):
                sp.dma_start(wm[:, k, :], T["w_merge"][0, k * P:(k + 1) * P, :]).then_inc(wm_in[k], 16)
            sp.dma_start(bm[:], T["b_merge"].to_broadcast([P, NBR * D])).then_inc(bm_in, 16)
            for n in range(NBR):
                sp.dma_start(wb[:, n], T["w_branch"][0, n].rearrange("(k p) d -> p k d", p=P)).then_inc(wb_in[n], 16)
            load(1, 0, 0)
            load(2, 1, 1)
            store(0)
            with sp.Fori(0, LAT // 2 - 1) as i:
                for u in range(2):
                    load(2 * i + (3 + u), u, i + 1 + u)
                    store(2 * i + (1 + u))
            store(LAT - 1)
            store(LAT)
            sp.wait_ge(stored, 16 * TILES)

        @block.tensor
        def _(pe):
            def turn(t):
                pe.wait_ge(prod_done, NJ * t + NJ)
                if not is_first(t):
                    pe.wait_ge(m_out, 2 * t)
                for k in range(DC):
                    tr = nc.tensor.transpose(ps_t[k // 4][:, (k % 4) * P:(k % 4 + 1) * P], merged[:, k * P:(k + 1) * P], ident[:])
                    if k % 4 == 3:
                        tr.then_inc(m_t, 1)

            def tile(t, u, n):
                pe.wait_ge(tile_in[u], 64 * n + 64)
                for j in range(NJ):
                    br, half = j // 2, j % 2
                    if not is_first(t) or j >= 3:
                        pe.wait_ge(sum_done, NJ * t + j - 2)
                    for k in range(DC):
                        if is_first(t) and j == 0:
                            pe.wait_ge(wm_in[k], 16)
                        mm = nc.tensor.matmul(ps_g[j % 3][:], ht[u][:, k, :], wm[:, k, j * 512:(j + 1) * 512], start=(k == 0), stop=(k == DC - 1))
                    mm.then_inc(g_done, 1)
                    if not is_first(t) or j >= 2:
                        pe.wait_ge(prod_done, NJ * t + j - 1)
                    if is_first(t) and half == 0:
                        pe.wait_ge(wb_in[br], 16)
                    for k in range(4):
                        mm = nc.tensor.matmul(ps_p[j % 2][:], yt[u][:, br, k, :], wb[:, br, k, half * 512:(half + 1) * 512], start=(k == 0), stop=(k == 3))
                    mm.then_inc(p_done, 1)
                    if j == 0 and not is_first(t):
                        turn(t - 1)

            pairs(pe, tile)
            turn(LAT)

        @block.scalar
        def _(act):
            def out(t):
                for b in range(2):
                    act.wait_ge(m_t, 2 * t + b + 1)
                    if b == 0 and not is_first(t):
                        act.wait_ge(stored, 16 * t)
                    nc.scalar.copy(mt[:, b * 512:(b + 1) * 512], ps_t[b][:]).then_inc(m_out, 1)

            def tile(t, u, n):
                for j in range(NJ):
                    act.wait_ge(sum_done, NJ * t + j + 1)
                    if not is_first(t) or j >= 2:
                        act.wait_ge(prod_done, NJ * t + j - 1)
                    nc.scalar.activation(gate[j % 2][:], gsum[j % 2][:], ACT.Sigmoid).then_inc(gate_done, 1)
                    if j == 0 and not is_first(t):
                        out(t - 1)

            pairs(act, tile)
            out(LAT)

        @block.vector
        def _(dve):
            s_ = Steps(dve, step)
            dve.wait_ge(bm_in, 16)

            def tile(t, u, n):
                def add_bias(j):
                    dve.wait_ge(g_done, NJ * t + j + 1)
                    if not is_first(t) or j >= 2:
                        dve.wait_ge(gate_done, NJ * t + j - 1)
                    nc.vector.tensor_tensor(gsum[j % 2][:], ps_g[j % 3][:], bm[:, j * 512:(j + 1) * 512], ALU.add).then_inc(sum_done, 1)

                def add_product(j):
                    dve.wait_ge(gate_done, NJ * t + j + 1)
                    dve.wait_ge(p_done, NJ * t + j + 1)
                    into = merged[:, (j % 2) * 512:(j % 2 + 1) * 512]
                    if j == 0 and not is_first(t):
                        dve.wait_ge(m_t, 2 * t)
                    if j < 2:
                        nc.vector.tensor_tensor(into, gate[j % 2][:], ps_p[j % 2][:], ALU.mult).then_inc(prod_done, 1)
                    else:
                        s_.link(nc.vector.tensor_tensor(gate[j % 2][:], gate[j % 2][:], ps_p[j % 2][:], ALU.mult))
                        nc.vector.tensor_tensor(into, into, gate[j % 2][:], ALU.add).then_inc(prod_done, 1)

                for j in range(NJ):
                    add_bias(j)
                    if j >= 1:
                        add_product(j - 1)
                add_product(NJ - 1)

            tile(0, 1, 0)
            with dve.Fori(0, LAT // 2) as i:
                s_.enter(i, 2 * (NJ - 2))
                for u in range(2):
                    tile(2 * i + (1 + u), u, i + u)
            s_.leave(LAT // 2)


def route(nc, T, keep):
    HP = 2 * PH
    with nc.cleanup_on_exit(), ExitStack() as ctx:
        sb = lambda n, s, d=F32: ctx.enter_context(nc.sbuf_tensor(n, s, d))
        sem = nc.alloc_semaphore
        bank = lambda n: ctx.enter_context(nc.psum_tensor(n, [P, 512], F32))
        ident = keep.ident
        wo = sb("rt_wo", [P, DC, D])
        wq = sb("rt_wq", [P, DC, HP * P])
        keyt = sb("rt_keyt", [P, HP, P])
        gate1, scale2, shift2, gain2 = (sb(f"rt_{n}", [P, D]) for n in ("gate1", "scale2", "shift2", "gain2"))
        mt = sb("rt_mt", [P, DC, P])
        x = sb("rt_x", [P, D])
        x1 = sb("rt_x1", [P, D])
        h2 = sb("rt_h2", [P, D])
        sq = sb("rt_sq", [P, D])
        h2t = sb("rt_h2t", [P, DC, P])
        qt = sb("rt_qt", [P, HP, P])
        sc = sb("rt_sc", [P, HP, P])
        ss = sb("rt_ss", [P, 3])
        half = sb("rt_half", [P, 1])
        hold = sb("rt_hold", [P, 1])
        v16 = sb("rt_v16", [P, PH, 2, TOPK])
        i16 = sb("rt_i16", [P, PH, 2, TOPK], U32)
        i16f = sb("rt_i16f", [P, PH, 2, TOPK])
        cand = sb("rt_cand", [P, PH, TOPK, TOPK])
        vs = sb("rt_vs", [P, PH, TOPK])
        ic = sb("rt_ic", [P, PH, TOPK], U32)
        part = sb("rt_part", [P, PH, TOPK], U32)
        partf = sb("rt_partf", [P, PH, TOPK])
        oh = sb("rt_oh", [P, PH, TOPK, TOPK])
        e12 = [sb(f"rt_e{a}", [P, PH, TOPK]) for a in range(2)]
        ids = sb("rt_ids", [P, PH, TOPK], U32)
        ex = sb("rt_ex", [P, PH, TOPK])
        tot = sb("rt_tot", [P, PH])
        gw = sb("rt_gw", [P, PH, TOPK])
        iota = sb("rt_iota", [P, TOPK])
        ps_y = [bank(f"rt_ps_y{b}") for b in range(2)]
        ps_x = [bank(f"rt_ps_x{b}") for b in range(2)]
        ps_q = [bank(f"rt_ps_q{b}") for b in range(2)]
        ps_s = [bank(f"rt_ps_s{b}") for b in range(2)]
        wo_in, wq_in = sem("rt_wo_in"), sem("rt_wq_in")
        keys_in, rows_in, rows2_in, small_in = (sem(f"rt_{n}") for n in ("keys_in", "rows_in", "rows2_in", "small_in"))
        mt_in, x_in, half_set, key_t, key_out = (sem(f"rt_{n}") for n in ("mt_in", "x_in", "half_set", "key_t", "key_out"))
        y_done, x1_done, ss_done, ms_done, rstd_done, h2_done = (sem(f"rt_{n}") for n in ("y", "x1", "ss", "ms", "rstd", "h2"))
        h2_t, h2t_done, q_done, qt_done, s_done, sc_done = (sem(f"rt_{n}") for n in ("h2_t", "h2t", "q", "qt", "sco", "sc"))
        picked, ex_in, ex_done, ids_done, gw_done = (sem(f"rt_{n}") for n in ("picked", "ex_in", "ex", "ids", "gw"))
        st_x1, st_h2, st_ids, st_gw, step = (sem(f"rt_{n}") for n in ("st_x1", "st_h2", "st_ids", "st_gw", "step"))
        block = ctx.enter_context(nc.Block())

        @block.sync
        def _(sp):
            sp.dma_start(wo[:], T["w_out"][0].rearrange("(k p) n -> p k n", p=P)).then_inc(wo_in, 16)
            for dst, c in ((gate1, 2), (scale2, 4), (shift2, 3)):
                sp.dma_start(dst[:], T["mod"][0:1, c * D:(c + 1) * D].to_broadcast([P, D])).then_inc(rows_in, 16)
            sp.dma_start(gain2[:], T["g_norm2"].to_broadcast([P, D])).then_inc(rows_in, 16)
            sp.dma_start(qt[:], T["peer_keys"][0].rearrange("h a k d -> k (h a) d")).then_inc(keys_in, 16)
            sp.dma_start(iota[:], T["const_iota"]).then_inc(small_in, 16)
            sp.dma_start(wq[:], T["w_peer_q"][0].rearrange("(k p) n -> p k n", p=P)).then_inc(wq_in, 16)

            def store_norm(t):
                sp.wait_ge(x1_done, 2 * t + 2)
                sp.dma_start(row(T["x1"], t), x1[:]).then_inc(st_x1, 16)
                sp.wait_ge(h2_done, t + 1)
                sp.dma_start(row(T["h2"], t), h2[:]).then_inc(st_h2, 16)

            def store_picks(t):
                sp.wait_ge(ids_done, t + 1)
                sp.dma_start(row(T["ids"], t), ids[:].rearrange("p h k -> p (h k)")).then_inc(st_ids, 16)
                sp.wait_ge(gw_done, t + 1)
                sp.dma_start(row(T["gw"], t), gw[:].rearrange("p h k -> p (h k)")).then_inc(st_gw, 16)

            store_norm(0)
            for dst, c in ((gate1, 2), (scale2, 4), (shift2, 3)):
                sp.dma_start(dst[:], T["mod"][1:2, c * D:(c + 1) * D].to_broadcast([P, D])).then_inc(rows2_in, 16)
            with sp.Fori(0, LAT) as i:
                store_norm(i + 1)
                store_picks(i)
            store_picks(LAT)
            for s in (st_x1, st_h2, st_ids, st_gw):
                sp.wait_ge(s, 16 * TILES)

        @block.gpsimd
        def _(pool):
            nc.gpsimd.memset(half[:], -0.5).then_inc(half_set, 1)
            pool.dma_start(mt[:].rearrange("p k n -> p (k n)"), row(T["mt"], 0)).then_inc(mt_in, 16)
            pool.dma_start(x[:], T["x_prompt"][0]).then_inc(x_in, 16)
            pool.wait_ge(half_set, 1)

            def rsqrt(t):
                pool.wait_ge(ms_done, t + 1)
                nc.gpsimd.tensor_tensor(ss[:, 2:3], ss[:, 1:2], half[:], ALU.pow).then_inc(rstd_done, 1)

            rsqrt(0)
            with pool.Fori(0, LAT) as i:
                pool.wait_ge(y_done, 2 * i + 2)
                pool.wait_ge(half_set, 1)
                pool.dma_start(mt[:].rearrange("p k n -> p (k n)"), row(T["mt"], i + 1)).then_inc(mt_in, 16)
                pool.wait_ge(x1_done, 2 * i + 2)
                pool.wait_ge(half_set, 1)
                pool.dma_start(x[:], row(T["x_sample"][0].rearrange("(t p) d -> t p d", p=P), i)).then_inc(x_in, 16)
                rsqrt(i + 1)

        @block.tensor
        def _(pe):
            pe.wait_ge(keys_in, 16)
            pe.wait_ge(half_set, 1)
            for b in range(4):
                if b >= 2:
                    pe.wait_ge(key_out, b - 1)
                for a in range(4):
                    tr = nc.tensor.transpose(ps_q[b % 2][:, a * P:(a + 1) * P], qt[:, 4 * b + a, :], ident[:])
                tr.then_inc(key_t, 1)

            def project_out(t):
                pe.wait_ge(mt_in, 16 * t + 16)
                if is_first(t):
                    pe.wait_ge(wo_in, 16)
                for b in range(2):
                    if not is_first(t):
                        pe.wait_ge(x1_done, 2 * t + b - 1)
                    for k in range(DC):
                        mm = nc.tensor.matmul(ps_y[b][:], mt[:, k, :], wo[:, k, b * 512:(b + 1) * 512], start=(k == 0), stop=(k == DC - 1))
                    mm.then_inc(y_done, 1)

            def queries(t):
                pe.wait_ge(h2_done, t + 1)
                if not is_first(t):
                    pe.wait_ge(h2t_done, 2 * t)
                for k in range(DC):
                    tr = nc.tensor.transpose(ps_x[k // 4][:, (k % 4) * P:(k % 4 + 1) * P], h2[:, k * P:(k + 1) * P], ident[:])
                    if k % 4 == 3:
                        tr.then_inc(h2_t, 1)
                pe.wait_ge(h2t_done, 2 * t + 2)

                def query(b):
                    if not is_first(t) or b >= 2:
                        pe.wait_ge(qt_done, 4 * t + b - 1)
                    for a in range(4):
                        for k in range(DC):
                            mm = nc.tensor.matmul(ps_q[b % 2][:, a * P:(a + 1) * P], wq[:, k, (4 * b + a) * P:(4 * b + a + 1) * P],
                                                  h2t[:, k, :], start=(k == 0), stop=(k == DC - 1))
                    mm.then_inc(q_done, 1)

                def score(b):
                    pe.wait_ge(qt_done, 4 * t + b + 1)
                    if not is_first(t) or b >= 2:
                        pe.wait_ge(sc_done, 4 * t + b - 1)
                    for a in range(4):
                        mm = nc.tensor.matmul(ps_s[b % 2][:, a * P:(a + 1) * P], qt[:, 4 * b + a, :], keyt[:, 4 * b + a, :], start=True, stop=True)
                    mm.then_inc(s_done, 1)

                query(0)
                for b in range(1, 4):
                    query(b)
                    score(b - 1)
                score(3)

            project_out(0)
            pe.wait_ge(wq_in, 16)
            pe.wait_ge(key_out, 4)
            project_out(1)
            queries(0)
            with pe.Fori(0, LAT - 1) as i:
                project_out(i + 2)
                queries(i + 1)
            queries(LAT)

        @block.scalar
        def _(act):
            for b in range(4):
                act.wait_ge(key_t, b + 1)
                nc.scalar.copy(keyt[:, 4 * b:4 * b + 4, :].rearrange("p a n -> p (a n)"), ps_q[b % 2][:]).then_inc(key_out, 1)

            def square(t):
                act.wait_ge(x1_done, 2 * t + 2)
                nc.scalar.activation(sq[:], x1[:], ACT.Square, accum_out=ss[:, 0:1]).then_inc(ss_done, 1)

            def outs(t):
                for b in range(2):
                    act.wait_ge(h2_t, 2 * t + b + 1)
                    if not is_first(t) and b == 0:
                        act.wait_ge(q_done, 4 * t)
                    nc.scalar.copy(h2t[:, 4 * b:4 * b + 4, :].rearrange("p a n -> p (a n)"), ps_x[b][:]).then_inc(h2t_done, 1)

                def query(b):
                    act.wait_ge(q_done, 4 * t + b + 1)
                    if is_first(t):
                        act.wait_ge(key_t, 4)
                    else:
                        act.wait_ge(s_done, 4 * (t - 1) + b + 1)
                    nc.scalar.copy(qt[:, 4 * b:4 * b + 4, :].rearrange("p a n -> p (a n)"), ps_q[b % 2][:]).then_inc(qt_done, 1)

                def score(b):
                    act.wait_ge(s_done, 4 * t + b + 1)
                    if not is_first(t):
                        act.wait_ge(picked, t)
                    nc.scalar.copy(sc[:, 4 * b:4 * b + 4, :].rearrange("p a n -> p (a n)"), ps_s[b % 2][:]).then_inc(sc_done, 1)

                query(0)
                for b in range(1, 4):
                    query(b)
                    score(b - 1)
                score(3)
                act.wait_ge(ex_in, t + 1)
                nc.scalar.activation(ex[:], ex[:], ACT.Exp).then_inc(ex_done, 1)

            square(0)
            square(1)
            outs(0)
            with act.Fori(0, LAT - 1) as i:
                square(i + 2)
                outs(i + 1)
            outs(LAT)

        @block.vector
        def _(dve):
            s_ = Steps(dve, step)

            def carry():
                nc.vector.memset(hold[:], 0.0)

            def norm(t):
                if not is_first(t):
                    dve.wait_ge(st_x1, 16 * t)
                    dve.wait_ge(ss_done, t)
                dve.wait_ge(x_in, 16 * t + 16)
                for b in range(2):
                    half_ = slice(b * 512, (b + 1) * 512)
                    dve.wait_ge(y_done, 2 * t + b + 1)
                    s_.link(nc.vector.tensor_tensor(x1[:, half_], ps_y[b][:], gate1[:, half_], ALU.mult))
                    nc.vector.tensor_tensor(x1[:, half_], x1[:, half_], x[:, half_], ALU.add).then_inc(x1_done, 1)
                dve.wait_ge(ss_done, t + 1)
                nc.vector.tensor_scalar(ss[:, 1:2], ss[:, 0:1], 1.0 / D, EPS, ALU.mult, ALU.add).then_inc(ms_done, 1)
                dve.wait_ge(rstd_done, t + 1)
                if not is_first(t):
                    dve.wait_ge(h2_t, 2 * t)
                    dve.wait_ge(st_h2, 16 * t)
                s_.link(nc.vector.scalar_tensor_tensor(out=h2[:], in0=x1[:], scalar=ss[:, 2:3], in1=scale2[:], op0=ALU.mult, op1=ALU.mult))
                nc.vector.tensor_tensor(h2[:], h2[:], shift2[:], ALU.add).then_inc(h2_done, 1)

            def top16(rows, values, indices):
                n = len(rows)
                for r in range(n):
                    last = nc.vector.max(values[r][:, 0:8], rows[r])
                s_.link(last)
                carry()
                for r in range(n):
                    nc.vector.max_index(indices[r][:, 0:8], values[r][:, 0:8], rows[r])
                for r in range(n):
                    last = nc.vector.match_replace(rows[r], values[r][:, 0:8], rows[r], BIG)
                s_.link(last)
                carry()
                for r in range(n):
                    last = nc.vector.max(values[r][:, 8:16], rows[r])
                s_.link(last)
                carry()
                for r in range(n):
                    last = nc.vector.max_index(indices[r][:, 8:16], values[r][:, 8:16], rows[r])
                s_.link(last)

            FULL = [P, PH, TOPK, TOPK]

            def picks(t):
                dve.wait_ge(sc_done, 4 * t + 4)
                carry()
                hp = [(h, a) for h in range(PH) for a in range(2)]
                top16([sc[:, r, :] for r in range(HP)], [v16[:, h, a, :] for h, a in hp], [i16[:, h, a, :] for h, a in hp])
                nc.vector.tensor_copy(i16f[:], i16[:]).then_inc(picked, 1)
                s_.link(nc.vector.tensor_tensor(cand[:], v16[:, :, 0, :].unsqueeze(3).to_broadcast(FULL),
                                                v16[:, :, 1, :].unsqueeze(2).to_broadcast(FULL), ALU.add))
                carry()
                top16([cand[:, h].rearrange("p a b -> p (a b)") for h in range(PH)], [vs[:, h, :] for h in range(PH)],
                      [ic[:, h, :] for h in range(PH)])
                if not is_first(t):
                    dve.wait_ge(ex_done, t)
                nc.vector.tensor_tensor(ex[:], vs[:], vs[:, :, 0:1].to_broadcast([P, PH, TOPK]), ALU.subtract).then_inc(ex_in, 1)
                for a in range(2):
                    op, by = ((ALU.logical_shift_right, 4), (ALU.bitwise_and, TOPK - 1))[a]
                    s_.link(nc.vector.tensor_scalar(part[:], ic[:], by, None, op))
                    s_.link(nc.vector.tensor_copy(partf[:], part[:]))
                    s_.link(nc.vector.tensor_tensor(oh[:], partf[:].unsqueeze(3).to_broadcast(FULL),
                                                    iota[:].unsqueeze(1).unsqueeze(1).to_broadcast(FULL), ALU.is_equal))
                    s_.link(nc.vector.tensor_tensor(oh[:], oh[:], i16f[:, :, a, :].unsqueeze(2).to_broadcast(FULL), ALU.mult))
                    s_.link(nc.vector.tensor_reduce(e12[a][:], oh[:], AX_X, ALU.add))
                if not is_first(t):
                    dve.wait_ge(st_ids, 16 * t)
                    dve.wait_ge(st_gw, 16 * t)
                nc.vector.scalar_tensor_tensor(out=ids[:], in0=e12[0][:], scalar=float(P), in1=e12[1][:], op0=ALU.mult, op1=ALU.add).then_inc(ids_done, 1)
                dve.wait_ge(ex_done, t + 1)
                s_.link(nc.vector.tensor_reduce(tot[:], ex[:], AX_X, ALU.add))
                s_.link(nc.vector.reciprocal(tot[:], tot[:]))
                nc.vector.tensor_tensor(gw[:], ex[:], tot[:].unsqueeze(2).to_broadcast([P, PH, TOPK]), ALU.mult).then_inc(gw_done, 1)

            def scale_rows():
                s_.link(nc.vector.scalar_tensor_tensor(out=scale2[:], in0=scale2[:], scalar=1.0, in1=gain2[:], op0=ALU.add, op1=ALU.mult))

            dve.wait_ge(rows_in, 64)
            dve.wait_ge(small_in, 16)
            scale_rows()
            norm(0)
            dve.wait_ge(rows2_in, 48)
            scale_rows()
            norm(1)
            picks(0)
            with dve.Fori(0, LAT - 1) as i:
                s_.enter(i, 3 + 4 + 1 + 4 + 10 + 2)
                norm(i + 2)
                picks(i + 1)
            s_.leave(LAT - 1)
            picks(LAT)


def experts(nc, T, keep):
    R = 16
    NG = PICKS // R
    with nc.cleanup_on_exit(), ExitStack() as ctx:
        sb = lambda n, s, d=F32: ctx.enter_context(nc.sbuf_tensor(n, s, d))
        sem = nc.alloc_semaphore
        ring_u = sb("ex_ring_u", [P, R, D])
        ring_v = sb("ex_ring_v", [P, R, D])
        ids = [sb(f"ex_ids{u}", [P, PICKS], U32) for u in range(2)]
        gw = [sb(f"ex_gw{u}", [P, PICKS]) for u in range(2)]
        h2 = [sb(f"ex_h2{u}", [P, D]) for u in range(2)]
        x1 = [sb(f"ex_x1{u}", [P, D]) for u in range(2)]
        idx_u, idx_v = ([sb(f"ex_idx_{n}{b}", [P, R], U32) for b in range(2)] for n in "uv")
        hold = sb("ex_hold", [P, 1])
        gate2, gfin = sb("ex_gate2", [P, D]), sb("ex_gfin", [P, D])
        dots = sb("ex_dots", [P, PICKS])
        gelu = sb("ex_gelu", [P, PICKS])
        wts = sb("ex_wts", [P, PICKS])
        acc = [sb(f"ex_acc{a}", [P, D]) for a in range(2)]
        x2 = sb("ex_x2", [P, D])
        y = sb("ex_y", [P, D])
        ss = sb("ex_ss", [P, 5])
        rows_in, rows2_in = sem("ex_rows_in"), sem("ex_rows2_in")
        tile_in = [sem(f"ex_tile_in{u}") for u in range(2)]
        u_in, v_in = [sem(f"ex_u_in{k}") for k in range(R)], [sem(f"ex_v_in{k}") for k in range(R)]
        used_u, used_v, copied_u, copied_v, waited = (sem(f"ex_{n}") for n in ("used_u", "used_v", "copied_u", "copied_v", "waited"))
        dots_done, gelu_done, x2_done, ss_done, ms_done, root_done, y_done, stored, step = (
            sem(f"ex_{n}") for n in ("dots", "gelu", "x2", "ss", "ms", "root", "y", "stored", "step"))
        block = ctx.enter_context(nc.Block())

        @block.sync
        def _(sp):
            def load(t, u, n):
                if not isinstance(t, int) or t >= 2:
                    sp.wait_ge(y_done, t - 1)
                sp.dma_start(ids[u][:], row(T["ids"], t)).then_inc(tile_in[u], 16)
                sp.dma_start(gw[u][:], row(T["gw"], t)).then_inc(tile_in[u], 16)
                sp.dma_start(h2[u][:], row(T["h2"], t)).then_inc(tile_in[u], 16)
                sp.dma_start(x1[u][:], row(T["x1"], t)).then_inc(tile_in[u], 16)

            y_lat = T["y_sample"][0].rearrange("(t p) d -> t p d", p=P)

            def store(t):
                sp.wait_ge(y_done, t + 1)
                sp.dma_start(row(y_lat, t - 1), y[:]).then_inc(stored, 16)

            load(0, 1, 0)
            sp.dma_start(gate2[:], T["mod"][0:1, 5 * D:6 * D].to_broadcast([P, D])).then_inc(rows_in, 16)
            sp.dma_start(gfin[:], T["g_final"].rearrange("(a d) -> a d", a=1).to_broadcast([P, D])).then_inc(rows_in, 16)
            load(1, 0, 0)
            sp.wait_ge(y_done, 1)
            sp.dma_start(T["y_prompt"][0], y[:]).then_inc(stored, 16)
            sp.dma_start(gate2[:], T["mod"][1:2, 5 * D:6 * D].to_broadcast([P, D])).then_inc(rows2_in, 16)
            load(2, 1, 1)
            store(1)
            with sp.Fori(0, LAT // 2 - 1) as i:
                for u in range(2):
                    load(2 * i + (3 + u), u, i + 1 + u)
                    store(2 * i + (2 + u))
            store(LAT)
            sp.wait_ge(stored, 16 * TILES)

        @block.gpsimd
        def _(pool):
            def tile(t, u, n):
                pool.wait_ge(tile_in[u], 64 * n + 64)
                pool.sem_inc(waited, 1)
                for table, ring, idx, used, arrived, copied in (
                        (T["peer_u"], ring_u, idx_u, used_u, u_in, copied_u), (T["peer_v"], ring_v, idx_v, used_v, v_in, copied_v)):
                    with pool.Fori(0, NG // 2) as g2:
                        for b in range(2):
                            q = t * NG + g2 * 2 + b
                            pool.wait_ge(used, q * R + 1)
                            nc.gpsimd.tensor_copy(idx[b][:], cols(ids[u], g2 * (2 * R) + b * R, R)).then_inc(copied, 1)
                            pool.wait_ge(copied, q + 1)
                            pool.sem_inc(waited, 1)
                            for k in range(R):
                                if k:
                                    pool.wait_ge(used, q * R + k + 1)
                                    pool.sem_inc(waited, 1)
                                nc.gpsimd.indirect_dma_start(ring[:, k, :], None, table[0], bass.IndirectOffsetOnAxis(
                                    ap=idx[b][:, k:k + 1], axis=0)).then_inc(arrived[k], 16)

            pairs(pool, tile)

        @block.scalar
        def _(act):
            def tile(t, u, n):
                act.wait_ge(dots_done, t + 1)
                nc.scalar.activation(gelu[:], dots[:], ACT.Gelu_apprx_tanh).then_inc(gelu_done, 1)
                act.wait_ge(x2_done, t + 1)
                nc.scalar.activation(acc[1][:], x2[:], ACT.Square, accum_out=ss[:, 0:1]).then_inc(ss_done, 1)
                act.wait_ge(ms_done, t + 1)
                nc.scalar.activation(ss[:, 2:3], ss[:, 1:2], ACT.Sqrt).then_inc(root_done, 1)

            pairs(act, tile)

        @block.vector
        def _(dve):
            s_ = Steps(dve, step)
            nc.vector.memset(ss[:, 0:1], 0.0).then_inc(used_u, R)
            nc.vector.memset(ss[:, 1:2], 0.0).then_inc(used_v, R)
            dve.wait_ge(rows_in, 32)

            def tile(t, u, n):
                dve.wait_ge(tile_in[u], 64 * n + 64)
                nc.vector.memset(hold[:], 0.0)
                with dve.Fori(0, NG) as g:
                    q = t * NG + g
                    for k in range(R):
                        dve.wait_ge(u_in[k], 16 * q + 16)
                        nc.vector.scalar_tensor_tensor(out=ring_u[:, k, :], in0=ring_u[:, k, :], scalar=1.0, in1=h2[u][:], op0=ALU.mult, op1=ALU.mult,
                                                       accum_out=cols(dots, g * R + k, 1)).then_inc(used_u, 1)
                dve.wait_ge(used_u, (t + 1) * PICKS + R)
                if not is_first(t):
                    dve.wait_ge(ss_done, t)
                nc.vector.memset(acc[0][:], 0.0).then_inc(dots_done, 1)
                s_.link(nc.vector.memset(acc[1][:], 0.0))
                dve.wait_ge(gelu_done, t + 1)
                s_.link(nc.vector.tensor_tensor(wts[:], gelu[:], gw[u][:], ALU.mult))
                nc.vector.memset(hold[:], 0.0)
                with dve.Fori(0, NG) as g:
                    q = t * NG + g
                    for k in range(R):
                        dve.wait_ge(v_in[k], 16 * q + 16)
                        dve.wait_ge(used_v, q * R + k + (R - 1))
                        nc.vector.scalar_tensor_tensor(out=acc[k % 2][:], in0=ring_v[:, k, :], scalar=cols(wts, g * R + k, 1),
                                                       in1=acc[k % 2][:], op0=ALU.mult, op1=ALU.add).then_inc(used_v, 1)
                dve.wait_ge(used_v, (t + 1) * PICKS + R)
                s_.link(nc.vector.tensor_tensor(acc[0][:], acc[0][:], acc[1][:], ALU.add))
                s_.link(nc.vector.tensor_tensor(acc[0][:], acc[0][:], gate2[:], ALU.mult))
                nc.vector.tensor_tensor(x2[:], acc[0][:], x1[u][:], ALU.add).then_inc(x2_done, 1)
                dve.wait_ge(ss_done, t + 1)
                nc.vector.tensor_scalar(ss[:, 1:2], ss[:, 0:1], 1.0 / D, EPS, ALU.mult, ALU.add).then_inc(ms_done, 1)
                dve.wait_ge(root_done, t + 1)
                s_.link(nc.vector.reciprocal(ss[:, 3:4], ss[:, 2:3]))
                s_.link(nc.vector.scalar_tensor_tensor(out=ss[:, 4:5], in0=ss[:, 3:4], scalar=ss[:, 1:2], in1=ss[:, 3:4], op0=ALU.mult, op1=ALU.mult))
                s_.link(nc.vector.tensor_scalar(ss[:, 4:5], ss[:, 4:5], -0.5, 1.5, ALU.mult, ALU.add))
                s_.link(nc.vector.tensor_tensor(ss[:, 4:5], ss[:, 4:5], ss[:, 3:4], ALU.mult))
                if not is_first(t):
                    dve.wait_ge(stored, 16 * t)
                nc.vector.scalar_tensor_tensor(out=y[:], in0=x2[:], scalar=ss[:, 4:5], in1=gfin[:], op0=ALU.mult, op1=ALU.mult).then_inc(y_done, 1)

            tile(0, 1, 0)
            dve.wait_ge(rows2_in, 16)
            with dve.Fori(0, LAT // 2) as i:
                s_.enter(i, 2 * 8)
                for u in range(2):
                    tile(2 * i + (1 + u), u, i + u)
            s_.leave(LAT // 2)


SCRATCH = {"mod": [2, 6 * D], "ht": [TILES, P, D], "kv": [TILES, P, 2 * MIX], "og": [TILES, P, MIX],
           "qat": [TILES, AD, AH * P], "qkt": [TILES, P, 2 * MIX], "yct": [TILES, P, MIX],
           "yt": [TILES, P, 2 * MIX], "mt": [TILES, P, D], "x1": [TILES, P, D], "h2": [TILES, P, D],
           "gw": [TILES, P, PICKS], "ids": [TILES, P, PICKS]}


class Keep:
    pass


def trunk(nc, ins, outs, phases=99, debug=False):
    kind = {"kind": "ExternalOutput"} if debug else {}
    scratch = {name: nc.dram_tensor(f"s_{name}", shape, U32 if name == "ids" else F32, **kind).ap() for name, shape in SCRATCH.items()}
    T = {**ins, **outs, **scratch}
    modulate(nc, T)
    keep = Keep()
    with ExitStack() as ctx:
        keep.ident = ctx.enter_context(nc.sbuf_tensor("ident", [P, P], F32))
        with ExitStack() as mixer:
            keep.gates = mixer.enter_context(nc.sbuf_tensor("gates", [P, TILES, 16], F32))
            keep.kat = mixer.enter_context(nc.sbuf_tensor("kat", [AD, AKV, (TILES + 1) * P], F32))
            keep.va = mixer.enter_context(nc.sbuf_tensor("va", [P, TILES + 1, P], F32))
            project(nc, T, keep)
            keep.hd = mixer.enter_context(nc.sbuf_tensor("hd", [P, 2, TILES * MIX], F32))
            mlstm(nc, T, keep)
            attend(nc, T, keep)
        for n, phase in enumerate((merge, route, experts)):
            if n < phases:
                phase(nc, T, keep)


_INS = ['x_prompt', 'x_sample', 'cache_k', 'cache_v', 'state_C', 'state_n', 'state_m', 'c', 'c_ctx',
        'w_ada', 'b_ada', 'g_norm1', 'g_norm2', 'w_in', 'b_gates_m', 'g_mlstm', 'w_spatial', 'b_spatial', 'sink',
        'w_branch', 'w_merge', 'b_merge', 'w_out', 'w_peer_q', 'peer_keys', 'peer_u', 'peer_v', 'g_final']
_OUTS = [("y_prompt", (1, P, D)), ("y_sample", (1, LAT * P, D)), ("new_k", (1, 1, P, AKV, AD)), ("new_v", (1, 1, P, AKV, AD)),
         ("new_C", (1, 1, 2, MH, MD, MD)), ("new_n", (1, 1, 2, MH, MD)), ("new_m", (1, 1, 2, MH))]


def kernel(**inputs):
    import concourse.bacc as bacc
    from concourse.bass_utils import run_bass_kernel_spmd

    nc = bacc.Bacc("TRN2", target_bir_lowering=False, num_devices=1)
    arrays, ins, outs = {}, {}, {}
    given = {name: np.ascontiguousarray(inputs[name]) for name in _INS}
    for name, a in {**given, **host_constants()}.items():
        arrays[f"in_{name}"] = a
        ins[name] = nc.dram_tensor(f"in_{name}", a.shape, mybir.dt.from_np(a.dtype), kind="ExternalInput").ap()
    for name, shape in _OUTS:
        outs[name] = nc.dram_tensor(f"out_{name}", shape, F32, kind="ExternalOutput").ap()
    trunk(nc, ins, outs)
    r = run_bass_kernel_spmd(nc, [arrays], core_ids=[0])
    return tuple(r.results[0][f"out_{name}"] for name, _ in _OUTS)
```

```python
from contextlib import ExitStack

import numpy as np

import concourse.bass as bass
from concourse import mybir

F32 = mybir.dt.float32
U32 = mybir.dt.uint32
ALU = mybir.AluOpType
ACT = mybir.ActivationFunctionType
AX_X = mybir.AxisListType.X

P = 128
D = 1024
DC = D // P
LAT = 8
TILES = 1 + LAT
EPS = 1e-6
MIX = D // 2
MH, MD = 4, 128
AH, AKV, AD = 8, 2, 64
IN_W = 7 * MIX + 4 * MH + 2 * AKV * AD
NEXP = 16384
PH, TOPK = 8, 16
PICKS = PH * TOPK
HP = 2 * PH
GRID_W = 64
NEG = -1e30
BIG = -3.0e38


class Steps:

    def __init__(self, eng, sem):
        self.eng, self.sem, self.base, self.n, self.i, self.per = eng, sem, 0, 0, None, 0

    def enter(self, i, per):
        self.base, self.n, self.i, self.per = self.base + self.n, 0, i, per

    def leave(self, turns):
        assert self.n == self.per, f"{self.sem}: {self.n} steps a turn, {self.per} said"
        self.base, self.n, self.i = self.base + self.per * turns, 0, None

    def value(self):
        flat = self.base + self.n
        return flat if self.i is None else self.i * self.per + flat

    def link(self, ins):
        ins.then_inc(self.sem, 1)
        self.n += 1
        self.eng.wait_ge(self.sem, self.value())


def is_first(t):
    return isinstance(t, int) and t == 0


def cols(ap, a, n):
    return ap[:, bass.ds(a, n)]


def row(ap, t):
    return ap[bass.ds(t, 1)].rearrange("a p n -> (a p) n")


def host_constants():
    n = LAT * P
    pos = np.arange(n)
    freqs = 10000.0 ** (-np.arange(16, dtype=np.float32) / 16)
    tabs = []
    for axis in (pos // GRID_W, pos % GRID_W):
        ang = axis.astype(np.float32)[:, None] * freqs[None, :].astype(np.float32)
        tabs.append((np.cos(ang), np.sin(ang)))
    cos = np.concatenate([tabs[0][0], tabs[0][0], tabs[1][0], tabs[1][0]], 1).astype(np.float32)
    sin = np.concatenate([-tabs[0][1], tabs[0][1], -tabs[1][1], tabs[1][1]], 1).astype(np.float32)
    rope = np.concatenate([cos, sin], 1).reshape(LAT, P, 2 * AD)
    q, k = np.arange(P)[:, None], np.arange(3 * P)[None, :] - P
    band = np.where(np.abs(q - k) <= P, 0.0, NEG * 8)
    win = np.zeros((LAT, P, 4 * P), np.float32)
    for t in range(LAT):
        win[t, :, P:] = band
        if t == 0:
            win[t, :, P:2 * P] = NEG * 8
        if t == LAT - 1:
            win[t, :, 3 * P:] = NEG * 8
    s, tt = np.arange(P)[:, None], np.arange(P)[None, :]
    causal = np.stack([np.where(s <= tt, 0.0, NEG), np.where(s >= tt, 0.0, NEG)]).astype(np.float32)
    restart = np.ones((MH, 2, TILES, P), np.float32)
    restart[:, 0, :, 0] = 0.0
    restart[:, 1, :, P - 1] = 0.0
    head_row = np.zeros((MH, MH, P), np.float32)
    for h in range(MH):
        head_row[h, h] = 1.0
    return {
        "const_ident": np.eye(P, dtype=np.float32), "const_rope": rope, "const_window": win,
        "const_causal": causal, "const_restart": restart.reshape(MH, -1),
        "const_head_row": head_row.reshape(MH, -1),
        "const_iota": np.tile(np.arange(TOPK, dtype=np.float32), (P, 1)),
    }


def modulate(nc, T):
    NB = 6 * D // 512
    with nc.cleanup_on_exit(), ExitStack() as ctx:
        sb = lambda n, s, d=F32: ctx.enter_context(nc.sbuf_tensor(n, s, d))
        sem = nc.alloc_semaphore
        cond = sb("mo_cond", [P, 2, DC])
        act = sb("mo_silu", [P, DC, 2])
        wa = [sb(f"mo_w{u}", [P, DC, 512]) for u in range(2)]
        bias = sb("mo_bias", [2, 6 * D])
        mod = sb("mo_mod", [2, 6 * D])
        ps = [ctx.enter_context(nc.psum_tensor(f"mo_ps{u}", [P, 512], F32)) for u in range(2)]
        cond_in, bias_in, silu_done = sem("mo_cond_in"), sem("mo_bias_in"), sem("mo_silu_done")
        w_in_ = [sem(f"mo_w_in{u}") for u in range(2)]
        prod, mod_done, stored = sem("mo_prod"), sem("mo_mod_done"), sem("mo_stored")
        w_view = T["w_ada"][0].rearrange("(k p) n -> p k n", p=P)
        block = ctx.enter_context(nc.Block())

        @block.sync
        def _(sp):
            sp.dma_start(cond[:, 0, :], T["c_ctx"].rearrange("(k p) -> p k", p=P), allow_slow_non_contiguous=True).then_inc(cond_in, 16)
            sp.dma_start(cond[:, 1, :], T["c"][0].rearrange("(k p) -> p k", p=P), allow_slow_non_contiguous=True).then_inc(cond_in, 16)
            sp.dma_start(bias[:], T["b_ada"].to_broadcast([2, 6 * D])).then_inc(bias_in, 16)
            for u in range(2):
                sp.dma_start(wa[u][:], w_view[:, :, u * 512:u * 512 + 512]).then_inc(w_in_[u], 16)
            with sp.Fori(1, NB // 2) as i:
                for u in range(2):
                    sp.wait_ge(prod, 2 * i + u - 1)
                    sp.dma_start(wa[u][:], w_view[:, :, bass.ds((2 * i + u) * 512, 512)]).then_inc(w_in_[u], 16)
            sp.wait_ge(mod_done, NB)
            sp.dma_start(T["mod"], mod[:]).then_inc(stored, 16)
            sp.wait_ge(stored, 16)

        @block.scalar
        def _(act_eng):
            act_eng.wait_ge(cond_in, 32)
            nc.scalar.activation(act[:].rearrange("p k c -> p c k"), cond[:], ACT.Silu).then_inc(silu_done, 1)

        @block.tensor
        def _(pe):
            pe.wait_ge(silu_done, 1)

            def column_block(i, u, first):
                pe.wait_ge(w_in_[u], 16 * i + 16)
                if not first:
                    pe.wait_ge(mod_done, 2 * i + u - 1)
                for k in range(DC):
                    mm = nc.tensor.matmul(ps[u][0:2, :], act[:, k, :], wa[u][:, k, :], start=(k == 0), stop=(k == DC - 1))
                mm.then_inc(prod, 1)

            column_block(0, 0, True)
            column_block(0, 1, True)
            with pe.Fori(1, NB // 2) as i:
                for u in range(2):
                    column_block(i, u, False)

        @block.vector
        def _(dve):
            dve.wait_ge(bias_in, 16)
            with dve.Fori(0, NB // 2) as i:
                for u in range(2):
                    dve.wait_ge(prod, 2 * i + u + 1)
                    at = (2 * i + u) * 512
                    nc.vector.tensor_tensor(cols(mod, at, 512), ps[u][0:2, :], cols(bias, at, 512),
                                            ALU.add).then_inc(mod_done, 1)


def load_norm_rows(sp, T, scale_t, shift_t, gain_t, row, sc_col, sh_col, gain, done):
    sp.dma_start(scale_t, T["mod"][row:row + 1, sc_col * D:(sc_col + 1) * D].to_broadcast([P, D])).then_inc(done, 16)
    sp.dma_start(shift_t, T["mod"][row:row + 1, sh_col * D:(sh_col + 1) * D].to_broadcast([P, D])).then_inc(done, 16)
    sp.dma_start(gain_t, gain.to_broadcast([P, D])).then_inc(done, 16)


Q0, K0, V0, O0, G0, U0, S0, A0 = 0, MIX, 2 * MIX, 3 * MIX, 4 * MIX, 4 * MIX + 16, 5 * MIX + 16, 6 * MIX + 16


def project(nc, T, keep):
    with nc.cleanup_on_exit(), ExitStack() as ctx:
        sb = lambda n, s, d=F32: ctx.enter_context(nc.sbuf_tensor(n, s, d))
        sem = nc.alloc_semaphore
        bank = lambda n: ctx.enter_context(nc.psum_tensor(n, [P, 512], F32))
        ident, gates, kat, va = keep.ident, keep.gates, keep.kat, keep.va
        w = sb("pj_w", [P, DC, IN_W])
        x = sb("pj_x", [P, D])
        h = sb("pj_h", [P, D])
        scale1, shift1 = sb("pj_scale1", [P, D]), sb("pj_shift1", [P, D])
        ht = sb("pj_ht", [P, DC, P])
        qkv = sb("pj_qkv", [P, 3 * MIX])
        og = sb("pj_og", [P, MIX])
        u = sb("pj_u", [P, MIX])
        sv = sb("pj_sv", [P, MIX])
        vr = sb("pj_vr", [P, MIX])
        yc = sb("pj_yc", [P, MIX])
        qka = sb("pj_qka", [P, MIX + 2 * AKV * AD])
        rot_c = sb("pj_rot_c", [P, 10, AD])
        rot_s = sb("pj_rot_s", [P, 10, 2, 2, 16])
        qr = sb("pj_qr", [P, 10, AD])
        qkt = sb("pj_qkt", [P, 2 * MIX])
        qat = sb("pj_qat", [AD, AH * P])
        yct = sb("pj_yct", [P, MIX])
        rope = sb("pj_rope", [P, 2 * AD])
        ws = sb("pj_ws", [P, 4, P])
        wst = sb("pj_wst", [P, 4, P])
        bs = sb("pj_bs", [P, 4])
        gb = sb("pj_gb", [P, 16])
        ss = sb("pj_ss", [P, 8])
        half = sb("pj_half", [P, 1])
        gain1 = sb("pj_gain1", [P, D])
        ps_x = ctx.enter_context(nc.psum_tensor("pj_ps_x", [P, 2, 512], F32))
        ps_z = [bank(f"pj_ps_z{b}") for b in range(3)]
        ps_t = [bank(f"pj_ps_t{b}") for b in range(2)]
        ps_m = bank("pj_ps_m")

        w_in_ = [sem(f"pj_w_in{k}") for k in range(DC)]
        rows_in, small_in, rope_in, x_in = sem("pj_rows_in"), sem("pj_small_in"), sem("pj_rope_in"), sem("pj_x_in")
        rows2_in, half_set = sem("pj_rows2_in"), sem("pj_half_set")
        ws_t, ws_done = sem("pj_ws_t"), sem("pj_ws_done")
        ss_done, ms_done, rstd_done = sem("pj_ss_done"), sem("pj_ms_done"), sem("pj_rstd_done")
        h_done, x_t, ht_done = sem("pj_h_done"), sem("pj_x_t"), sem("pj_ht_done")
        z_done, z_act, z_dve = sem("pj_z_done"), sem("pj_z_act"), sem("pj_z_dve")
        ssv_done, msv_done, rstdv_done, vr_done = sem("pj_ssv"), sem("pj_msv"), sem("pj_rstdv"), sem("pj_vr_done")
        qr_done, gm_done, yc_done = sem("pj_qr_done"), sem("pj_gm_done"), sem("pj_yc_done")
        t_done, t_out = sem("pj_t_done"), sem("pj_t_out")
        st_h, st_qa, st_qk, st_kv, st_o, st_yc, st_new = (sem(f"pj_st_{n}") for n in ("h", "qa", "qk", "kv", "o", "yc", "new"))
        step = sem("pj_dve_step")
        block = ctx.enter_context(nc.Block())

        ZB = [(A0, 512, "d"), (A0 + 512, 256, "d"), (S0, 512, "a"), (U0, 512, "a"), (Q0, 512, "d"),
              (K0, 512, "a"), (V0, 512, "d"), (O0, 512, "a"), (G0, 16, "d")]
        NZ = len(ZB)
        NT = 6
        per = {"d": sum(b[2] == "d" for b in ZB), "a": sum(b[2] == "a" for b in ZB)}
        rank = [sum(c[2] == b[2] for c in ZB[:j + 1]) for j, b in enumerate(ZB)]
        zsem = {"d": z_dve, "a": z_act}

        @block.sync
        def _(sp):
            sp.dma_start(ident[:], T["const_ident"]).then_inc(small_in, 16)
            load_norm_rows(sp, T, scale1[:], shift1[:], gain1[:], 0, 1, 0, T["g_norm1"], rows_in)
            sp.dma_start(ws[:], T["w_spatial"][0].rearrange("g p q -> p g q")).then_inc(small_in, 16)
            sp.dma_start(bs[:], T["b_spatial"][0].rearrange("g p -> p g"), allow_slow_non_contiguous=True).then_inc(small_in, 16)
            sp.dma_start(gb[:], T["b_gates_m"].rearrange("a g h -> a (g h)").to_broadcast([P, 16])).then_inc(small_in, 16)
            for k in range(DC):
                sp.dma_start(w[:, k, :], T["w_in"][0, k * P:(k + 1) * P, :]).then_inc(w_in_[k], 16)

            def stores(t):
                sp.wait_ge(ht_done, 2 * t + 2)
                sp.dma_start(row(T["ht"], t), ht[:].rearrange("p k n -> p (k n)")).then_inc(st_h, 16)
                if is_first(t):
                    sp.wait_ge(z_dve, 2)
                    sp.dma_start(T["new_k"][0, 0].rearrange("s k d -> s (k d)"), qka[:, 512:640]).then_inc(st_new, 16)
                    sp.dma_start(T["new_v"][0, 0].rearrange("s k d -> s (k d)"), qka[:, 640:768]).then_inc(st_new, 16)
                sp.wait_ge(z_act, t * per["a"] + rank[5])
                sp.wait_ge(z_dve, t * per["d"] + rank[6])
                sp.dma_start(row(T["kv"], t), qkv[:, MIX:]).then_inc(st_kv, 16)
                sp.wait_ge(z_act, t * per["a"] + rank[7])
                sp.dma_start(row(T["og"], t), og[:]).then_inc(st_o, 16)
                sp.wait_ge(t_out, t * NT + 2)
                sp.dma_start(row(T["qat"], t), qat[:]).then_inc(st_qa, 16)
                sp.wait_ge(t_out, t * NT + 5)
                sp.dma_start(row(T["qkt"], t), qkt[:]).then_inc(st_qk, 16)
                sp.wait_ge(t_out, t * NT + 6)
                sp.dma_start(row(T["yct"], t), yct[:]).then_inc(st_yc, 16)

            stores(0)
            with sp.Fori(0, LAT) as i:
                stores(i + 1)
            for s in (st_h, st_qa, st_qk, st_kv, st_o, st_yc):
                sp.wait_ge(s, 16 * TILES)

        @block.gpsimd
        def _(pool):
            nc.gpsimd.memset(half[:], -0.5).then_inc(half_set, 1)
            nc.gpsimd.memset(kat[:, :, TILES * P:], 0.0).then_inc(half_set, 1)
            nc.gpsimd.memset(va[:, TILES, :], 0.0).then_inc(half_set, 1)
            pool.wait_ge(half_set, 3)

            def rsqrt(t, ready, a, b, done):
                pool.wait_ge(ready, t + 1)
                nc.gpsimd.tensor_tensor(ss[:, b:b + 1], ss[:, a:a + 1], half[:], ALU.pow).then_inc(done, 1)

            pool.dma_start(x[:], T["x_prompt"][0]).then_inc(x_in, 16)
            rsqrt(0, ms_done, 1, 2, rstd_done)
            pool.wait_ge(h_done, 1)
            for tile_, col in ((scale1, 1), (shift1, 0)):
                pool.dma_start(tile_[:], T["mod"][1:2, col * D:(col + 1) * D].to_broadcast([P, D])).then_inc(rows2_in, 16)
            rsqrt(0, msv_done, 4, 5, rstdv_done)
            with pool.Fori(0, LAT) as i:
                pool.wait_ge(h_done, i + 1)
                pool.wait_ge(half_set, 1)
                pool.dma_start(x[:], T["x_sample"][0].rearrange("(t p) d -> t p d", p=P)[bass.ds(i, 1)].rearrange(
                    "a p d -> (a p) d")).then_inc(x_in, 16)
                rsqrt(i + 1, ms_done, 1, 2, rstd_done)
                pool.wait_ge(qr_done, i + 1)
                pool.wait_ge(half_set, 1)
                pool.dma_start(rope[:], row(T["const_rope"], i)).then_inc(rope_in, 16)
                rsqrt(i + 1, msv_done, 4, 5, rstdv_done)

        @block.tensor
        def _(pe):
            pe.wait_ge(small_in, 64)
            for g in range(4):
                tr = nc.tensor.transpose(ps_m[:, g * P:(g + 1) * P], ws[:, g, :], ident[:])
            tr.then_inc(ws_t, 1)

            def tile(t):
                pe.wait_ge(h_done, t + 1)
                if not is_first(t):
                    pe.wait_ge(ht_done, 2 * t)
                for k in range(DC):
                    tr = nc.tensor.transpose(ps_x[:, k // 4, (k % 4) * P:(k % 4 + 1) * P], h[:, k * P:(k + 1) * P], ident[:])
                    if k % 4 == 3:
                        tr.then_inc(x_t, 1)
                pe.wait_ge(ht_done, 2 * t + 2)
                for j, (c0, n, _) in enumerate(ZB):
                    if not is_first(t) or j >= 3:
                        prev = j - 3 if j >= 3 else j - 3 + NZ
                        eng = ZB[prev][2]
                        back = t if j >= 3 else t - 1
                        pe.wait_ge(zsem[eng], back * per[eng] + rank[prev])
                    for k in range(DC):
                        if is_first(t) and j == 0:
                            pe.wait_ge(w_in_[k], 16)
                        mm = nc.tensor.matmul(ps_z[j % 3][:, 0:n], ht[:, k, :], w[:, k, c0:c0 + n], start=(k == 0), stop=(k == DC - 1))
                    mm.then_inc(z_done, 1)

                def group(g, n, src, ready, value, rows=P):
                    pe.wait_ge(ready, value)
                    if not is_first(t) or g >= 2:
                        pe.wait_ge(t_out, t * NT + g - 1)
                    for a in range(n):
                        dst = ps_t[g % 2][0:rows, a * P:(a + 1) * P]
                        if rows < P:
                            tr = nc.tensor.matmul(dst, src(a), ident[:], start=True, stop=True)
                        else:
                            tr = nc.tensor.transpose(dst, src(a), ident[:])
                    tr.then_inc(t_done, 1)

                group(0, 4, lambda a: qr[:, a, :], qr_done, t + 1, AD)
                group(1, 4, lambda a: qr[:, 4 + a, :], qr_done, t + 1, AD)
                group(2, 2, lambda a: qr[:, 8 + a, :], qr_done, t + 1, AD)
                group(3, 4, lambda a: qkv[:, a * P:(a + 1) * P], z_dve, t * per["d"] + rank[4])
                group(4, 4, lambda a: qkv[:, MIX + a * P:MIX + (a + 1) * P], z_act, t * per["a"] + rank[5])
                pe.wait_ge(vr_done, t + 1)
                if is_first(t):
                    pe.wait_ge(ws_done, 1)
                else:
                    pe.wait_ge(yc_done, t)
                for g in range(4):
                    mm = nc.tensor.matmul(ps_m[:, g * P:(g + 1) * P], wst[:, g, :], vr[:, g * P:(g + 1) * P], start=True, stop=True)
                mm.then_inc(gm_done, 1)
                group(5, 4, lambda a: yc[:, a * P:(a + 1) * P], yc_done, t + 1)

            tile(0)
            with pe.Fori(0, LAT) as i:
                tile(i + 1)

        @block.scalar
        def _(act):
            act.wait_ge(ws_t, 1)
            nc.scalar.copy(wst[:].rearrange("p g q -> p (g q)"), ps_m[:]).then_inc(ws_done, 1)

            def tile(t):
                act.wait_ge(x_in, 16 * t + 16)
                if not is_first(t):
                    act.wait_ge(x_t, 2 * t)
                nc.scalar.activation(h[:], x[:], ACT.Square, accum_out=ss[:, 0:1]).then_inc(ss_done, 1)
                for b in range(2):
                    act.wait_ge(x_t, 2 * t + b + 1)
                    if not is_first(t) and b == 0:
                        act.wait_ge(z_done, NZ * t)
                        act.wait_ge(st_h, 16 * t)
                    nc.scalar.copy(ht[:].rearrange("p k n -> p (k n)")[:, b * 512:(b + 1) * 512], ps_x[:, b, :]).then_inc(ht_done, 1)
                act.wait_ge(z_done, t * NZ + 3)
                if not is_first(t):
                    act.wait_ge(vr_done, t)
                nc.scalar.copy(sv[:], ps_z[2][:]).then_inc(z_act, 1)
                if not is_first(t):
                    act.wait_ge(gm_done, t)
                act.wait_ge(z_act, t * per["a"] + 1)
                nc.scalar.activation(vr[:], sv[:], ACT.Square, accum_out=ss[:, 3:4]).then_inc(ssv_done, 1)
                act.wait_ge(z_done, t * NZ + 4)
                if not is_first(t):
                    act.wait_ge(yc_done, t)
                nc.scalar.copy(u[:], ps_z[0][:]).then_inc(z_act, 1)
                act.wait_ge(z_done, t * NZ + 6)
                if not is_first(t):
                    act.wait_ge(st_kv, 16 * t)
                nc.scalar.mul(qkv[:, MIX:2 * MIX], ps_z[2][:], MD ** -0.5).then_inc(z_act, 1)
                act.wait_ge(z_done, t * NZ + 8)
                if not is_first(t):
                    act.wait_ge(st_o, 16 * t)
                nc.scalar.activation(og[:], ps_z[1][:], ACT.Sigmoid).then_inc(z_act, 1)
                outs = [(qat[:, 0:512], ps_t[0][0:AD, :], st_qa), (qat[:, 512:1024], ps_t[1][0:AD, :], None),
                        (kat[:, :, bass.ds(t * P, P)], ps_t[0][0:AD, 0:256].rearrange("p (k n) -> p k n", k=2), None),
                        (qkt[:, 0:512], ps_t[1][:], st_qk), (qkt[:, 512:1024], ps_t[0][:], None),
                        (yct[:], ps_t[1][:], st_yc)]
                for g, (dst, src, stored) in enumerate(outs):
                    act.wait_ge(t_done, t * NT + g + 1)
                    if stored is not None and not is_first(t):
                        act.wait_ge(stored, 16 * t)
                    nc.scalar.copy(dst, src).then_inc(t_out, 1)

            tile(0)
            with act.Fori(0, LAT) as i:
                tile(i + 1)

        @block.vector
        def _(dve):
            s = Steps(dve, step)
            dve.wait_ge(rows_in, 48)
            s.link(nc.vector.scalar_tensor_tensor(out=scale1[:], in0=scale1[:], scalar=1.0, in1=gain1[:], op0=ALU.add, op1=ALU.mult))

            def tile(t):
                dve.wait_ge(ss_done, t + 1)
                nc.vector.tensor_scalar(ss[:, 1:2], ss[:, 0:1], 1.0 / D, EPS, ALU.mult, ALU.add).then_inc(ms_done, 1)
                dve.wait_ge(rstd_done, t + 1)
                s.link(nc.vector.scalar_tensor_tensor(out=h[:], in0=x[:], scalar=ss[:, 2:3], in1=scale1[:], op0=ALU.mult, op1=ALU.mult))
                nc.vector.tensor_tensor(h[:], h[:], shift1[:], ALU.add).then_inc(h_done, 1)
                dve.wait_ge(z_done, t * NZ + 1)
                nc.vector.tensor_copy(qka[:, 0:512], ps_z[0][:]).then_inc(z_dve, 1)
                dve.wait_ge(z_done, t * NZ + 2)
                nc.vector.tensor_copy(cols(va[:].rearrange("p t n -> p (t n)"), t * P, P), ps_z[1][:, P:2 * P])
                if not is_first(t):
                    dve.wait_ge(st_new, 32)
                nc.vector.tensor_copy(qka[:, 512:768], ps_z[1][:, 0:256]).then_inc(z_dve, 1)
                dve.wait_ge(z_dve, t * per["d"] + 2)
                heads = qka[:, 0:640].rearrange("p (h d) -> p h d", h=10)
                if is_first(t):
                    nc.vector.tensor_copy(qr[:], heads).then_inc(qr_done, 1)
                else:
                    dve.wait_ge(rope_in, 16 * t)
                    nc.vector.tensor_tensor(rot_c[:], heads, rope[:, 0:AD].unsqueeze(1).to_broadcast([P, 10, AD]), ALU.mult)
                    split = qka[:, 0:640].rearrange("p (h a b c) -> p h a b c", h=10, a=2, b=2)
                    sine = rope[:, AD:].rearrange("p (a b c) -> p a b c", a=2, b=2)
                    for b in range(2):
                        for a in range(2):
                            last = nc.vector.tensor_tensor(rot_s[:, :, a, b, :], split[:, :, a, 1 - b, :],
                                                           sine[:, a, b, :].unsqueeze(1).to_broadcast([P, 10, 16]), ALU.mult)
                    s.link(last)
                    nc.vector.tensor_tensor(qr[:], rot_c[:], rot_s[:].rearrange("p h a b c -> p h (a b c)"), ALU.add).then_inc(qr_done, 1)
                dve.wait_ge(ssv_done, t + 1)
                nc.vector.tensor_scalar(ss[:, 4:5], ss[:, 3:4], 1.0 / MIX, EPS, ALU.mult, ALU.add).then_inc(msv_done, 1)
                dve.wait_ge(z_done, t * NZ + 5)
                nc.vector.tensor_copy(qkv[:, 0:MIX], ps_z[1][:]).then_inc(z_dve, 1)
                dve.wait_ge(rstdv_done, t + 1)
                nc.vector.tensor_scalar(vr[:], sv[:], ss[:, 5:6], None, ALU.mult).then_inc(vr_done, 1)
                dve.wait_ge(z_done, t * NZ + 7)
                if not is_first(t):
                    dve.wait_ge(st_kv, 16 * t)
                nc.vector.tensor_copy(qkv[:, 2 * MIX:], ps_z[0][:]).then_inc(z_dve, 1)
                dve.wait_ge(z_done, t * NZ + 9)
                nc.vector.tensor_tensor(cols(gates[:].rearrange("p t g -> p (t g)"), t * 16, 16), ps_z[2][:, 0:16], gb[:], ALU.add).then_inc(z_dve, 1)
                dve.wait_ge(gm_done, t + 1)
                dve.wait_ge(z_act, t * per["a"] + 2)
                for g in range(4):
                    last = nc.vector.scalar_tensor_tensor(out=yc[:, g * P:(g + 1) * P], in0=ps_m[:, g * P:(g + 1) * P],
                                                          scalar=bs[:, g:g + 1], in1=u[:, g * P:(g + 1) * P], op0=ALU.add, op1=ALU.mult)
                last.then_inc(yc_done, 1)

            dve.wait_ge(small_in, 64)
            tile(0)
            dve.wait_ge(rows2_in, 32)
            s.link(nc.vector.scalar_tensor_tensor(out=scale1[:], in0=scale1[:], scalar=1.0, in1=gain1[:], op0=ALU.add, op1=ALU.mult))
            with dve.Fori(0, LAT) as i:
                s.enter(i, 2)
                tile(i + 1)
            s.leave(LAT)


def mlstm(nc, T, keep):
    W = MD + 1
    NCOL = TILES + 2
    PREV0 = (0, TILES)
    END0 = TILES + 1
    with nc.cleanup_on_exit(), ExitStack() as ctx:
        sb = lambda n, s, d=F32: ctx.enter_context(nc.sbuf_tensor(n, s, d))
        sem = nc.alloc_semaphore
        ident, gates, hd = keep.ident, keep.gates, keep.hd
        log_f = sb("ml_log_f", [P, TILES, 16])
        tmp = sb("ml_tmp", [P, TILES, 16])
        causal = sb("ml_causal", [P, 2, P])
        restart = sb("ml_restart", [MH, 2, TILES * P])
        head_row = sb("ml_head_row", [MH, MH, P])
        li = sb("ml_li", [MH, 2, TILES * P])
        lf = sb("ml_lf", [MH, 2, TILES * P])
        b = sb("ml_b", [MH, 2, TILES * P])
        g = sb("ml_g", [MH, 2, TILES * P])
        mx = sb("ml_mx", [MH, 2, TILES * P])
        m = sb("ml_m", [MH, 2, TILES * P])
        prev = sb("ml_prev", [MH, 2, NCOL])
        end = sb("ml_end", [MH, 2, TILES])
        col = sb("ml_col", [P, 3, 2, TILES, MH])
        prevb = sb("ml_prevb", [P, 2, MH, NCOL])
        endb = sb("ml_endb", [P, 2, MH, TILES])
        w0 = sb("ml_w0", [P, 2, TILES, MH])
        em = sb("ml_em", [P, 2, TILES, MH])
        we0 = sb("ml_we0", [P, 2, TILES, MH])
        qkt = [sb(f"ml_qkt{d}", [P, 2 * MIX]) for d in range(2)]
        kk = [sb(f"ml_k{d}", [P, MIX]) for d in range(2)]
        v1 = [sb(f"ml_v{d}", [P, MH, W]) for d in range(2)]
        cn = [sb(f"ml_cn{d}", [P, MH, W]) for d in range(2)]
        arg = sb("ml_arg", [P, MIX])
        wt = sb("ml_wt", [P, MH, P])
        pw = sb("ml_pw", [P, MIX])
        vw = sb("ml_vw", [P, MH, W])
        ic = sb("ml_ic", [P, MH, W])
        tot = sb("ml_tot", [P, MH, W])
        den = sb("ml_den", [P, MH])
        cs = sb("ml_cs", [P, 2 * MH, P])
        ps = [ctx.enter_context(nc.psum_tensor(f"ml_ps{i}", [P, 512], F32)) for i in range(2)]
        ps_i, ps_l, ps_u = (ctx.enter_context(nc.psum_tensor(f"ml_ps_{n}", [P, 2, 512], F32)) for n in "ilu")
        banks = [ps_i[:, 0, :], ps_i[:, 1, :], ps_l[:, 0, :], ps_l[:, 1, :], ps_u[:, 0, :], ps_u[:, 1, :]]

        small_in, m0_in = sem("ml_small_in"), sem("ml_m0_in")
        cell_in = [sem(f"ml_cell_in{d}") for d in range(2)]
        c0_in, n0_in, c_stored = sem("ml_c0_in"), sem("ml_n0_in"), sem("ml_c_stored")
        abs_done, exp_done, ln_done, f_done = sem("ml_abs"), sem("ml_exp"), sem("ml_ln"), sem("ml_f_done")
        rows_t, rows_out, ones_set, zero_set = sem("ml_rows_t"), sem("ml_rows_out"), sem("ml_ones"), sem("ml_zero")
        scan_done, col_t, col_out, diff_done, w_cols = (sem(f"ml_{n}") for n in ("scan", "col_t", "col_out", "diff", "w_cols"))
        mb_done, arg_done, wt_done, st_done, p_done = (sem(f"ml_{n}") for n in ("mb", "arg", "wt", "st", "p"))
        inter_done, ic_done, local_done, tot_done = (sem(f"ml_{n}") for n in ("inter", "ic", "local", "tot"))
        vw_done, upd_done, cn_done = (sem(f"ml_{n}") for n in ("vw", "upd", "cn"))
        cs_t, cs_out, c0_t, c0_out = (sem(f"ml_{n}") for n in ("cs_t", "cs_out", "c0_t", "c0_out"))
        step = sem("ml_dve_step")
        block = ctx.enter_context(nc.Block())

        def order(eng, cell, between=None):
            for d in range(2):
                cell(d, 0, d, 0)
            if between is not None:
                between()
            with eng.Fori(0, LAT) as i:
                tiles = (i + 1, LAT - i)
                eng.to_reg(tiles[1])
                for d in range(2):
                    cell(2 * i + (2 + d), i + 1, d, tiles[d])

        @block.sync
        def _(sp):
            sp.dma_start(causal[:], T["const_causal"].rearrange("d s t -> s d t")).then_inc(small_in, 16)
            sp.dma_start(restart[:].rearrange("h d n -> h (d n)"), T["const_restart"]).then_inc(small_in, 16)
            sp.dma_start(head_row[:].rearrange("h r n -> h (r n)"), T["const_head_row"]).then_inc(small_in, 16)
            sp.wait_ge(zero_set, 3)
            for d, c in ((0, 1), (1, LAT)):
                sp.dma_start(prev[:, d, c:c + 1], T["state_m"][0, 0, d].rearrange("(h a) -> h a", a=1)).then_inc(m0_in, 16)
            sp.wait_ge(ones_set, 2)

            def cell(s, n, d, t):
                if not isinstance(s, int):
                    sp.wait_ge(upd_done, s - 1)
                sp.dma_start(qkt[d][:], row(T["qkt"], t)).then_inc(cell_in[d], 16)
                sp.dma_start(kk[d][:], row(T["kv"], t)[:, 0:MIX]).then_inc(cell_in[d], 16)
                sp.dma_start(v1[d][:, :, 0:MD], row(T["kv"], t)[:, MIX:].rearrange("p (h n) -> p h n", h=MH)).then_inc(cell_in[d], 16)

            def states():
                sp.wait_ge(cn_done, 2)
                for d in range(2):
                    sp.dma_start(T["new_n"][0, 0, d].rearrange("h e -> e h"), cn[d][:, :, MD:W].rearrange("p h a -> p (h a)"),
                                 allow_slow_non_contiguous=True).then_inc(c_stored, 16)
                    sp.dma_start(T["new_m"][0, 0, d].rearrange("(h a) -> h a", a=1), prev[:, d, END0:END0 + 1]).then_inc(c_stored, 16)
                sp.wait_ge(cs_out, 2)
                sp.dma_start(T["new_C"][0, 0].rearrange("d h r e -> r (d h) e"), cs[:]).then_inc(c_stored, 16)
                sp.wait_ge(c_stored, 80)
                sp.dma_start(cs[:], T["state_C"][0, 0].rearrange("d h r e -> r (d h) e")).then_inc(c0_in, 16)
                for d in range(2):
                    sp.dma_start(cn[d][:, :, MD:W].rearrange("p h a -> p (h a)"), T["state_n"][0, 0, d].rearrange("h e -> e h"),
                                 allow_slow_non_contiguous=True).then_inc(n0_in, 16)

            order(sp, cell, states)

        @block.gpsimd
        def _(pool):
            nc.gpsimd.memset(prev[:], 0.0).then_inc(zero_set, 1)
            for d in range(2):
                nc.gpsimd.memset(cn[d][:], 0.0).then_inc(zero_set, 1)
            for d in range(2):
                nc.gpsimd.memset(v1[d][:, :, MD:W], 1.0).then_inc(ones_set, 1)

        @block.tensor
        def _(pe):
            pe.wait_ge(f_done, 1)
            k = 0
            for kind in range(2):
                for d in range(2):
                    src = gates if kind == 0 else log_f
                    if k >= 2:
                        pe.wait_ge(rows_out, k - 1)
                    for t in range(TILES):
                        c = 8 * d + 4 * kind
                        mm = nc.tensor.matmul(banks[3 * (k % 2) + t // 3][0:MH, (t % 3) * P:(t % 3 + 1) * P],
                                              src[:, t, c:c + MH], ident[:], start=True, stop=True)
                    mm.then_inc(rows_t, 1)
                    k += 1
            pe.wait_ge(scan_done, 1)
            for j, src in enumerate((g, mx, m)):
                for d in range(2):
                    for t in range(TILES):
                        c = ((j * 2 + d) * TILES + t) * MH
                        nc.tensor.matmul(ps[0][:, c:c + MH], src[:, d, t * P:(t + 1) * P], ident[0:MH, 0:MH], start=True, stop=True)
            pe.wait_ge(small_in, 48)
            for d in range(2):
                for h in range(MH):
                    c = (d * MH + h) * NCOL
                    nc.tensor.matmul(ps[1][:, c:c + NCOL], head_row[:, h, :], prev[:, d, :], start=True, stop=True)
                    c = 2 * MH * NCOL + (d * MH + h) * TILES
                    mm = nc.tensor.matmul(ps[1][:, c:c + TILES], head_row[:, h, :], end[:, d, :], start=True, stop=True)
            mm.then_inc(col_t, 1)
            pe.wait_ge(col_out, 3)

            def cell(s, n, d, t):
                first = isinstance(s, int) and s == 0
                if not first:
                    pe.wait_ge(arg_done, s)
                row = mx[:, d, :]
                for h in range(MH):
                    mm = nc.tensor.matmul(ps[0][:, h * P:(h + 1) * P], head_row[:, h, :], cols(row, t * P, P), start=True, stop=True)
                mm.then_inc(mb_done, 1)
                pe.wait_ge(cell_in[d], 48 * n + 48)
                if not first:
                    pe.wait_ge(p_done, s)
                for h in range(MH):
                    mm = nc.tensor.matmul(ps[1][:, h * P:(h + 1) * P], qkt[d][:, MIX + h * P:MIX + (h + 1) * P],
                                          qkt[d][:, h * P:(h + 1) * P], start=True, stop=True)
                mm.then_inc(st_done, 1)
                if isinstance(s, int):
                    pe.wait_ge(zero_set, 3)
                else:
                    pe.wait_ge(cn_done, s - 1)
                    pe.wait_ge(c0_out, 4)
                    pe.wait_ge(n0_in, 32)
                if not first:
                    pe.wait_ge(ic_done, s)
                for h in range(MH):
                    mm = nc.tensor.matmul(ps_i[:, h // 2, (h % 2) * W:(h % 2 + 1) * W], qkt[d][:, h * P:(h + 1) * P],
                                          cn[d][:, h, :], start=True, stop=True)
                mm.then_inc(inter_done, 1)
                pe.wait_ge(p_done, s + 1)
                if not first:
                    pe.wait_ge(tot_done, s)
                for h in range(MH):
                    mm = nc.tensor.matmul(ps_l[:, h // 2, (h % 2) * W:(h % 2 + 1) * W], pw[:, h * P:(h + 1) * P],
                                          v1[d][:, h, :], start=True, stop=True)
                mm.then_inc(local_done, 1)
                pe.wait_ge(vw_done, s + 1)
                if not first:
                    pe.wait_ge(cn_done, s)
                for h in range(MH):
                    mm = nc.tensor.matmul(ps_u[:, h // 2, (h % 2) * W:(h % 2 + 1) * W], kk[d][:, h * P:(h + 1) * P],
                                          vw[:, h, :], start=True, stop=True)
                mm.then_inc(upd_done, 1)

            def states():
                for d in range(2):
                    pe.wait_ge(cn_done, 2)
                    for h in range(MH):
                        tr = nc.tensor.transpose(banks[d][:, h * P:(h + 1) * P], cn[d][:, h, 0:MD], ident[:])
                    tr.then_inc(cs_t, 1)
                pe.wait_ge(c0_in, 16)
                pe.wait_ge(cs_out, 2)
                for d in range(2):
                    for h in range(MH):
                        tr = nc.tensor.transpose(banks[d][:, h * P:(h + 1) * P], cs[:, d * MH + h, :], ident[:])
                    tr.then_inc(c0_t, 1)
                pe.wait_ge(c0_out, 4)

            order(pe, cell, states)

        @block.scalar
        def _(act):
            act.wait_ge(abs_done, 1)
            nc.scalar.activation(tmp[:], log_f[:], ACT.Exp, scale=-1.0).then_inc(exp_done, 1)
            act.wait_ge(exp_done, 1)
            nc.scalar.activation(tmp[:], tmp[:], ACT.Ln, bias=1.0).then_inc(ln_done, 1)
            act.wait_ge(col_out, 3)
            act.wait_ge(diff_done, 1)
            for x in (w0, we0):
                nc.scalar.activation(x[:], x[:], ACT.Exp).then_inc(w_cols, 1)
            nc.scalar.activation(em[:], col[:, 2], ACT.Exp, scale=-1.0).then_inc(w_cols, 1)

            def cell(s, n, d, t):
                first = isinstance(s, int) and s == 0
                act.wait_ge(arg_done, s + 1)
                if not first:
                    act.wait_ge(vw_done, s)
                for h in range(MH):
                    bias = cols(col[:, 0, d].rearrange("p t h -> p (t h)"), t * MH + h, 1)
                    a = nc.scalar.activation(wt[:, h, :], arg[:, h * P:(h + 1) * P], ACT.Exp, bias=bias)
                a.then_inc(wt_done, 1)
                act.wait_ge(inter_done, s + 1)
                act.wait_ge(w_cols, 3)
                if not first:
                    act.wait_ge(tot_done, s)
                for h in range(MH):
                    scale = cols(w0[:, d].rearrange("p t h -> p (t h)"), t * MH + h, 1)
                    a = nc.scalar.activation(ic[:, h, :], ps_i[:, h // 2, (h % 2) * W:(h % 2 + 1) * W], ACT.Copy, scale=scale)
                a.then_inc(ic_done, 1)

            def states():
                for d in range(2):
                    act.wait_ge(cs_t, d + 1)
                    nc.scalar.copy(cs[:, d * MH:(d + 1) * MH, :].rearrange("p h n -> p (h n)"), banks[d]).then_inc(cs_out, 1)

            order(act, cell, states)

        @block.vector
        def _(dve):
            s_ = Steps(dve, step)
            nc.vector.scalar_tensor_tensor(out=log_f[:], in0=gates[:], scalar=-1.0, in1=gates[:], op0=ALU.mult, op1=ALU.max).then_inc(abs_done, 1)
            dve.wait_ge(ln_done, 1)
            s_.link(nc.vector.tensor_scalar(log_f[:], gates[:], 0.0, None, ALU.min))
            nc.vector.tensor_tensor(log_f[:], log_f[:], tmp[:], ALU.subtract).then_inc(f_done, 1)
            k = 0
            for kind in range(2):
                for d in range(2):
                    dve.wait_ge(rows_t, k + 1)
                    for j in range(3):
                        dst = (li if kind == 0 else lf)[:, d, j * 3 * P:(j + 1) * 3 * P]
                        c = nc.vector.tensor_copy(dst, banks[3 * (k % 2) + j][0:MH, 0:3 * P])
                    c.then_inc(rows_out, 1)
                    k += 1
            dve.wait_ge(rows_out, 4)
            dve.wait_ge(small_in, 48)
            flip = lambda ap: ap[:, ::-1]
            for d in range(2):
                way = (lambda ap: ap) if d == 0 else flip
                last = nc.vector.tensor_tensor_scan(way(b[:, d, :]), way(restart[:, d, :]), way(lf[:, d, :]), 0.0, ALU.mult, ALU.add)
            s_.link(last)
            s_.link(nc.vector.tensor_tensor(g[:], li[:], b[:], ALU.subtract))
            dve.wait_ge(zero_set, 1)
            dve.wait_ge(m0_in, 32)

            def scan(tiles, c_prev, c_next):
                for d in range(2):
                    way = (lambda ap: ap) if d == 0 else flip
                    row = cols(g[:, d, :], tiles[d] * P, P)
                    last = nc.vector.tensor_tensor_scan(way(cols(mx[:, d, :], tiles[d] * P, P)), way(row), way(row),
                                                        cols(prev[:, d, :], c_prev[d], 1), ALU.max, ALU.max)
                s_.link(last)
                for d in range(2):
                    e = tiles[d] * P + (P - 1 if d == 0 else 0)
                    last = nc.vector.tensor_tensor(cols(prev[:, d, :], c_next[d], 1), cols(mx[:, d, :], e, 1), cols(b[:, d, :], e, 1), ALU.add)
                s_.link(last)

            scan((0, 0), PREV0, (END0, END0))
            for i in range(LAT):
                scan((i + 1, LAT - i), (i + 1, LAT - i), (i + 2, LAT - i - 1))
            nc.vector.tensor_tensor(m[:], mx[:], b[:], ALU.add)
            for d in range(2):
                e = P - 1 if d == 0 else 0
                last = nc.vector.tensor_copy(end[:, d, :], mx[:, d, :].rearrange("h (t n) -> h t n", t=TILES)[:, :, e])
            s_.link(last)
            nc.vector.memset(prev[:, 1, 0:1], 0.0).then_inc(scan_done, 1)
            dve.wait_ge(col_t, 1)
            nc.vector.tensor_copy(col[:].rearrange("p k d t h -> p (k d t h)"), ps[0][:, 0:3 * 2 * TILES * MH]).then_inc(col_out, 1)
            nc.vector.tensor_copy(prevb[:].rearrange("p d h t -> p (d h t)"), ps[1][:, 0:2 * MH * NCOL]).then_inc(col_out, 1)
            nc.vector.tensor_copy(endb[:].rearrange("p d h t -> p (d h t)"), ps[1][:, 2 * MH * NCOL:2 * MH * (NCOL + TILES)]).then_inc(col_out, 1)
            dve.wait_ge(col_out, 3)
            for d in range(2):
                before = prevb[:, d, :, 0:TILES].rearrange("p h t -> p t h")
                nc.vector.tensor_tensor(w0[:, d], before, col[:, 1, d], ALU.subtract)
                last = nc.vector.tensor_tensor(we0[:, d], before, endb[:, d].rearrange("p h t -> p t h"), ALU.subtract)
            last.then_inc(diff_done, 1)
            dve.wait_ge(w_cols, 3)

            def cell(s, n, d, t):
                first = isinstance(s, int) and s == 0
                dve.wait_ge(mb_done, s + 1)
                if not first:
                    dve.wait_ge(wt_done, s)
                nc.vector.scalar_tensor_tensor(out=arg[:].rearrange("p (h n) -> p h n", h=MH), in0=ps[0][:].rearrange("p (h n) -> p h n", h=MH),
                                               scalar=-1.0, in1=causal[:, d, :].unsqueeze(1).to_broadcast([P, MH, P]),
                                               op0=ALU.mult, op1=ALU.add).then_inc(arg_done, 1)
                dve.wait_ge(wt_done, s + 1)
                dve.wait_ge(st_done, s + 1)
                if not first:
                    dve.wait_ge(local_done, s)
                nc.vector.tensor_tensor(pw[:], ps[1][:], wt[:].rearrange("p h n -> p (h n)"), ALU.mult).then_inc(p_done, 1)
                dve.wait_ge(cell_in[d], 48 * n + 48)
                if not first:
                    dve.wait_ge(upd_done, s)
                e = P - 1 if d == 0 else 0
                nc.vector.tensor_tensor(vw[:], v1[d][:], wt[:, :, e:e + 1].to_broadcast([P, MH, W]), ALU.mult).then_inc(vw_done, 1)
                dve.wait_ge(ic_done, s + 1)
                dve.wait_ge(local_done, s + 1)
                for a in range(2):
                    last = nc.vector.tensor_tensor(tot[:, 2 * a:2 * a + 2, :].rearrange("p h n -> p (h n)"),
                                                   ic[:, 2 * a:2 * a + 2, :].rearrange("p h n -> p (h n)"), ps_l[:, a, 0:2 * W], ALU.add)
                last.then_inc(tot_done, 1)
                dve.wait_ge(tot_done, s + 1)
                raw = tot[:, :, MD:W].rearrange("p h a -> p (h a)")
                s_.link(nc.vector.scalar_tensor_tensor(out=den[:], in0=raw, scalar=-1.0, in1=raw, op0=ALU.mult, op1=ALU.max))
                s_.link(nc.vector.tensor_tensor(den[:], den[:], cols(em[:, d].rearrange("p t h -> p (t h)"), t * MH, MH), ALU.max))
                s_.link(nc.vector.reciprocal(den[:], den[:]))
                nc.vector.tensor_tensor(cols(hd[:, d], t * MIX, MIX).rearrange("p (h n) -> p h n", h=MH), tot[:, :, 0:MD],
                                        den[:].unsqueeze(2).to_broadcast([P, MH, MD]), ALU.mult)
                dve.wait_ge(upd_done, s + 1)
                for h in range(MH):
                    carry = cols(we0[:, d].rearrange("p t h -> p (t h)"), t * MH + h, 1)
                    last = nc.vector.scalar_tensor_tensor(out=cn[d][:, h, :], in0=cn[d][:, h, :], scalar=carry,
                                                          in1=ps_u[:, h // 2, (h % 2) * W:(h % 2 + 1) * W], op0=ALU.mult, op1=ALU.add)
                last.then_inc(cn_done, 1)

            for d in range(2):
                cell(d, 0, d, 0)
            dve.wait_ge(n0_in, 32)
            for d in range(2):
                dve.wait_ge(c0_t, d + 1)
                for a in range(2):
                    nc.vector.tensor_copy(cn[d][:, 2 * a:2 * a + 2, 0:MD], banks[d][:, a * 256:(a + 1) * 256].rearrange(
                        "p (h n) -> p h n", h=2)).then_inc(c0_out, 1)
            dve.wait_ge(c0_out, 4)
            with dve.Fori(0, LAT) as i:
                s_.enter(i, 6)
                tiles = (i + 1, LAT - i)
                dve.to_reg(tiles[1])
                for d in range(2):
                    cell(2 * i + (2 + d), i + 1, d, tiles[d])
            s_.leave(LAT)


def attend(nc, T, keep):
    with nc.cleanup_on_exit(), ExitStack() as ctx:
        sb = lambda n, s, d=F32: ctx.enter_context(nc.sbuf_tensor(n, s, d))
        sem = nc.alloc_semaphore
        bank = lambda n: ctx.enter_context(nc.psum_tensor(n, [P, 512], F32))
        ident, kat, va, hd = keep.ident, keep.kat, keep.va, keep.hd
        ck = sb("at_ck", [P, AKV * AD])
        ckt = sb("at_ckt", [AD, AKV, P])
        cv = sb("at_cv", [P, AKV * AD])
        sink = sb("at_sink", [P, AH])
        gm = sb("at_gm", [P, MIX])
        half = sb("at_half", [P, MH])
        qat = [sb(f"at_qat{u}", [AD, AH * P]) for u in range(2)]
        win = [sb(f"at_win{u}", [P, 4 * P]) for u in range(2)]
        og = [sb(f"at_og{u}", [P, MIX]) for u in range(2)]
        sm = [sb(f"at_sm{u}", [P, 512]) for u in range(2)]
        pr = [sb(f"at_pr{u}", [P, 512]) for u in range(2)]
        pt = [sb(f"at_pt{u}", [P, 512]) for u in range(2)]
        top = sb("at_top", [P, AH])
        ntop = sb("at_ntop", [P, AH])
        total = sb("at_total", [P, AH])
        es = sb("at_es", [P, AH])
        rec = sb("at_rec", [P, AH])
        ya = sb("at_ya", [P, MIX])
        hs = sb("at_hs", [P, MIX])
        sq = sb("at_sq", [P, MIX])
        ms = sb("at_ms", [P, MH])
        rstd = sb("at_rstd", [P, MH])
        ym = sb("at_ym", [P, MIX])
        yt = sb("at_yt", [P, 2 * MIX])
        ps_s = [bank(f"at_ps_s{b}") for b in range(3)]
        ps_t = [bank(f"at_ps_t{b}") for b in range(2)]
        ps_o = bank("at_ps_o")
        ps_y = [bank(f"at_ps_y{b}") for b in range(2)]

        small_in, ckt_t, ckt_out, half_set = (sem(f"at_{n}") for n in ("small_in", "ckt_t", "ckt_out", "half_set"))
        tile_in = [sem(f"at_tile_in{u}") for u in range(2)]
        s_done, top_done, pr_done, pt_t, pt_done, o_done = (sem(f"at_{n}") for n in ("s", "top", "pr", "pt_t", "pt", "o"))
        diff_done, es_done, ya_done, ym_done = (sem(f"at_{n}") for n in ("diff", "es", "ya", "ym"))
        ms_done, rstd_done, y_t, y_out, stored = (sem(f"at_{n}") for n in ("ms", "rstd", "y_t", "y_out", "stored"))
        step = sem("at_dve_step")
        block = ctx.enter_context(nc.Block())
        SCALE = AD ** -0.5

        def order(eng, tile):
            tile(0, 1, 0)
            with eng.Fori(0, LAT // 2) as i:
                for u in range(2):
                    tile(2 * i + (1 + u), u, i + u)

        @block.sync
        def _(sp):
            sp.dma_start(ck[:], T["cache_k"][0, 0].rearrange("s k d -> s (k d)")).then_inc(small_in, 16)
            sp.dma_start(cv[:], T["cache_v"][0, 0].rearrange("s k d -> s (k d)")).then_inc(small_in, 16)
            sp.dma_start(sink[:], T["sink"].to_broadcast([P, AH])).then_inc(small_in, 16)
            sp.dma_start(gm[:], T["g_mlstm"].rearrange("a h n -> a (h n)").to_broadcast([P, MIX])).then_inc(small_in, 16)

            def load(t, u, n):
                if not isinstance(t, int) or t >= 2:
                    sp.wait_ge(ya_done, t - 1)
                    sp.wait_ge(ym_done, t - 1)
                sp.dma_start(qat[u][:], row(T["qat"], t)).then_inc(tile_in[u], 16)
                sp.dma_start(og[u][:], row(T["og"], t)).then_inc(tile_in[u], 16)
                if is_first(t):
                    sp.dma_start(win[u][:, 0:P], row(T["const_window"], 3)[:, 2 * P:3 * P]).then_inc(tile_in[u], 16)
                else:
                    sp.dma_start(win[u][:], row(T["const_window"], t - 1)).then_inc(tile_in[u], 16)

            def store(t):
                sp.wait_ge(y_out, 2 * t + 2)
                sp.dma_start(row(T["yt"], t), yt[:]).then_inc(stored, 16)

            load(0, 1, 0)
            load(1, 0, 0)
            store(0)
            load(2, 1, 1)
            store(1)
            with sp.Fori(0, LAT // 2 - 1) as i:
                for u in range(2):
                    load(2 * i + (3 + u), u, i + 1 + u)
                    store(2 * i + (2 + u))
            store(LAT)
            sp.wait_ge(stored, 16 * TILES)

        @block.gpsimd
        def _(pool):
            nc.gpsimd.memset(half[:], -0.5).then_inc(half_set, 1)
            pool.wait_ge(half_set, 1)

            def tile(t, u, n):
                pool.wait_ge(ms_done, t + 1)
                nc.gpsimd.tensor_tensor(rstd[:], ms[:], half[:], ALU.pow).then_inc(rstd_done, 1)

            order(pool, tile)

        @block.tensor
        def _(pe):
            pe.wait_ge(small_in, 64)
            for k in range(AKV):
                tr = nc.tensor.transpose(ps_t[0][0:AD, k * P:(k + 1) * P], ck[:, k * AD:(k + 1) * AD], ident[:])
            tr.then_inc(ckt_t, 1)
            pe.wait_ge(ckt_out, 1)

            def tile(t, u, n):
                nb = 1 if is_first(t) else 4

                def scores(h):
                    if not is_first(t) or h >= 3:
                        pe.wait_ge(top_done, AH * t + h - 2)
                    q, kv = qat[u][:, h * P:(h + 1) * P], h // (AH // AKV)
                    if is_first(t):
                        mm = nc.tensor.matmul(ps_s[h % 3][:, 0:P], q, kat[:, kv, 0:P], start=True, stop=True)
                    else:
                        nc.tensor.matmul(ps_s[h % 3][:, 0:P], q, ckt[:, kv, :], start=True, stop=True)
                        mm = nc.tensor.matmul(ps_s[h % 3][:, P:4 * P], q, cols(kat[:, kv, :], (t - 1) * P, 3 * P), start=True, stop=True)
                    mm.then_inc(s_done, 1)

                def turn(h):
                    pe.wait_ge(pr_done, AH * t + h + 1)
                    if not is_first(t) or h >= 2:
                        pe.wait_ge(pt_done, AH * t + h - 1)
                    for b in range(nb):
                        tr = nc.tensor.transpose(ps_t[h % 2][:, b * P:(b + 1) * P], pr[h % 2][:, b * P:(b + 1) * P], ident[:])
                    tr.then_inc(pt_t, 1)

                def values(h):
                    pe.wait_ge(pt_done, AH * t + h + 1)
                    if h == 0 and not is_first(t):
                        pe.wait_ge(ya_done, t)
                    kv = h // (AH // AKV)
                    for b in range(nb):
                        if is_first(t):
                            v = va[:, 0, kv * AD:(kv + 1) * AD]
                        elif b == 0:
                            v = cv[:, kv * AD:(kv + 1) * AD]
                        else:
                            v = cols(va[:].rearrange("p t n -> p (t n)"), (t + (b - 2)) * P + kv * AD, AD)
                        mm = nc.tensor.matmul(ps_o[:, h * AD:(h + 1) * AD], pt[h % 2][:, b * P:(b + 1) * P], v, start=(b == 0), stop=(b == nb - 1))
                    mm.then_inc(o_done, 1)

                pe.wait_ge(tile_in[u], 48 * n + 48)
                scores(0)
                scores(1)
                for h in range(AH):
                    if h + 2 < AH:
                        scores(h + 2)
                    turn(h)
                    if h >= 1:
                        values(h - 1)
                values(AH - 1)
                for k, (y, ready) in enumerate(((ym, ym_done), (ya, ya_done))):
                    pe.wait_ge(ready, t + 1)
                    if not is_first(t):
                        pe.wait_ge(y_out, 2 * t - 1 + k)
                    for a in range(4):
                        tr = nc.tensor.transpose(ps_y[k][:, a * P:(a + 1) * P], y[:, a * P:(a + 1) * P], ident[:])
                    tr.then_inc(y_t, 1)

            order(pe, tile)

        @block.scalar
        def _(act):
            act.wait_ge(ckt_t, 1)
            nc.scalar.copy(ckt[:].rearrange("p k n -> p (k n)"), ps_t[0][0:AD, 0:2 * P]).then_inc(ckt_out, 1)

            def tile(t, u, n):
                w = P if is_first(t) else 4 * P
                for h in range(AH):
                    act.wait_ge(top_done, AH * t + h + 1)
                    if not is_first(t) or h >= 2:
                        act.wait_ge(pt_t, AH * t + h - 1)
                    nc.scalar.activation(pr[h % 2][:, 0:w], sm[h % 2][:, 0:w], ACT.Exp, bias=ntop[:, h:h + 1],
                                         accum_out=total[:, h:h + 1]).then_inc(pr_done, 1)
                    if h % 2 == 1:
                        act.wait_ge(pt_t, AH * t + h)
                        if not is_first(t) or h >= 2:
                            act.wait_ge(o_done, AH * t + h - 2)
                        nc.scalar.copy(pt[0][:, 0:w], ps_t[0][:, 0:w]).then_inc(pt_done, 1)
                        act.wait_ge(pt_t, AH * t + h + 1)
                        if not is_first(t) or h >= 2:
                            act.wait_ge(o_done, AH * t + h - 1)
                        nc.scalar.copy(pt[1][:, 0:w], ps_t[1][:, 0:w]).then_inc(pt_done, 1)
                act.wait_ge(diff_done, t + 1)
                nc.scalar.activation(es[:], es[:], ACT.Exp).then_inc(es_done, 1)
                for k in range(2):
                    act.wait_ge(y_t, 2 * t + k + 1)
                    if not is_first(t):
                        act.wait_ge(stored, 16 * t)
                    nc.scalar.copy(yt[:, k * MIX:(k + 1) * MIX], ps_y[k][:]).then_inc(y_out, 1)

            order(act, tile)

        @block.vector
        def _(dve):
            s_ = Steps(dve, step)
            dve.wait_ge(small_in, 64)

            def tile(t, u, n):
                w = P if is_first(t) else 4 * P
                dve.wait_ge(tile_in[u], 48 * n + 48)
                hf, hb = (cols(hd[:, d], t * MIX, MIX) for d in range(2))
                if not is_first(t):
                    dve.wait_ge(y_t, 2 * t)
                s_.link(nc.vector.tensor_tensor(hs[:], hf, hb, ALU.add))
                s_.link(nc.vector.tensor_tensor(sq[:], hs[:], hs[:], ALU.mult))
                s_.link(nc.vector.tensor_reduce(ms[:], sq[:].rearrange("p (h n) -> p h n", h=MH), AX_X, ALU.add))
                nc.vector.tensor_scalar(ms[:], ms[:], 1.0 / MD, EPS, ALU.mult, ALU.add).then_inc(ms_done, 1)
                nc.vector.tensor_tensor(sq[:], gm[:], og[u][:], ALU.mult)
                dve.wait_ge(rstd_done, t + 1)
                s_.link(nc.vector.tensor_tensor(hs[:].rearrange("p (h n) -> p h n", h=MH), hs[:].rearrange("p (h n) -> p h n", h=MH),
                                                rstd[:].unsqueeze(2).to_broadcast([P, MH, MD]), ALU.mult))
                nc.vector.tensor_tensor(ym[:], hs[:], sq[:], ALU.mult).then_inc(ym_done, 1)
                for h in range(AH):
                    if not is_first(t) or h >= 2:
                        dve.wait_ge(pr_done, AH * t + h - 1)
                    dve.wait_ge(s_done, AH * t + h + 1)
                    s_.link(nc.vector.tensor_tensor(sm[h % 2][:, 0:w], ps_s[h % 3][:, 0:w], win[u][:, 0:w], ALU.add))
                    s_.link(nc.vector.tensor_reduce(top[:, h:h + 1], sm[h % 2][:, 0:w], AX_X, ALU.max))
                    nc.vector.tensor_scalar(sm[h % 2][:, 0:w], sm[h % 2][:, 0:w], SCALE, None, ALU.mult)
                    s_.link(nc.vector.scalar_tensor_tensor(out=top[:, h:h + 1], in0=top[:, h:h + 1], scalar=SCALE, in1=sink[:, h:h + 1],
                                                           op0=ALU.mult, op1=ALU.max))
                    nc.vector.tensor_scalar(ntop[:, h:h + 1], top[:, h:h + 1], -1.0, None, ALU.mult).then_inc(top_done, 1)
                nc.vector.tensor_tensor(es[:], sink[:], top[:], ALU.subtract).then_inc(diff_done, 1)
                dve.wait_ge(es_done, t + 1)
                s_.link(nc.vector.tensor_tensor(rec[:], es[:], total[:], ALU.add))
                s_.link(nc.vector.reciprocal(rec[:], rec[:]))
                dve.wait_ge(o_done, AH * t + AH)
                nc.vector.tensor_tensor(ya[:].rearrange("p (h n) -> p h n", h=AH), ps_o[:].rearrange("p (h n) -> p h n", h=AH),
                                        rec[:].unsqueeze(2).to_broadcast([P, AH, AD]), ALU.mult).then_inc(ya_done, 1)

            tile(0, 1, 0)
            PER = 4 + 3 * AH + 2
            with dve.Fori(0, LAT // 2) as i:
                s_.enter(i, 2 * PER)
                for u in range(2):
                    tile(2 * i + (1 + u), u, i + u)
            s_.leave(LAT // 2)


def pairs(eng, tile):
    tile(0, 1, 0)
    with eng.Fori(0, LAT // 2) as i:
        for u in range(2):
            tile(2 * i + (1 + u), u, i + u)


def merge(nc, T, keep):
    NBR = 3
    NJ = 2 * NBR
    with nc.cleanup_on_exit(), ExitStack() as ctx:
        sb = lambda n, s, d=F32: ctx.enter_context(nc.sbuf_tensor(n, s, d))
        sem = nc.alloc_semaphore
        bank = lambda n: ctx.enter_context(nc.psum_tensor(n, [P, 512], F32))
        ident = keep.ident
        wm = sb("mg_wm", [P, DC, NBR * D])
        wb = sb("mg_wb", [P, NBR, 4, D])
        bm = sb("mg_bm", [P, NBR * D])
        ht = [sb(f"mg_ht{u}", [P, DC, P]) for u in range(2)]
        yt = [sb(f"mg_yt{u}", [P, 3, 4, P]) for u in range(2)]
        gsum = [sb(f"mg_gsum{u}", [P, 512]) for u in range(2)]
        gate = [sb(f"mg_gate{u}", [P, 512]) for u in range(2)]
        merged = sb("mg_merged", [P, D])
        mt = sb("mg_mt", [P, D])
        ps_g = [bank(f"mg_ps_g{b}") for b in range(3)]
        ps_p = [bank(f"mg_ps_p{b}") for b in range(2)]
        ps_t = [bank(f"mg_ps_t{b}") for b in range(2)]
        wm_in, wb_in = [sem(f"mg_wm_in{k}") for k in range(DC)], [sem(f"mg_wb_in{n}") for n in range(NBR)]
        bm_in = sem("mg_bm_in")
        tile_in = [sem(f"mg_tile_in{u}") for u in range(2)]
        g_done, p_done, sum_done, gate_done, prod_done = (sem(f"mg_{n}") for n in ("g", "p", "sum", "gate", "prod"))
        m_t, m_out, stored = (sem(f"mg_{n}") for n in ("m_t", "m_out", "stored"))
        step = sem("mg_dve_step")
        block = ctx.enter_context(nc.Block())

        @block.sync
        def _(sp):
            def load(t, u, n):
                if not isinstance(t, int) or t >= 2:
                    sp.wait_ge(p_done, NJ * (t - 1))
                sp.dma_start(ht[u][:].rearrange("p k n -> p (k n)"), row(T["ht"], t)).then_inc(tile_in[u], 16)
                flat = yt[u][:].rearrange("p b k n -> p b (k n)")
                sp.dma_start(flat[:, 0, :], row(T["yt"], t)[:, 0:MIX]).then_inc(tile_in[u], 16)
                sp.dma_start(flat[:, 1, :], row(T["yct"], t)).then_inc(tile_in[u], 16)
                sp.dma_start(flat[:, 2, :], row(T["yt"], t)[:, MIX:]).then_inc(tile_in[u], 16)

            def store(t):
                sp.wait_ge(m_out, 2 * t + 2)
                sp.dma_start(row(T["mt"], t), mt[:]).then_inc(stored, 16)

            load(0, 1, 0)
            for k in range(DC):
                sp.dma_start(wm[:, k, :], T["w_merge"][0, k * P:(k + 1) * P, :]).then_inc(wm_in[k], 16)
            sp.dma_start(bm[:], T["b_merge"].to_broadcast([P, NBR * D])).then_inc(bm_in, 16)
            for n in range(NBR):
                sp.dma_start(wb[:, n], T["w_branch"][0, n].rearrange("(k p) d -> p k d", p=P)).then_inc(wb_in[n], 16)
            load(1, 0, 0)
            load(2, 1, 1)
            store(0)
            with sp.Fori(0, LAT // 2 - 1) as i:
                for u in range(2):
                    load(2 * i + (3 + u), u, i + 1 + u)
                    store(2 * i + (1 + u))
            store(LAT - 1)
            store(LAT)
            sp.wait_ge(stored, 16 * TILES)

        @block.tensor
        def _(pe):
            def turn(t):
                pe.wait_ge(prod_done, NJ * t + NJ)
                if not is_first(t):
                    pe.wait_ge(m_out, 2 * t)
                for k in range(DC):
                    tr = nc.tensor.transpose(ps_t[k // 4][:, (k % 4) * P:(k % 4 + 1) * P], merged[:, k * P:(k + 1) * P], ident[:])
                    if k % 4 == 3:
                        tr.then_inc(m_t, 1)

            def tile(t, u, n):
                pe.wait_ge(tile_in[u], 64 * n + 64)
                for j in range(NJ):
                    br, half = j // 2, j % 2
                    if not is_first(t) or j >= 3:
                        pe.wait_ge(sum_done, NJ * t + j - 2)
                    for k in range(DC):
                        if is_first(t) and j == 0:
                            pe.wait_ge(wm_in[k], 16)
                        mm = nc.tensor.matmul(ps_g[j % 3][:], ht[u][:, k, :], wm[:, k, j * 512:(j + 1) * 512], start=(k == 0), stop=(k == DC - 1))
                    mm.then_inc(g_done, 1)
                    if not is_first(t) or j >= 2:
                        pe.wait_ge(prod_done, NJ * t + j - 1)
                    if is_first(t) and half == 0:
                        pe.wait_ge(wb_in[br], 16)
                    for k in range(4):
                        mm = nc.tensor.matmul(ps_p[j % 2][:], yt[u][:, br, k, :], wb[:, br, k, half * 512:(half + 1) * 512], start=(k == 0), stop=(k == 3))
                    mm.then_inc(p_done, 1)
                    if j == 0 and not is_first(t):
                        turn(t - 1)

            pairs(pe, tile)
            turn(LAT)

        @block.scalar
        def _(act):
            def out(t):
                for b in range(2):
                    act.wait_ge(m_t, 2 * t + b + 1)
                    if b == 0 and not is_first(t):
                        act.wait_ge(stored, 16 * t)
                    nc.scalar.copy(mt[:, b * 512:(b + 1) * 512], ps_t[b][:]).then_inc(m_out, 1)

            def tile(t, u, n):
                for j in range(NJ):
                    act.wait_ge(sum_done, NJ * t + j + 1)
                    if not is_first(t) or j >= 2:
                        act.wait_ge(prod_done, NJ * t + j - 1)
                    nc.scalar.activation(gate[j % 2][:], gsum[j % 2][:], ACT.Sigmoid).then_inc(gate_done, 1)
                    if j == 0 and not is_first(t):
                        out(t - 1)

            pairs(act, tile)
            out(LAT)

        @block.vector
        def _(dve):
            s_ = Steps(dve, step)
            dve.wait_ge(bm_in, 16)

            def tile(t, u, n):
                def add_bias(j):
                    dve.wait_ge(g_done, NJ * t + j + 1)
                    if not is_first(t) or j >= 2:
                        dve.wait_ge(gate_done, NJ * t + j - 1)
                    nc.vector.tensor_tensor(gsum[j % 2][:], ps_g[j % 3][:], bm[:, j * 512:(j + 1) * 512], ALU.add).then_inc(sum_done, 1)

                def add_product(j):
                    dve.wait_ge(gate_done, NJ * t + j + 1)
                    dve.wait_ge(p_done, NJ * t + j + 1)
                    into = merged[:, (j % 2) * 512:(j % 2 + 1) * 512]
                    if j == 0 and not is_first(t):
                        dve.wait_ge(m_t, 2 * t)
                    if j < 2:
                        nc.vector.tensor_tensor(into, gate[j % 2][:], ps_p[j % 2][:], ALU.mult).then_inc(prod_done, 1)
                    else:
                        s_.link(nc.vector.tensor_tensor(gate[j % 2][:], gate[j % 2][:], ps_p[j % 2][:], ALU.mult))
                        nc.vector.tensor_tensor(into, into, gate[j % 2][:], ALU.add).then_inc(prod_done, 1)

                for j in range(NJ):
                    add_bias(j)
                    if j >= 1:
                        add_product(j - 1)
                add_product(NJ - 1)

            tile(0, 1, 0)
            with dve.Fori(0, LAT // 2) as i:
                s_.enter(i, 2 * (NJ - 2))
                for u in range(2):
                    tile(2 * i + (1 + u), u, i + u)
            s_.leave(LAT // 2)


def route(nc, T, keep):
    with nc.cleanup_on_exit(), ExitStack() as ctx:
        sb = lambda n, s, d=F32: ctx.enter_context(nc.sbuf_tensor(n, s, d))
        sem = nc.alloc_semaphore
        bank = lambda n: ctx.enter_context(nc.psum_tensor(n, [P, 512], F32))
        ident = keep.ident
        wo = sb("rt_wo", [P, DC, D])
        wq = sb("rt_wq", [P, DC, HP * P])
        keyt = sb("rt_keyt", [P, HP, P])
        gate1, scale2, shift2, gain2 = (sb(f"rt_{n}", [P, D]) for n in ("gate1", "scale2", "shift2", "gain2"))
        mt = sb("rt_mt", [P, DC, P])
        x = sb("rt_x", [P, D])
        x1 = sb("rt_x1", [P, D])
        h2 = sb("rt_h2", [P, D])
        sq = sb("rt_sq", [P, D])
        h2t = sb("rt_h2t", [P, DC, P])
        qt = sb("rt_qt", [P, HP, P])
        sc = sb("rt_sc", [P, HP, P])
        ss = sb("rt_ss", [P, 3])
        half = sb("rt_half", [P, 1])
        ps_y = [bank(f"rt_ps_y{b}") for b in range(2)]
        ps_x = [bank(f"rt_ps_x{b}") for b in range(2)]
        ps_q = [bank(f"rt_ps_q{b}") for b in range(2)]
        ps_s = [bank(f"rt_ps_s{b}") for b in range(2)]
        wo_in, wq_in = sem("rt_wo_in"), sem("rt_wq_in")
        keys_in, rows_in, rows2_in = (sem(f"rt_{n}") for n in ("keys_in", "rows_in", "rows2_in"))
        mt_in, x_in, half_set, key_t, key_out = (sem(f"rt_{n}") for n in ("mt_in", "x_in", "half_set", "key_t", "key_out"))
        y_done, x1_done, ss_done, ms_done, rstd_done, h2_done = (sem(f"rt_{n}") for n in ("y", "x1", "ss", "ms", "rstd", "h2"))
        h2_t, h2t_done, q_done, qt_done, s_done, sc_done = (sem(f"rt_{n}") for n in ("h2_t", "h2t", "q", "qt", "sco", "sc"))
        st_x1, st_h2, st_sc, step = (sem(f"rt_{n}") for n in ("st_x1", "st_h2", "st_sc", "step"))
        block = ctx.enter_context(nc.Block())

        @block.sync
        def _(sp):
            sp.dma_start(wo[:], T["w_out"][0].rearrange("(k p) n -> p k n", p=P)).then_inc(wo_in, 16)
            for dst, c in ((gate1, 2), (scale2, 4), (shift2, 3)):
                sp.dma_start(dst[:], T["mod"][0:1, c * D:(c + 1) * D].to_broadcast([P, D])).then_inc(rows_in, 16)
            sp.dma_start(gain2[:], T["g_norm2"].to_broadcast([P, D])).then_inc(rows_in, 16)
            sp.dma_start(qt[:], T["peer_keys"][0].rearrange("h a k d -> k (h a) d")).then_inc(keys_in, 16)
            sp.dma_start(wq[:], T["w_peer_q"][0].rearrange("(k p) n -> p k n", p=P)).then_inc(wq_in, 16)

            def store_norm(t):
                sp.wait_ge(x1_done, 2 * t + 2)
                sp.dma_start(row(T["x1"], t), x1[:]).then_inc(st_x1, 16)
                sp.wait_ge(h2_done, t + 1)
                sp.dma_start(row(T["h2"], t), h2[:]).then_inc(st_h2, 16)

            def store_scores(t):
                sp.wait_ge(sc_done, 4 * t + 4)
                sp.dma_start(row(T["sc"], t), sc[:].rearrange("p a n -> p (a n)")).then_inc(st_sc, 16)

            store_norm(0)
            for dst, c in ((gate1, 2), (scale2, 4), (shift2, 3)):
                sp.dma_start(dst[:], T["mod"][1:2, c * D:(c + 1) * D].to_broadcast([P, D])).then_inc(rows2_in, 16)
            with sp.Fori(0, LAT) as i:
                store_norm(i + 1)
                store_scores(i)
            store_scores(LAT)
            for s in (st_x1, st_h2, st_sc):
                sp.wait_ge(s, 16 * TILES)

        @block.gpsimd
        def _(pool):
            nc.gpsimd.memset(half[:], -0.5).then_inc(half_set, 1)
            pool.dma_start(mt[:].rearrange("p k n -> p (k n)"), row(T["mt"], 0)).then_inc(mt_in, 16)
            pool.dma_start(x[:], T["x_prompt"][0]).then_inc(x_in, 16)
            pool.wait_ge(half_set, 1)

            def rsqrt(t):
                pool.wait_ge(ms_done, t + 1)
                nc.gpsimd.tensor_tensor(ss[:, 2:3], ss[:, 1:2], half[:], ALU.pow).then_inc(rstd_done, 1)

            rsqrt(0)
            with pool.Fori(0, LAT) as i:
                pool.wait_ge(y_done, 2 * i + 2)
                pool.wait_ge(half_set, 1)
                pool.dma_start(mt[:].rearrange("p k n -> p (k n)"), row(T["mt"], i + 1)).then_inc(mt_in, 16)
                pool.wait_ge(x1_done, 2 * i + 2)
                pool.wait_ge(half_set, 1)
                pool.dma_start(x[:], row(T["x_sample"][0].rearrange("(t p) d -> t p d", p=P), i)).then_inc(x_in, 16)
                rsqrt(i + 1)

        @block.tensor
        def _(pe):
            pe.wait_ge(keys_in, 16)
            pe.wait_ge(half_set, 1)
            for b in range(4):
                if b >= 2:
                    pe.wait_ge(key_out, b - 1)
                for a in range(4):
                    tr = nc.tensor.transpose(ps_q[b % 2][:, a * P:(a + 1) * P], qt[:, 4 * b + a, :], ident[:])
                tr.then_inc(key_t, 1)

            def project_out(t):
                pe.wait_ge(mt_in, 16 * t + 16)
                if is_first(t):
                    pe.wait_ge(wo_in, 16)
                for b in range(2):
                    if not is_first(t):
                        pe.wait_ge(x1_done, 2 * t + b - 1)
                    for k in range(DC):
                        mm = nc.tensor.matmul(ps_y[b][:], mt[:, k, :], wo[:, k, b * 512:(b + 1) * 512], start=(k == 0), stop=(k == DC - 1))
                    mm.then_inc(y_done, 1)

            def queries(t):
                pe.wait_ge(h2_done, t + 1)
                if not is_first(t):
                    pe.wait_ge(h2t_done, 2 * t)
                for k in range(DC):
                    tr = nc.tensor.transpose(ps_x[k // 4][:, (k % 4) * P:(k % 4 + 1) * P], h2[:, k * P:(k + 1) * P], ident[:])
                    if k % 4 == 3:
                        tr.then_inc(h2_t, 1)
                pe.wait_ge(h2t_done, 2 * t + 2)

                def query(b):
                    if not is_first(t) or b >= 2:
                        pe.wait_ge(qt_done, 4 * t + b - 1)
                    for a in range(4):
                        for k in range(DC):
                            mm = nc.tensor.matmul(ps_q[b % 2][:, a * P:(a + 1) * P], wq[:, k, (4 * b + a) * P:(4 * b + a + 1) * P],
                                                  h2t[:, k, :], start=(k == 0), stop=(k == DC - 1))
                    mm.then_inc(q_done, 1)

                def score(b):
                    pe.wait_ge(qt_done, 4 * t + b + 1)
                    if not is_first(t) or b >= 2:
                        pe.wait_ge(sc_done, 4 * t + b - 1)
                    for a in range(4):
                        mm = nc.tensor.matmul(ps_s[b % 2][:, a * P:(a + 1) * P], qt[:, 4 * b + a, :], keyt[:, 4 * b + a, :], start=True, stop=True)
                    mm.then_inc(s_done, 1)

                query(0)
                for b in range(1, 4):
                    query(b)
                    score(b - 1)
                score(3)

            project_out(0)
            pe.wait_ge(wq_in, 16)
            pe.wait_ge(key_out, 4)
            project_out(1)
            queries(0)
            with pe.Fori(0, LAT - 1) as i:
                project_out(i + 2)
                queries(i + 1)
            queries(LAT)

        @block.scalar
        def _(act):
            for b in range(4):
                act.wait_ge(key_t, b + 1)
                nc.scalar.copy(keyt[:, 4 * b:4 * b + 4, :].rearrange("p a n -> p (a n)"), ps_q[b % 2][:]).then_inc(key_out, 1)

            def square(t):
                act.wait_ge(x1_done, 2 * t + 2)
                nc.scalar.activation(sq[:], x1[:], ACT.Square, accum_out=ss[:, 0:1]).then_inc(ss_done, 1)

            def outs(t):
                for b in range(2):
                    act.wait_ge(h2_t, 2 * t + b + 1)
                    if not is_first(t) and b == 0:
                        act.wait_ge(q_done, 4 * t)
                    nc.scalar.copy(h2t[:, 4 * b:4 * b + 4, :].rearrange("p a n -> p (a n)"), ps_x[b][:]).then_inc(h2t_done, 1)

                def query(b):
                    act.wait_ge(q_done, 4 * t + b + 1)
                    if is_first(t):
                        act.wait_ge(key_t, 4)
                    else:
                        act.wait_ge(s_done, 4 * (t - 1) + b + 1)
                    nc.scalar.copy(qt[:, 4 * b:4 * b + 4, :].rearrange("p a n -> p (a n)"), ps_q[b % 2][:]).then_inc(qt_done, 1)

                def score(b):
                    act.wait_ge(s_done, 4 * t + b + 1)
                    if not is_first(t):
                        act.wait_ge(st_sc, 16 * t)
                    nc.scalar.copy(sc[:, 4 * b:4 * b + 4, :].rearrange("p a n -> p (a n)"), ps_s[b % 2][:]).then_inc(sc_done, 1)

                query(0)
                for b in range(1, 4):
                    query(b)
                    score(b - 1)
                score(3)

            square(0)
            square(1)
            outs(0)
            with act.Fori(0, LAT - 1) as i:
                square(i + 2)
                outs(i + 1)
            outs(LAT)

        @block.vector
        def _(dve):
            s_ = Steps(dve, step)

            def norm(t):
                if not is_first(t):
                    dve.wait_ge(st_x1, 16 * t)
                    dve.wait_ge(ss_done, t)
                dve.wait_ge(x_in, 16 * t + 16)
                for b in range(2):
                    half_ = slice(b * 512, (b + 1) * 512)
                    dve.wait_ge(y_done, 2 * t + b + 1)
                    s_.link(nc.vector.tensor_tensor(x1[:, half_], ps_y[b][:], gate1[:, half_], ALU.mult))
                    nc.vector.tensor_tensor(x1[:, half_], x1[:, half_], x[:, half_], ALU.add).then_inc(x1_done, 1)
                dve.wait_ge(ss_done, t + 1)
                nc.vector.tensor_scalar(ss[:, 1:2], ss[:, 0:1], 1.0 / D, EPS, ALU.mult, ALU.add).then_inc(ms_done, 1)
                dve.wait_ge(rstd_done, t + 1)
                if not is_first(t):
                    dve.wait_ge(h2_t, 2 * t)
                    dve.wait_ge(st_h2, 16 * t)
                s_.link(nc.vector.scalar_tensor_tensor(out=h2[:], in0=x1[:], scalar=ss[:, 2:3], in1=scale2[:], op0=ALU.mult, op1=ALU.mult))
                nc.vector.tensor_tensor(h2[:], h2[:], shift2[:], ALU.add).then_inc(h2_done, 1)

            def scale_rows():
                s_.link(nc.vector.scalar_tensor_tensor(out=scale2[:], in0=scale2[:], scalar=1.0, in1=gain2[:], op0=ALU.add, op1=ALU.mult))

            dve.wait_ge(rows_in, 64)
            scale_rows()
            norm(0)
            dve.wait_ge(rows2_in, 48)
            scale_rows()
            with dve.Fori(0, LAT) as i:
                s_.enter(i, 3)
                norm(i + 1)
            s_.leave(LAT)


def experts(nc, T, keep):
    R = TOPK
    NG = PH
    ND = 10
    NPE = R - ND
    with nc.cleanup_on_exit(), ExitStack() as ctx:
        sb = lambda n, s, d=F32: ctx.enter_context(nc.sbuf_tensor(n, s, d))
        sem = nc.alloc_semaphore
        ident = keep.ident
        ring_u = sb("ex_ring_u", [P, R, D])
        ring_v = sb("ex_ring_v", [P, R, D])
        sc = sb("ex_sc", [P, HP * P])
        h2 = [sb(f"ex_h2{u}", [P, D]) for u in range(2)]
        x1 = [sb(f"ex_x1{u}", [P, D]) for u in range(2)]
        ids = [sb(f"ex_ids{u}", [P, PICKS], U32) for u in range(2)]
        ex = [sb(f"ex_ex{u}", [P, PH, TOPK]) for u in range(2)]
        idx_u, idx_v = ([sb(f"ex_idx_{n}{b}", [P, R], U32) for b in range(2)] for n in "uv")
        hold = sb("ex_hold", [P, 4])
        iota = sb("ex_iota", [P, TOPK])
        zero = sb("ex_zero", [P, P])
        diag = sb("ex_diag", [P, NPE, P])
        gate2, gfin = sb("ex_gate2", [P, D]), sb("ex_gfin", [P, D])
        head = sb("ex_head", [P, 2, P])
        v16 = sb("ex_v16", [P, 2, TOPK])
        i16 = sb("ex_i16", [P, 2, TOPK], U32)
        i16f = sb("ex_i16f", [P, 2, TOPK])
        cand = sb("ex_cand", [P, TOPK, TOPK])
        vs = sb("ex_vs", [P, TOPK])
        ic = sb("ex_ic", [P, TOPK], U32)
        part = sb("ex_part", [P, 2, TOPK], U32)
        partf = sb("ex_partf", [P, 2, TOPK])
        oh = sb("ex_oh", [P, 2, TOPK, TOPK])
        e12 = sb("ex_e12", [P, 2, TOPK])
        tot = sb("ex_tot", [P, PH])
        gw = sb("ex_gw", [P, PH, TOPK])
        dots = sb("ex_dots", [P, PICKS])
        gelu = sb("ex_gelu", [P, PICKS])
        wts = sb("ex_wts", [P, PICKS])
        acc = [sb(f"ex_acc{a}", [P, D]) for a in range(2)]
        x2 = sb("ex_x2", [P, D])
        y = sb("ex_y", [P, D])
        ss = sb("ex_ss", [P, 5])
        ps = ctx.enter_context(nc.psum_tensor("ex_ps", [P, 2, 512], F32))
        rows_in, rows2_in = sem("ex_rows_in"), sem("ex_rows2_in")
        tile_in = [sem(f"ex_tile_in{u}") for u in range(2)]
        sc_in, picked, sc_used = sem("ex_sc_in"), sem("ex_picked"), sem("ex_sc_used")
        u_in, v_in = [sem(f"ex_u_in{k}") for k in range(R)], [sem(f"ex_v_in{k}") for k in range(R)]
        used_u, used_vd, used_vp, copied_u, copied_v, waited = (
            sem(f"ex_{n}") for n in ("used_u", "used_vd", "used_vp", "copied_u", "copied_v", "waited"))
        ex_in, ex_done, dots_done, gelu_done, wts_done, diag_done, pv_done, x2_done, ss_done, ms_done, root_done, y_done, stored, step = (
            sem(f"ex_{n}") for n in ("ex_in", "ex", "dots", "gelu", "wts", "diag", "pv", "x2", "ss", "ms", "root", "y", "stored", "step"))
        zero_set, step2 = sem("ex_zero_set"), sem("ex_step2")
        block = ctx.enter_context(nc.Block())

        def order(eng, tile):
            tile(0, 1, 0)
            with eng.Fori(0, LAT // 2 - 1) as i:
                for u in range(2):
                    tile(2 * i + (1 + u), u, i + u)
            for u in range(2):
                tile(LAT - 1 + u, u, LAT // 2 - 1 + u)

        @block.sync
        def _(sp):
            def load(t, u):
                if not isinstance(t, int) or t >= 2:
                    sp.wait_ge(y_done, t - 1)
                sp.dma_start(h2[u][:], row(T["h2"], t)).then_inc(tile_in[u], 16)
                sp.dma_start(x1[u][:], row(T["x1"], t)).then_inc(tile_in[u], 16)

            def load_scores(t):
                if not is_first(t):
                    sp.wait_ge(sc_used, NG * t)
                sp.dma_start(sc[:], row(T["sc"], t)).then_inc(sc_in, 16)

            y_lat = T["y_sample"][0].rearrange("(t p) d -> t p d", p=P)

            def store(t):
                sp.wait_ge(y_done, t + 1)
                sp.dma_start(row(y_lat, t - 1), y[:]).then_inc(stored, 16)

            load_scores(0)
            sp.dma_start(iota[:], T["const_iota"]).then_inc(rows_in, 16)
            load(0, 1)
            sp.dma_start(gate2[:], T["mod"][0:1, 5 * D:6 * D].to_broadcast([P, D])).then_inc(rows_in, 16)
            sp.dma_start(gfin[:], T["g_final"].rearrange("(a d) -> a d", a=1).to_broadcast([P, D])).then_inc(rows_in, 16)
            load(1, 0)
            load_scores(1)
            sp.wait_ge(y_done, 1)
            sp.dma_start(T["y_prompt"][0], y[:]).then_inc(stored, 16)
            sp.dma_start(gate2[:], T["mod"][1:2, 5 * D:6 * D].to_broadcast([P, D])).then_inc(rows2_in, 16)
            load_scores(2)
            load(2, 1)
            store(1)
            with sp.Fori(0, LAT // 2 - 1) as i:
                for u in range(2):
                    load_scores(2 * i + (3 + u))
                    load(2 * i + (3 + u), u)
                    store(2 * i + (2 + u))
            store(LAT)
            sp.wait_ge(stored, 16 * TILES)

        @block.gpsimd
        def _(pool):
            nc.gpsimd.memset(zero[:], 0.0).then_inc(zero_set, 1)

            def tile(t, u, n):
                def group(g2, b, table, ring, idx, arrived, copied, waits):
                    q = t * NG + g2 * 2 + b
                    for used, first, per in waits:
                        pool.wait_ge(used, q * per + 1)
                    nc.gpsimd.tensor_copy(idx[b][:], cols(ids[u], g2 * (2 * R) + b * R, R)).then_inc(copied, 1)
                    pool.wait_ge(copied, q + 1)
                    pool.sem_inc(waited, 1)
                    for k in range(R):
                        used, first, per = [w for w in waits if k >= w[1]][-1]
                        if k > first:
                            pool.wait_ge(used, q * per + (k - first + 1))
                            pool.sem_inc(waited, 1)
                        nc.gpsimd.indirect_dma_start(ring[:, k, :], None, table[0], bass.IndirectOffsetOnAxis(
                            ap=idx[b][:, k:k + 1], axis=0)).then_inc(arrived[k], 16)

                with pool.Fori(0, NG // 2) as g2:
                    for b in range(2):
                        pool.wait_ge(picked, t * NG + g2 * 2 + (b + 1))
                        group(g2, b, T["peer_u"], ring_u, idx_u, u_in, copied_u, ((used_u, 0, R),))
                with pool.Fori(0, NG // 2) as g2:
                    for b in range(2):
                        group(g2, b, T["peer_v"], ring_v, idx_v, v_in, copied_v, ((used_vd, 0, ND), (used_vp, ND, NPE)))

            order(pool, tile)

        @block.tensor
        def _(pe):
            pe.wait_ge(zero_set, 1)
            pe.wait_ge(rows_in, 48)

            def tile(t, u, n):
                if not is_first(t):
                    pe.wait_ge(x2_done, t)
                for b in range(2):
                    nc.tensor.matmul(ps[:, b, :], zero[:], gfin[:, b * 512:(b + 1) * 512], start=True, stop=False)
                with pe.Fori(0, NG) as g:
                    q = t * NG + g
                    for j in range(NPE):
                        pe.wait_ge(diag_done, q * NPE + (j + 1))
                        pe.wait_ge(v_in[ND + j], 16 * q + 16)
                        for b in range(2):
                            mm = nc.tensor.matmul(ps[:, b, :], diag[:, j, :], ring_v[:, ND + j, b * 512:(b + 1) * 512], start=False, stop=False)
                        mm.then_inc(used_vp, 1)
                for b in range(2):
                    mm = nc.tensor.matmul(ps[:, b, :], zero[:], gfin[:, b * 512:(b + 1) * 512], start=False, stop=True)
                mm.then_inc(pv_done, 1)

            order(pe, tile)

        @block.scalar
        def _(act):
            act.wait_ge(ex_in, 1)
            nc.scalar.activation(ex[1][:], ex[1][:], ACT.Exp).then_inc(ex_done, 1)

            def tile(t, u, n):
                act.wait_ge(dots_done, t + 1)
                nc.scalar.activation(gelu[:], dots[:], ACT.Gelu_apprx_tanh).then_inc(gelu_done, 1)
                act.wait_ge(wts_done, t + 1)
                nc.scalar.copy(ss[:, 3:4], ss[:, 2:3])
                with act.Fori(0, NG) as g:
                    q = t * NG + g
                    for j in range(NPE):
                        act.wait_ge(used_vp, q * NPE + (j + 1))
                        nc.scalar.activation(diag[:, j, :], ident[:], ACT.Copy, scale=cols(wts, g * R + (ND + j), 1)).then_inc(diag_done, 1)
                if not (isinstance(t, int) and t == LAT):
                    act.wait_ge(ex_in, t + 2)
                    nc.scalar.activation(ex[1 - u][:], ex[1 - u][:], ACT.Exp).then_inc(ex_done, 1)
                act.wait_ge(x2_done, t + 1)
                nc.scalar.activation(acc[1][:], x2[:], ACT.Square, accum_out=ss[:, 0:1]).then_inc(ss_done, 1)
                act.wait_ge(ms_done, t + 1)
                nc.scalar.activation(ss[:, 2:3], ss[:, 1:2], ACT.Sqrt).then_inc(root_done, 1)

            order(act, tile)

        @block.vector
        def _(dve):
            nc.vector.memset(hold[:, 0:1], 0.0).then_inc(used_u, R)
            nc.vector.memset(ss[:], 1.0).then_inc(used_vd, ND)
            nc.vector.memset(gw[:, 0, 0:1], 0.0).then_inc(used_vp, NPE)
            dve.wait_ge(rows_in, 48)

            def pick(link, t, u, g):
                dve.wait_ge(sc_in, 16 * t + 16)
                link(nc.vector.tensor_copy(head[:].rearrange("p a n -> p (a n)"), cols(sc, g * (2 * P), 2 * P)), sc_used)

                def top16(rows, values, indices):
                    for r, v in zip(rows, values):
                        last = nc.vector.max(v[:, 0:8], r)
                    link(last)
                    nc.vector.memset(hold[:, 0:1], 0.0)
                    for r, v, i in zip(rows, values, indices):
                        last = nc.vector.max_index(i[:, 0:8], v[:, 0:8], r)
                    link(last)
                    nc.vector.memset(hold[:, 0:1], 0.0)
                    for r, v in zip(rows, values):
                        last = nc.vector.match_replace(r, v[:, 0:8], r, BIG)
                    link(last)
                    nc.vector.memset(hold[:, 0:1], 0.0)
                    for r, v in zip(rows, values):
                        last = nc.vector.max(v[:, 8:16], r)
                    link(last)
                    nc.vector.memset(hold[:, 0:1], 0.0)
                    for r, v, i in zip(rows, values, indices):
                        last = nc.vector.max_index(i[:, 8:16], v[:, 8:16], r)
                    link(last)

                nc.vector.memset(hold[:, 0:1], 0.0)
                top16([head[:, a, :] for a in range(2)], [v16[:, a, :] for a in range(2)], [i16[:, a, :] for a in range(2)])
                nc.vector.tensor_copy(i16f[:], i16[:])
                square = [P, TOPK, TOPK]
                link(nc.vector.tensor_tensor(cand[:], v16[:, 0, :].unsqueeze(2).to_broadcast(square),
                                             v16[:, 1, :].unsqueeze(1).to_broadcast(square), ALU.add))
                nc.vector.memset(hold[:, 0:1], 0.0)
                top16([cand[:].rearrange("p a b -> p (a b)")], [vs[:]], [ic[:]])
                nc.vector.tensor_tensor(cols(ex[u][:].rearrange("p h k -> p (h k)"), g * TOPK, TOPK), vs[:],
                                        vs[:, 0:1].to_broadcast([P, TOPK]), ALU.subtract)
                nc.vector.tensor_scalar(part[:, 0, :], ic[:], 4, None, ALU.logical_shift_right)
                link(nc.vector.tensor_scalar(part[:, 1, :], ic[:], TOPK - 1, None, ALU.bitwise_and))
                link(nc.vector.tensor_copy(partf[:], part[:]))
                both = [P, 2, TOPK, TOPK]
                link(nc.vector.tensor_tensor(oh[:], partf[:].unsqueeze(3).to_broadcast(both),
                                             iota[:].unsqueeze(1).unsqueeze(1).to_broadcast(both), ALU.is_equal))
                link(nc.vector.tensor_tensor(oh[:], oh[:], i16f[:].unsqueeze(2).to_broadcast(both), ALU.mult))
                link(nc.vector.tensor_reduce(e12[:], oh[:], AX_X, ALU.add))
                link(nc.vector.scalar_tensor_tensor(out=cols(ids[u], g * TOPK, TOPK), in0=e12[:, 0, :], scalar=float(P), in1=e12[:, 1, :],
                                                    op0=ALU.mult, op1=ALU.add), picked)

            NL = 5 + 1 + 5 + 1 + 1 + 3
            step_of = lambda t, g, c: (t * NG + g) * NL + c

            def pick_at(t, u, g):
                count = [0]

                def link(ins, named=None):
                    if named is not None:
                        ins.then_inc(named, 1)
                        dve.wait_ge(named, t * NG + g + 1)
                        return
                    ins.then_inc(step, 1)
                    count[0] += 1
                    dve.wait_ge(step, step_of(t, g, count[0]))

                pick(link, t, u, g)
                assert count[0] == NL, count
                nc.vector.memset(hold[:, 0:1], 0.0)

            s_ = Steps(dve, step2)

            def tile(t, u, n):
                last_tile = isinstance(t, int) and t == LAT
                dve.wait_ge(tile_in[u], 32 * n + 32)
                nc.vector.memset(hold[:, 2:3], 0.0)
                with dve.Fori(0, NG) as g:
                    q = t * NG + g
                    for k in range(R):
                        dve.wait_ge(u_in[k], 16 * q + 16)
                        nc.vector.scalar_tensor_tensor(out=ring_u[:, k, :], in0=ring_u[:, k, :], scalar=1.0, in1=h2[u][:], op0=ALU.mult, op1=ALU.mult,
                                                       accum_out=cols(dots, g * R + k, 1)).then_inc(used_u, 1)
                dve.wait_ge(used_u, (t + 1) * PICKS + R)
                if not is_first(t):
                    dve.wait_ge(ss_done, t)
                nc.vector.memset(acc[0][:], 0.0).then_inc(dots_done, 1)
                s_.link(nc.vector.memset(acc[1][:], 0.0))
                dve.wait_ge(ex_done, t + 1)
                s_.link(nc.vector.tensor_reduce(tot[:], ex[u][:], AX_X, ALU.add))
                s_.link(nc.vector.reciprocal(tot[:], tot[:]))
                s_.link(nc.vector.tensor_tensor(gw[:], ex[u][:], tot[:].unsqueeze(2).to_broadcast([P, PH, TOPK]), ALU.mult))
                dve.wait_ge(gelu_done, t + 1)
                if not is_first(t):
                    dve.wait_ge(diag_done, t * NG * NPE)
                nc.vector.tensor_tensor(wts[:], gelu[:], gw[:].rearrange("p h k -> p (h k)"), ALU.mult).then_inc(wts_done, 1)
                dve.wait_ge(wts_done, t + 1)
                nc.vector.memset(hold[:, 3:4], 0.0)
                with dve.Fori(0, NG) as g:
                    q = t * NG + g
                    for k in range(ND):
                        dve.wait_ge(v_in[k], 16 * q + 16)
                        dve.wait_ge(used_vd, q * ND + (k + ND - 1))
                        nc.vector.scalar_tensor_tensor(out=acc[k % 2][:], in0=ring_v[:, k, :], scalar=cols(wts, g * R + k, 1),
                                                       in1=acc[k % 2][:], op0=ALU.mult, op1=ALU.add).then_inc(used_vd, 1)
                    if not last_tile:
                        pick_at(t + 1, 1 - u, g)
                dve.wait_ge(used_vd, (t + 1) * NG * ND + ND)
                if not last_tile:
                    nc.vector.memset(hold[:, 1:2], 0.0).then_inc(ex_in, 1)
                s_.link(nc.vector.tensor_tensor(acc[0][:], acc[0][:], acc[1][:], ALU.add))
                dve.wait_ge(pv_done, t + 1)
                s_.link(nc.vector.tensor_tensor(acc[0][:], acc[0][:], ps[:].rearrange("p b n -> p (b n)"), ALU.add))
                s_.link(nc.vector.tensor_tensor(acc[0][:], acc[0][:], gate2[:], ALU.mult))
                nc.vector.tensor_tensor(x2[:], acc[0][:], x1[u][:], ALU.add).then_inc(x2_done, 1)
                dve.wait_ge(ss_done, t + 1)
                nc.vector.tensor_scalar(ss[:, 1:2], ss[:, 0:1], 1.0 / D, EPS, ALU.mult, ALU.add).then_inc(ms_done, 1)
                dve.wait_ge(root_done, t + 1)
                s_.link(nc.vector.reciprocal(ss[:, 3:4], ss[:, 2:3]))
                s_.link(nc.vector.scalar_tensor_tensor(out=ss[:, 4:5], in0=ss[:, 3:4], scalar=ss[:, 1:2], in1=ss[:, 3:4], op0=ALU.mult, op1=ALU.mult))
                s_.link(nc.vector.tensor_scalar(ss[:, 4:5], ss[:, 4:5], -0.5, 1.5, ALU.mult, ALU.add))
                s_.link(nc.vector.tensor_tensor(ss[:, 4:5], ss[:, 4:5], ss[:, 3:4], ALU.mult))
                if not is_first(t):
                    dve.wait_ge(stored, 16 * t)
                nc.vector.scalar_tensor_tensor(out=y[:], in0=x2[:], scalar=ss[:, 4:5], in1=gfin[:], op0=ALU.mult, op1=ALU.mult).then_inc(y_done, 1)

            with dve.Fori(0, NG) as g:
                pick_at(0, 1, g)
            nc.vector.memset(hold[:, 1:2], 0.0).then_inc(ex_in, 1)
            tile(0, 1, 0)
            dve.wait_ge(rows2_in, 16)
            PER = 11
            with dve.Fori(0, LAT // 2 - 1) as i:
                s_.enter(i, 2 * PER)
                for u in range(2):
                    tile(2 * i + (1 + u), u, i + u)
            s_.leave(LAT // 2 - 1)
            for u in range(2):
                tile(LAT - 1 + u, u, LAT // 2 - 1 + u)


SCRATCH = {"mod": [2, 6 * D], "ht": [TILES, P, D], "kv": [TILES, P, 2 * MIX], "og": [TILES, P, MIX],
           "qat": [TILES, AD, AH * P], "qkt": [TILES, P, 2 * MIX], "yct": [TILES, P, MIX],
           "yt": [TILES, P, 2 * MIX], "mt": [TILES, P, D], "x1": [TILES, P, D], "h2": [TILES, P, D],
           "sc": [TILES, P, HP * P]}


class Keep:
    pass


def trunk(nc, ins, outs, phases=99, debug=False):
    kind = {"kind": "ExternalOutput"} if debug else {}
    scratch = {name: nc.dram_tensor(f"s_{name}", shape, F32, **kind).ap() for name, shape in SCRATCH.items()}
    T = {**ins, **outs, **scratch}
    modulate(nc, T)
    keep = Keep()
    with ExitStack() as ctx:
        keep.ident = ctx.enter_context(nc.sbuf_tensor("ident", [P, P], F32))
        with ExitStack() as mixer:
            keep.gates = mixer.enter_context(nc.sbuf_tensor("gates", [P, TILES, 16], F32))
            keep.kat = mixer.enter_context(nc.sbuf_tensor("kat", [AD, AKV, (TILES + 1) * P], F32))
            keep.va = mixer.enter_context(nc.sbuf_tensor("va", [P, TILES + 1, P], F32))
            project(nc, T, keep)
            keep.hd = mixer.enter_context(nc.sbuf_tensor("hd", [P, 2, TILES * MIX], F32))
            mlstm(nc, T, keep)
            attend(nc, T, keep)
        for n, phase in enumerate((merge, route, experts)):
            if n < phases:
                phase(nc, T, keep)


_INS = ['x_prompt', 'x_sample', 'cache_k', 'cache_v', 'state_C', 'state_n', 'state_m', 'c', 'c_ctx',
        'w_ada', 'b_ada', 'g_norm1', 'g_norm2', 'w_in', 'b_gates_m', 'g_mlstm', 'w_spatial', 'b_spatial', 'sink',
        'w_branch', 'w_merge', 'b_merge', 'w_out', 'w_peer_q', 'peer_keys', 'peer_u', 'peer_v', 'g_final']
_OUTS = [("y_prompt", (1, P, D)), ("y_sample", (1, LAT * P, D)), ("new_k", (1, 1, P, AKV, AD)), ("new_v", (1, 1, P, AKV, AD)),
         ("new_C", (1, 1, 2, MH, MD, MD)), ("new_n", (1, 1, 2, MH, MD)), ("new_m", (1, 1, 2, MH))]


def kernel(**inputs):
    import concourse.bacc as bacc
    from concourse.bass_utils import run_bass_kernel_spmd

    nc = bacc.Bacc("TRN2", target_bir_lowering=False, num_devices=1)
    arrays, ins, outs = {}, {}, {}
    given = {name: np.ascontiguousarray(inputs[name]) for name in _INS}
    for name, a in {**given, **host_constants()}.items():
        arrays[f"in_{name}"] = a
        ins[name] = nc.dram_tensor(f"in_{name}", a.shape, mybir.dt.from_np(a.dtype), kind="ExternalInput").ap()
    for name, shape in _OUTS:
        outs[name] = nc.dram_tensor(f"out_{name}", shape, F32, kind="ExternalOutput").ap()
    trunk(nc, ins, outs)
    r = run_bass_kernel_spmd(nc, [arrays], core_ids=[0])
    return tuple(r.results[0][f"out_{name}"] for name, _ in _OUTS)
```

```python
from contextlib import ExitStack

import numpy as np

import concourse.bass as bass
from concourse import mybir

F32 = mybir.dt.float32
U32 = mybir.dt.uint32
ALU = mybir.AluOpType
ACT = mybir.ActivationFunctionType
AX_X = mybir.AxisListType.X

P = 128
D = 1024
DC = D // P
LAT = 8
TILES = 1 + LAT
EPS = 1e-6
MIX = D // 2
MH, MD = 4, 128
AH, AKV, AD = 8, 2, 64
IN_W = 7 * MIX + 4 * MH + 2 * AKV * AD
NEXP = 16384
PH, TOPK = 8, 16
PICKS = PH * TOPK
HP = 2 * PH
GRID_W = 64
NEG = -1e30
BIG = -3.0e38


class Steps:

    def __init__(self, eng, sem):
        self.eng, self.sem, self.base, self.n, self.i, self.per = eng, sem, 0, 0, None, 0

    def enter(self, i, per):
        self.base, self.n, self.i, self.per = self.base + self.n, 0, i, per

    def leave(self, turns):
        assert self.n == self.per, f"{self.sem}: {self.n} steps a turn, {self.per} said"
        self.base, self.n, self.i = self.base + self.per * turns, 0, None

    def value(self):
        flat = self.base + self.n
        return flat if self.i is None else self.i * self.per + flat

    def link(self, ins):
        ins.then_inc(self.sem, 1)
        self.n += 1
        self.eng.wait_ge(self.sem, self.value())


def is_first(t):
    return isinstance(t, int) and t == 0


def cols(ap, a, n):
    return ap[:, bass.ds(a, n)]


def row(ap, t):
    return ap[bass.ds(t, 1)].rearrange("a p n -> (a p) n")


def host_constants():
    n = LAT * P
    pos = np.arange(n)
    freqs = 10000.0 ** (-np.arange(16, dtype=np.float32) / 16)
    tabs = []
    for axis in (pos // GRID_W, pos % GRID_W):
        ang = axis.astype(np.float32)[:, None] * freqs[None, :].astype(np.float32)
        tabs.append((np.cos(ang), np.sin(ang)))
    cos = np.concatenate([tabs[0][0], tabs[0][0], tabs[1][0], tabs[1][0]], 1).astype(np.float32)
    sin = np.concatenate([-tabs[0][1], tabs[0][1], -tabs[1][1], tabs[1][1]], 1).astype(np.float32)
    rope = np.concatenate([cos, sin], 1).reshape(LAT, P, 2 * AD)
    q, k = np.arange(P)[:, None], np.arange(3 * P)[None, :] - P
    band = np.where(np.abs(q - k) <= P, 0.0, NEG * 8)
    win = np.zeros((LAT, P, 4 * P), np.float32)
    for t in range(LAT):
        win[t, :, P:] = band
        if t == 0:
            win[t, :, P:2 * P] = NEG * 8
        if t == LAT - 1:
            win[t, :, 3 * P:] = NEG * 8
    s, tt = np.arange(P)[:, None], np.arange(P)[None, :]
    causal = np.stack([np.where(s <= tt, 0.0, NEG), np.where(s >= tt, 0.0, NEG)]).astype(np.float32)
    restart = np.ones((MH, 2, TILES, P), np.float32)
    restart[:, 0, :, 0] = 0.0
    restart[:, 1, :, P - 1] = 0.0
    head_row = np.zeros((MH, MH, P), np.float32)
    for h in range(MH):
        head_row[h, h] = 1.0
    return {
        "const_ident": np.eye(P, dtype=np.float32), "const_rope": rope, "const_window": win,
        "const_causal": causal, "const_restart": restart.reshape(MH, -1),
        "const_head_row": head_row.reshape(MH, -1),
        "const_iota": np.tile(np.arange(TOPK, dtype=np.float32), (P, 1)),
    }


Q0, K0, V0, O0, G0, U0, S0, A0 = 0, MIX, 2 * MIX, 3 * MIX, 4 * MIX, 4 * MIX + 16, 5 * MIX + 16, 6 * MIX + 16


EARLY = 3


def load_w_in(sp, T, keep, k):
    rows = T["w_in"][0, k * P:(k + 1) * P, :]
    sp.dma_start(keep.big[:, k, 0:U0], rows[:, 0:U0]).then_inc(keep.w_in[k], 16)
    sp.dma_start(keep.w_us[:, k, :], rows[:, U0:A0]).then_inc(keep.w_in[k], 16)
    sp.dma_start(keep.big[:, k, U0:U0 + IN_W - A0], rows[:, A0:]).then_inc(keep.w_in[k], 16)


def modulate(nc, T, keep):
    NB = 6 * D // 512
    with nc.cleanup_on_exit(), ExitStack() as ctx:
        sb = lambda n, s, d=F32: ctx.enter_context(nc.sbuf_tensor(n, s, d))
        sem = nc.alloc_semaphore
        cond = sb("mo_cond", [P, 2, DC])
        act = sb("mo_silu", [P, DC, 2])
        wa = [sb(f"mo_w{u}", [P, DC, 512]) for u in range(2)]
        mod = sb("mo_mod", [2, 6 * D])
        ps = [ctx.enter_context(nc.psum_tensor(f"mo_ps{u}", [P, 512], F32)) for u in range(2)]
        cond_in, bias_in, silu_done = sem("mo_cond_in"), sem("mo_bias_in"), sem("mo_silu_done")
        w_in_ = [sem(f"mo_w_in{u}") for u in range(2)]
        prod, mod_done, stored = sem("mo_prod"), sem("mo_mod_done"), sem("mo_stored")
        w_view = T["w_ada"][0].rearrange("(k p) n -> p k n", p=P)
        block = ctx.enter_context(nc.Block())

        @block.sync
        def _(sp):
            sp.dma_start(cond[:, 0, :], T["c_ctx"].rearrange("(k p) -> p k", p=P), allow_slow_non_contiguous=True).then_inc(cond_in, 16)
            sp.dma_start(cond[:, 1, :], T["c"][0].rearrange("(k p) -> p k", p=P), allow_slow_non_contiguous=True).then_inc(cond_in, 16)
            sp.dma_start(mod[:], T["b_ada"].to_broadcast([2, 6 * D])).then_inc(bias_in, 16)
            for u in range(2):
                sp.dma_start(wa[u][:], w_view[:, :, u * 512:u * 512 + 512]).then_inc(w_in_[u], 16)
            with sp.Fori(1, NB // 2) as i:
                for u in range(2):
                    sp.wait_ge(prod, 2 * i + u - 1)
                    sp.dma_start(wa[u][:], w_view[:, :, bass.ds((2 * i + u) * 512, 512)]).then_inc(w_in_[u], 16)
            for k in range(EARLY):
                load_w_in(sp, T, keep, k)
            sp.wait_ge(mod_done, NB)
            sp.dma_start(T["mod"], mod[:]).then_inc(stored, 16)
            sp.wait_ge(stored, 16)

        @block.scalar
        def _(act_eng):
            act_eng.wait_ge(cond_in, 32)
            nc.scalar.activation(act[:].rearrange("p k c -> p c k"), cond[:], ACT.Silu).then_inc(silu_done, 1)

        @block.tensor
        def _(pe):
            pe.wait_ge(silu_done, 1)

            def column_block(i, u, first):
                pe.wait_ge(w_in_[u], 16 * i + 16)
                if not first:
                    pe.wait_ge(mod_done, 2 * i + u - 1)
                for k in range(DC):
                    mm = nc.tensor.matmul(ps[u][0:2, :], act[:, k, :], wa[u][:, k, :], start=(k == 0), stop=(k == DC - 1))
                mm.then_inc(prod, 1)

            column_block(0, 0, True)
            column_block(0, 1, True)
            with pe.Fori(1, NB // 2) as i:
                for u in range(2):
                    column_block(i, u, False)

        @block.vector
        def _(dve):
            dve.wait_ge(bias_in, 16)
            with dve.Fori(0, NB // 2) as i:
                for u in range(2):
                    dve.wait_ge(prod, 2 * i + u + 1)
                    at = (2 * i + u) * 512
                    nc.vector.tensor_tensor(cols(mod, at, 512), ps[u][0:2, :], cols(mod, at, 512),
                                            ALU.add).then_inc(mod_done, 1)


def load_norm_rows(sp, T, scale_t, shift_t, gain_t, row, sc_col, sh_col, gain, done):
    sp.dma_start(scale_t, T["mod"][row:row + 1, sc_col * D:(sc_col + 1) * D].to_broadcast([P, D])).then_inc(done, 16)
    sp.dma_start(shift_t, T["mod"][row:row + 1, sh_col * D:(sh_col + 1) * D].to_broadcast([P, D])).then_inc(done, 16)
    sp.dma_start(gain_t, gain.to_broadcast([P, D])).then_inc(done, 16)


def project(nc, T, keep):
    with nc.cleanup_on_exit(), ExitStack() as ctx:
        sb = lambda n, s, d=F32: ctx.enter_context(nc.sbuf_tensor(n, s, d))
        sem = nc.alloc_semaphore
        bank = lambda n: ctx.enter_context(nc.psum_tensor(n, [P, 512], F32))
        ident, gates, kat, va = keep.ident, keep.gates, keep.kat, keep.va
        x = sb("pj_x", [P, D])
        h = sb("pj_h", [P, D])
        scale1, shift1 = sb("pj_scale1", [P, D]), sb("pj_shift1", [P, D])
        ht = sb("pj_ht", [P, DC, P])
        qkv = sb("pj_qkv", [P, 3 * MIX])
        og = sb("pj_og", [P, MIX])
        u = sb("pj_u", [P, MIX])
        sv = sb("pj_sv", [P, MIX])
        vr = sb("pj_vr", [P, MIX])
        yc = sb("pj_yc", [P, MIX])
        qka = sb("pj_qka", [P, MIX + 2 * AKV * AD])
        rot_c = sb("pj_rot_c", [P, 10, AD])
        rot_s = sb("pj_rot_s", [P, 10, 2, 2, 16])
        qr = sb("pj_qr", [P, 10, AD])
        qkt = sb("pj_qkt", [P, 2 * MIX])
        qat = sb("pj_qat", [AD, AH * P])
        yct = sb("pj_yct", [P, MIX])
        rope = sb("pj_rope", [P, 2 * AD])
        spare = U0 + IN_W - A0
        ws, wst = keep.big[:, 0:4, spare:spare + P], keep.big[:, 4:8, spare:spare + P]
        bs = sb("pj_bs", [P, 4])
        gb = sb("pj_gb", [P, 16])
        ss = sb("pj_ss", [P, 8])
        half = sb("pj_half", [P, 1])
        gain1 = keep.acc
        ps_x = ctx.enter_context(nc.psum_tensor("pj_ps_x", [P, 2, 512], F32))
        ps_z = [bank(f"pj_ps_z{b}") for b in range(3)]
        ps_t = [bank(f"pj_ps_t{b}") for b in range(2)]
        ps_m = bank("pj_ps_m")

        rows_in, small_in, rope_in, x_in = sem("pj_rows_in"), sem("pj_small_in"), sem("pj_rope_in"), sem("pj_x_in")
        rows2_in, half_set = sem("pj_rows2_in"), sem("pj_half_set")
        ws_t, ws_done = sem("pj_ws_t"), sem("pj_ws_done")
        ss_done, ms_done, rstd_done = sem("pj_ss_done"), sem("pj_ms_done"), sem("pj_rstd_done")
        h_done, x_t, ht_done = sem("pj_h_done"), sem("pj_x_t"), sem("pj_ht_done")
        z_done, z_act, z_dve = sem("pj_z_done"), sem("pj_z_act"), sem("pj_z_dve")
        ssv_done, msv_done, rstdv_done, vr_done = sem("pj_ssv"), sem("pj_msv"), sem("pj_rstdv"), sem("pj_vr_done")
        qr_done, gm_done, yc_done = sem("pj_qr_done"), sem("pj_gm_done"), sem("pj_yc_done")
        t_done, t_out = sem("pj_t_done"), sem("pj_t_out")
        st_h, st_qa, st_qk, st_kv, st_o, st_yc, st_new = (sem(f"pj_st_{n}") for n in ("h", "qa", "qk", "kv", "o", "yc", "new"))
        step = sem("pj_dve_step")
        block = ctx.enter_context(nc.Block())

        ZB = [(A0, 512, "d"), (A0 + 512, 256, "d"), (S0, 512, "a"), (U0, 512, "a"), (Q0, 512, "d"),
              (K0, 512, "a"), (V0, 512, "d"), (O0, 512, "a"), (G0, 16, "d")]
        NZ = len(ZB)
        NT = 6
        per = {"d": sum(b[2] == "d" for b in ZB), "a": sum(b[2] == "a" for b in ZB)}
        rank = [sum(c[2] == b[2] for c in ZB[:j + 1]) for j, b in enumerate(ZB)]
        zsem = {"d": z_dve, "a": z_act}

        def weights(k, c0, n):
            if U0 <= c0 < A0:
                return keep.w_us[:, k, c0 - U0:c0 - U0 + n]
            at = c0 if c0 < U0 else c0 - A0 + U0
            return keep.big[:, k, at:at + n]

        @block.sync
        def _(sp):
            sp.dma_start(ident[:], T["const_ident"]).then_inc(small_in, 16)
            load_norm_rows(sp, T, scale1[:], shift1[:], gain1[:], 0, 1, 0, T["g_norm1"], rows_in)
            sp.dma_start(ws, T["w_spatial"][0].rearrange("g p q -> p g q")).then_inc(small_in, 16)
            sp.dma_start(bs[:], T["b_spatial"][0].rearrange("g p -> p g"), allow_slow_non_contiguous=True).then_inc(small_in, 16)
            sp.dma_start(gb[:], T["b_gates_m"].rearrange("a g h -> a (g h)").to_broadcast([P, 16])).then_inc(small_in, 16)

            for k in range(EARLY, DC):
                load_w_in(sp, T, keep, k)

            def stores(t):
                sp.wait_ge(ht_done, 2 * t + 2)
                sp.dma_start(row(T["ht"], t), ht[:].rearrange("p k n -> p (k n)")).then_inc(st_h, 16)
                if is_first(t):
                    sp.wait_ge(z_dve, 2)
                    sp.dma_start(T["new_k"][0, 0].rearrange("s k d -> s (k d)"), qka[:, 512:640]).then_inc(st_new, 16)
                    sp.dma_start(T["new_v"][0, 0].rearrange("s k d -> s (k d)"), qka[:, 640:768]).then_inc(st_new, 16)
                sp.wait_ge(z_act, t * per["a"] + rank[5])
                sp.wait_ge(z_dve, t * per["d"] + rank[6])
                sp.dma_start(row(T["kv"], t), qkv[:, MIX:]).then_inc(st_kv, 16)
                sp.wait_ge(z_act, t * per["a"] + rank[7])
                sp.dma_start(row(T["og"], t), og[:]).then_inc(st_o, 16)
                sp.wait_ge(t_out, t * NT + 2)
                sp.dma_start(row(T["qat"], t), qat[:]).then_inc(st_qa, 16)
                sp.wait_ge(t_out, t * NT + 5)
                sp.dma_start(row(T["qkt"], t), qkt[:]).then_inc(st_qk, 16)
                sp.wait_ge(t_out, t * NT + 6)
                sp.dma_start(row(T["yct"], t), yct[:]).then_inc(st_yc, 16)

            stores(0)
            with sp.Fori(0, LAT) as i:
                stores(i + 1)
            for s in (st_h, st_qa, st_qk, st_kv, st_o, st_yc):
                sp.wait_ge(s, 16 * TILES)

        @block.gpsimd
        def _(pool):
            nc.gpsimd.memset(half[:], -0.5).then_inc(half_set, 1)
            nc.gpsimd.memset(kat[:, :, TILES * P:], 0.0).then_inc(half_set, 1)
            nc.gpsimd.memset(va[:, TILES, :], 0.0).then_inc(half_set, 1)
            pool.wait_ge(half_set, 3)

            def rsqrt(t, ready, a, b, done):
                pool.wait_ge(ready, t + 1)
                nc.gpsimd.tensor_tensor(ss[:, b:b + 1], ss[:, a:a + 1], half[:], ALU.pow).then_inc(done, 1)

            pool.dma_start(x[:], T["x_prompt"][0]).then_inc(x_in, 16)
            rsqrt(0, ms_done, 1, 2, rstd_done)
            pool.wait_ge(h_done, 1)
            for tile_, col in ((scale1, 1), (shift1, 0)):
                pool.dma_start(tile_[:], T["mod"][1:2, col * D:(col + 1) * D].to_broadcast([P, D])).then_inc(rows2_in, 16)
            x_lat = T["x_sample"][0].rearrange("(t p) d -> t p d", p=P)
            pool.dma_start(x[:], row(x_lat, 0)).then_inc(x_in, 16)

            def tile(t, last=False):
                pool.wait_ge(qr_done, t + 1)
                pool.wait_ge(half_set, 1)
                pool.dma_start(rope[:], row(T["const_rope"], t)).then_inc(rope_in, 16)
                rsqrt(t, msv_done, 4, 5, rstdv_done)
                rsqrt(t + 1, ms_done, 1, 2, rstd_done)
                if not last:
                    pool.wait_ge(h_done, t + 2)
                    pool.wait_ge(half_set, 1)
                    pool.dma_start(x[:], row(x_lat, t + 1)).then_inc(x_in, 16)

            with pool.Fori(0, LAT - 1) as t:
                tile(t)
            tile(LAT - 1, last=True)
            rsqrt(LAT, msv_done, 4, 5, rstdv_done)

        @block.tensor
        def _(pe):
            pe.wait_ge(small_in, 64)
            for g in range(4):
                tr = nc.tensor.transpose(ps_m[:, g * P:(g + 1) * P], ws[:, g, :], ident[:])
            tr.then_inc(ws_t, 1)

            def turn(t):
                pe.wait_ge(h_done, t + 1)
                if not is_first(t):
                    pe.wait_ge(ht_done, 2 * t)
                for k in range(DC):
                    tr = nc.tensor.transpose(ps_x[:, k // 4, (k % 4) * P:(k % 4 + 1) * P], h[:, k * P:(k + 1) * P], ident[:])
                    if k % 4 == 3:
                        tr.then_inc(x_t, 1)

            def tile(t, last=False):
                pe.wait_ge(ht_done, 2 * t + 2)
                for j, (c0, n, _) in enumerate(ZB):
                    if not is_first(t) or j >= 3:
                        prev = j - 3 if j >= 3 else j - 3 + NZ
                        eng = ZB[prev][2]
                        back = t if j >= 3 else t - 1
                        pe.wait_ge(zsem[eng], back * per[eng] + rank[prev])
                    for k in range(DC):
                        if is_first(t) and j == 0:
                            pe.wait_ge(keep.w_in[k], 48)
                        mm = nc.tensor.matmul(ps_z[j % 3][:, 0:n], ht[:, k, :], weights(k, c0, n), start=(k == 0), stop=(k == DC - 1))
                    mm.then_inc(z_done, 1)
                if not last:
                    turn(t + 1)

                def group(g, n, src, ready, value, rows=P):
                    pe.wait_ge(ready, value)
                    if not is_first(t) or g >= 2:
                        pe.wait_ge(t_out, t * NT + g - 1)
                    for a in range(n):
                        dst = ps_t[g % 2][0:rows, a * P:(a + 1) * P]
                        if rows < P:
                            tr = nc.tensor.matmul(dst, src(a), ident[:], start=True, stop=True)
                        else:
                            tr = nc.tensor.transpose(dst, src(a), ident[:])
                    tr.then_inc(t_done, 1)

                group(0, 4, lambda a: qr[:, a, :], qr_done, t + 1, AD)
                group(1, 4, lambda a: qr[:, 4 + a, :], qr_done, t + 1, AD)
                group(2, 2, lambda a: qr[:, 8 + a, :], qr_done, t + 1, AD)
                group(3, 4, lambda a: qkv[:, a * P:(a + 1) * P], z_dve, t * per["d"] + rank[4])
                group(4, 4, lambda a: qkv[:, MIX + a * P:MIX + (a + 1) * P], z_act, t * per["a"] + rank[5])
                pe.wait_ge(vr_done, t + 1)
                if is_first(t):
                    pe.wait_ge(ws_done, 1)
                else:
                    pe.wait_ge(yc_done, t)
                for g in range(4):
                    mm = nc.tensor.matmul(ps_m[:, g * P:(g + 1) * P], wst[:, g, :], vr[:, g * P:(g + 1) * P], start=True, stop=True)
                mm.then_inc(gm_done, 1)
                group(5, 4, lambda a: yc[:, a * P:(a + 1) * P], yc_done, t + 1)

            turn(0)
            tile(0)
            with pe.Fori(1, LAT) as t:
                tile(t)
            tile(LAT, last=True)

        @block.scalar
        def _(act):
            act.wait_ge(ws_t, 1)
            nc.scalar.copy(wst, ps_m[:].rearrange("p (g q) -> p g q", g=4)).then_inc(ws_done, 1)

            def square(t):
                act.wait_ge(x_in, 16 * t + 16)
                if not is_first(t):
                    act.wait_ge(x_t, 2 * t)
                nc.scalar.activation(h[:], x[:], ACT.Square, accum_out=ss[:, 0:1]).then_inc(ss_done, 1)

            def turned(t):
                for b in range(2):
                    act.wait_ge(x_t, 2 * t + b + 1)
                    if not is_first(t) and b == 0:
                        act.wait_ge(z_done, NZ * t)
                        act.wait_ge(st_h, 16 * t)
                    nc.scalar.copy(ht[:].rearrange("p k n -> p (k n)")[:, b * 512:(b + 1) * 512], ps_x[:, b, :]).then_inc(ht_done, 1)

            def tile(t, last=False):
                act.wait_ge(z_done, t * NZ + 3)
                if not is_first(t):
                    act.wait_ge(vr_done, t)
                nc.scalar.copy(sv[:], ps_z[2][:]).then_inc(z_act, 1)
                if not is_first(t):
                    act.wait_ge(gm_done, t)
                act.wait_ge(z_act, t * per["a"] + 1)
                nc.scalar.activation(vr[:], sv[:], ACT.Square, accum_out=ss[:, 3:4]).then_inc(ssv_done, 1)
                act.wait_ge(z_done, t * NZ + 4)
                if not is_first(t):
                    act.wait_ge(yc_done, t)
                nc.scalar.copy(u[:], ps_z[0][:]).then_inc(z_act, 1)
                if not last:
                    square(t + 1)
                act.wait_ge(z_done, t * NZ + 6)
                if not is_first(t):
                    act.wait_ge(st_kv, 16 * t)
                nc.scalar.mul(qkv[:, MIX:2 * MIX], ps_z[2][:], MD ** -0.5).then_inc(z_act, 1)
                act.wait_ge(z_done, t * NZ + 8)
                if not is_first(t):
                    act.wait_ge(st_o, 16 * t)
                nc.scalar.activation(og[:], ps_z[1][:], ACT.Sigmoid).then_inc(z_act, 1)
                if not last:
                    turned(t + 1)
                outs = [(qat[:, 0:512], ps_t[0][0:AD, :], st_qa), (qat[:, 512:1024], ps_t[1][0:AD, :], None),
                        (kat[:, :, bass.ds(t * P, P)], ps_t[0][0:AD, 0:256].rearrange("p (k n) -> p k n", k=2), None),
                        (qkt[:, 0:512], ps_t[1][:], st_qk), (qkt[:, 512:1024], ps_t[0][:], None),
                        (yct[:], ps_t[1][:], st_yc)]
                for g, (dst, src, stored) in enumerate(outs):
                    act.wait_ge(t_done, t * NT + g + 1)
                    if stored is not None and not is_first(t):
                        act.wait_ge(stored, 16 * t)
                    nc.scalar.copy(dst, src).then_inc(t_out, 1)

            square(0)
            turned(0)
            tile(0)
            with act.Fori(1, LAT) as t:
                tile(t)
            tile(LAT, last=True)

        @block.vector
        def _(dve):
            s = Steps(dve, step)

            def scale_rows():
                s.link(nc.vector.scalar_tensor_tensor(out=scale1[:], in0=scale1[:], scalar=1.0, in1=gain1[:], op0=ALU.add, op1=ALU.mult))

            dve.wait_ge(rows_in, 48)
            scale_rows()

            def norm(t):
                dve.wait_ge(ss_done, t + 1)
                nc.vector.tensor_scalar(ss[:, 1:2], ss[:, 0:1], 1.0 / D, EPS, ALU.mult, ALU.add).then_inc(ms_done, 1)
                dve.wait_ge(rstd_done, t + 1)
                s.link(nc.vector.scalar_tensor_tensor(out=h[:], in0=x[:], scalar=ss[:, 2:3], in1=scale1[:], op0=ALU.mult, op1=ALU.mult))
                nc.vector.tensor_tensor(h[:], h[:], shift1[:], ALU.add).then_inc(h_done, 1)

            def tile(t, final=False):
                dve.wait_ge(z_done, t * NZ + 1)
                nc.vector.tensor_copy(qka[:, 0:512], ps_z[0][:]).then_inc(z_dve, 1)
                dve.wait_ge(z_done, t * NZ + 2)
                nc.vector.tensor_copy(cols(va[:].rearrange("p t n -> p (t n)"), t * P, P), ps_z[1][:, P:2 * P])
                if not is_first(t):
                    dve.wait_ge(st_new, 32)
                nc.vector.tensor_copy(qka[:, 512:768], ps_z[1][:, 0:256]).then_inc(z_dve, 1)
                dve.wait_ge(z_dve, t * per["d"] + 2)
                heads = qka[:, 0:640].rearrange("p (h d) -> p h d", h=10)
                if is_first(t):
                    nc.vector.tensor_copy(qr[:], heads).then_inc(qr_done, 1)
                else:
                    dve.wait_ge(rope_in, 16 * t)
                    nc.vector.tensor_tensor(rot_c[:], heads, rope[:, 0:AD].unsqueeze(1).to_broadcast([P, 10, AD]), ALU.mult)
                    split = qka[:, 0:640].rearrange("p (h a b c) -> p h a b c", h=10, a=2, b=2)
                    sine = rope[:, AD:].rearrange("p (a b c) -> p a b c", a=2, b=2)
                    for b in range(2):
                        for a in range(2):
                            last = nc.vector.tensor_tensor(rot_s[:, :, a, b, :], split[:, :, a, 1 - b, :],
                                                           sine[:, a, b, :].unsqueeze(1).to_broadcast([P, 10, 16]), ALU.mult)
                    s.link(last)
                    nc.vector.tensor_tensor(qr[:], rot_c[:], rot_s[:].rearrange("p h a b c -> p h (a b c)"), ALU.add).then_inc(qr_done, 1)
                dve.wait_ge(ssv_done, t + 1)
                nc.vector.tensor_scalar(ss[:, 4:5], ss[:, 3:4], 1.0 / MIX, EPS, ALU.mult, ALU.add).then_inc(msv_done, 1)
                dve.wait_ge(z_done, t * NZ + 5)
                nc.vector.tensor_copy(qkv[:, 0:MIX], ps_z[1][:]).then_inc(z_dve, 1)
                dve.wait_ge(rstdv_done, t + 1)
                nc.vector.tensor_scalar(vr[:], sv[:], ss[:, 5:6], None, ALU.mult).then_inc(vr_done, 1)
                if is_first(t):
                    dve.wait_ge(rows2_in, 32)
                    scale_rows()
                if not final:
                    norm(t + 1)
                dve.wait_ge(z_done, t * NZ + 7)
                if not is_first(t):
                    dve.wait_ge(st_kv, 16 * t)
                nc.vector.tensor_copy(qkv[:, 2 * MIX:], ps_z[0][:]).then_inc(z_dve, 1)
                dve.wait_ge(z_done, t * NZ + 9)
                nc.vector.tensor_tensor(cols(gates[:].rearrange("p t g -> p (t g)"), t * 16, 16), ps_z[2][:, 0:16], gb[:], ALU.add).then_inc(z_dve, 1)
                dve.wait_ge(gm_done, t + 1)
                dve.wait_ge(z_act, t * per["a"] + 2)
                for g in range(4):
                    last = nc.vector.scalar_tensor_tensor(out=yc[:, g * P:(g + 1) * P], in0=ps_m[:, g * P:(g + 1) * P],
                                                          scalar=bs[:, g:g + 1], in1=u[:, g * P:(g + 1) * P], op0=ALU.add, op1=ALU.mult)
                last.then_inc(yc_done, 1)

            norm(0)
            dve.wait_ge(small_in, 64)
            tile(0)
            with dve.Fori(0, LAT - 1) as i:
                s.enter(i, 2)
                tile(i + 1)
            s.leave(LAT - 1)
            tile(LAT, final=True)


def mlstm(nc, T, keep):
    W = MD + 1
    NCOL = TILES + 2
    PREV0 = (0, TILES)
    END0 = TILES + 1
    with nc.cleanup_on_exit(), ExitStack() as ctx:
        sb = lambda n, s, d=F32: ctx.enter_context(nc.sbuf_tensor(n, s, d))
        sem = nc.alloc_semaphore
        ident, gates, hd = keep.ident, keep.gates, keep.hd
        log_f = sb("ml_log_f", [P, TILES, 16])
        tmp = sb("ml_tmp", [P, TILES, 16])
        causal = sb("ml_causal", [P, 2, P])

        def rows_of(n):
            size = 2 * TILES * P
            return keep.big[0:MH].rearrange("h k n -> h (k n)")[:, n * size:(n + 1) * size].rearrange("h (d n) -> h d n", d=2)

        restart, li, lf, b, g, mx, m = (rows_of(n) for n in range(7))
        head_row = sb("ml_head_row", [MH, MH, P])
        prev = sb("ml_prev", [MH, 2, NCOL])
        end = sb("ml_end", [MH, 2, TILES])
        col = sb("ml_col", [P, 3, 2, TILES, MH])
        prevb = sb("ml_prevb", [P, 2, MH, NCOL])
        endb = sb("ml_endb", [P, 2, MH, TILES])
        w0 = sb("ml_w0", [P, 2, TILES, MH])
        em = sb("ml_em", [P, 2, TILES, MH])
        we0 = sb("ml_we0", [P, 2, TILES, MH])
        qkt = [sb(f"ml_qkt{d}", [P, 2 * MIX]) for d in range(2)]
        kk = [sb(f"ml_k{d}", [P, MIX]) for d in range(2)]
        v1 = [sb(f"ml_v{d}", [P, MH, W]) for d in range(2)]
        cn = [sb(f"ml_cn{d}", [P, MH, W]) for d in range(2)]
        arg = sb("ml_arg", [P, MIX])
        wt = sb("ml_wt", [P, MH, P])
        pw = sb("ml_pw", [P, MIX])
        vw = sb("ml_vw", [P, MH, W])
        ic = sb("ml_ic", [P, MH, W])
        tot = sb("ml_tot", [P, MH, W])
        den = sb("ml_den", [P, MH])
        cs = sb("ml_cs", [P, 2 * MH, P])
        cs0 = sb("ml_cs0", [P, 2 * MH, P])
        ns0 = sb("ml_ns0", [P, 2, MH])
        ps = [ctx.enter_context(nc.psum_tensor(f"ml_ps{i}", [P, 512], F32)) for i in range(2)]
        ps_i, ps_l, ps_u = (ctx.enter_context(nc.psum_tensor(f"ml_ps_{n}", [P, 2, 512], F32)) for n in "ilu")
        banks = [ps_i[:, 0, :], ps_i[:, 1, :], ps_l[:, 0, :], ps_l[:, 1, :], ps_u[:, 0, :], ps_u[:, 1, :]]

        small_in, m0_in = sem("ml_small_in"), sem("ml_m0_in")
        cell_in = [sem(f"ml_cell_in{d}") for d in range(2)]
        c0_in, n0_in, c_stored, n_stored = (sem(f"ml_{n}") for n in ("c0_in", "n0_in", "c_stored", "n_stored"))
        abs_done, exp_done, ln_done, f_done = sem("ml_abs"), sem("ml_exp"), sem("ml_ln"), sem("ml_f_done")
        rows_t, rows_out, ones_set, zero_set = sem("ml_rows_t"), sem("ml_rows_out"), sem("ml_ones"), sem("ml_zero")
        scan_done, col_t, col_out, diff_done, w_cols = (sem(f"ml_{n}") for n in ("scan", "col_t", "col_out", "diff", "w_cols"))
        mb_done, arg_done, wt_done, st_done, p_done = (sem(f"ml_{n}") for n in ("mb", "arg", "wt", "st", "p"))
        inter_done, ic_done, local_done, tot_done = (sem(f"ml_{n}") for n in ("inter", "ic", "local", "tot"))
        vw_done, upd_done, cn_done = (sem(f"ml_{n}") for n in ("vw", "upd", "cn"))
        cs_t, cs_out, c0_t, c0_out = (sem(f"ml_{n}") for n in ("cs_t", "cs_out", "c0_t", "c0_out"))
        step = sem("ml_dve_step")
        block = ctx.enter_context(nc.Block())

        def order(eng, cell, between=None, steps=None):
            cell(0, 0, 0, 0, (1, 1, 0))
            cell(1, 0, 1, 0, (2, 0, 1))
            if between is not None:
                between()
            with eng.Fori(0, LAT - 1) as i:
                if steps is not None:
                    steps.enter(i, 6)
                back = LAT - i
                eng.to_reg(back)
                cell(2 * i + 2, i + 1, 0, i + 1, (2 * i + 3, 1, back))
                cell(2 * i + 3, i + 1, 1, back, (2 * i + 4, 0, i + 2))
            if steps is not None:
                steps.leave(LAT - 1)
            cell(2 * LAT, LAT, 0, LAT, (2 * LAT + 1, 1, 1))
            cell(2 * LAT + 1, LAT, 1, 1, None)

        @block.sync
        def _(sp):
            sp.dma_start(causal[:], T["const_causal"].rearrange("d s t -> s d t")).then_inc(small_in, 16)
            sp.dma_start(restart[:].rearrange("h d n -> h (d n)"), T["const_restart"]).then_inc(small_in, 16)
            sp.dma_start(head_row[:].rearrange("h r n -> h (r n)"), T["const_head_row"]).then_inc(small_in, 16)
            sp.wait_ge(zero_set, 3)
            for d, c in ((0, 1), (1, LAT)):
                sp.dma_start(prev[:, d, c:c + 1], T["state_m"][0, 0, d].rearrange("(h a) -> h a", a=1)).then_inc(m0_in, 16)
            sp.wait_ge(ones_set, 2)

            def cell(s, n, d, t, following):
                if not isinstance(s, int) or s >= 2:
                    sp.wait_ge(upd_done, s - 1)
                sp.dma_start(qkt[d][:], row(T["qkt"], t)).then_inc(cell_in[d], 16)
                sp.dma_start(kk[d][:], row(T["kv"], t)[:, 0:MIX]).then_inc(cell_in[d], 16)
                sp.dma_start(v1[d][:, :, 0:MD], row(T["kv"], t)[:, MIX:].rearrange("p (h n) -> p h n", h=MH)).then_inc(cell_in[d], 16)

            sp.dma_start(cs0[:], T["state_C"][0, 0].rearrange("d h r e -> r (d h) e")).then_inc(c0_in, 16)
            for d in range(2):
                sp.dma_start(ns0[:, d, :], T["state_n"][0, 0, d].rearrange("h e -> e h"), allow_slow_non_contiguous=True).then_inc(n0_in, 16)

            def states():
                sp.wait_ge(cn_done, 2)
                for d in range(2):
                    sp.dma_start(T["new_n"][0, 0, d].rearrange("h e -> e h"), cn[d][:, :, MD:W].rearrange("p h a -> p (h a)"),
                                 allow_slow_non_contiguous=True).then_inc(n_stored, 16)
                    sp.dma_start(T["new_m"][0, 0, d].rearrange("(h a) -> h a", a=1), prev[:, d, END0:END0 + 1]).then_inc(c_stored, 16)
                sp.wait_ge(cs_out, 2)
                sp.dma_start(T["new_C"][0, 0].rearrange("d h r e -> r (d h) e"), cs[:]).then_inc(c_stored, 16)

            order(sp, cell, states)
            sp.wait_ge(c_stored, 48)

        @block.gpsimd
        def _(pool):
            nc.gpsimd.memset(prev[:], 0.0).then_inc(zero_set, 1)
            for d in range(2):
                nc.gpsimd.memset(cn[d][:], 0.0).then_inc(zero_set, 1)
            for d in range(2):
                nc.gpsimd.memset(v1[d][:, :, MD:W], 1.0).then_inc(ones_set, 1)

        @block.tensor
        def _(pe):
            pe.wait_ge(f_done, 1)
            k = 0
            for kind in range(2):
                for d in range(2):
                    src = gates if kind == 0 else log_f
                    if k >= 2:
                        pe.wait_ge(rows_out, k - 1)
                    for t in range(TILES):
                        c = 8 * d + 4 * kind
                        mm = nc.tensor.matmul(banks[3 * (k % 2) + t // 3][0:MH, (t % 3) * P:(t % 3 + 1) * P],
                                              src[:, t, c:c + MH], ident[:], start=True, stop=True)
                    mm.then_inc(rows_t, 1)
                    k += 1
            pe.wait_ge(scan_done, 1)
            for j, src in enumerate((g, mx, m)):
                for d in range(2):
                    for t in range(TILES):
                        c = ((j * 2 + d) * TILES + t) * MH
                        nc.tensor.matmul(ps[0][:, c:c + MH], src[:, d, t * P:(t + 1) * P], ident[0:MH, 0:MH], start=True, stop=True)
            pe.wait_ge(small_in, 48)
            for d in range(2):
                for h in range(MH):
                    c = (d * MH + h) * NCOL
                    nc.tensor.matmul(ps[1][:, c:c + NCOL], head_row[:, h, :], prev[:, d, :], start=True, stop=True)
                    c = 2 * MH * NCOL + (d * MH + h) * TILES
                    mm = nc.tensor.matmul(ps[1][:, c:c + TILES], head_row[:, h, :], end[:, d, :], start=True, stop=True)
            mm.then_inc(col_t, 1)
            pe.wait_ge(col_out, 3)

            def spread(s, d, t):
                if not (isinstance(s, int) and s == 0):
                    pe.wait_ge(arg_done, s)
                for h in range(MH):
                    mm = nc.tensor.matmul(ps[0][:, h * P:(h + 1) * P], head_row[:, h, :], cols(mx[:, d, :], t * P, P), start=True, stop=True)
                mm.then_inc(mb_done, 1)

            def cell(s, n, d, t, following):
                first = isinstance(s, int) and s == 0
                pe.wait_ge(cell_in[d], 48 * n + 48)
                if not first:
                    pe.wait_ge(p_done, s)
                for h in range(MH):
                    mm = nc.tensor.matmul(ps[1][:, h * P:(h + 1) * P], qkt[d][:, MIX + h * P:MIX + (h + 1) * P],
                                          qkt[d][:, h * P:(h + 1) * P], start=True, stop=True)
                mm.then_inc(st_done, 1)
                if isinstance(s, int) and s < 2:
                    pe.wait_ge(zero_set, 3)
                else:
                    pe.wait_ge(cn_done, s - 1)
                    pe.wait_ge(c0_out, 6)
                if not first:
                    pe.wait_ge(ic_done, s)
                for h in range(MH):
                    mm = nc.tensor.matmul(ps_i[:, h // 2, (h % 2) * W:(h % 2 + 1) * W], qkt[d][:, h * P:(h + 1) * P],
                                          cn[d][:, h, :], start=True, stop=True)
                mm.then_inc(inter_done, 1)
                if following is not None:
                    spread(*following)
                pe.wait_ge(p_done, s + 1)
                if not first:
                    pe.wait_ge(tot_done, s)
                for h in range(MH):
                    mm = nc.tensor.matmul(ps_l[:, h // 2, (h % 2) * W:(h % 2 + 1) * W], pw[:, h * P:(h + 1) * P],
                                          v1[d][:, h, :], start=True, stop=True)
                mm.then_inc(local_done, 1)
                pe.wait_ge(vw_done, s + 1)
                if not first:
                    pe.wait_ge(cn_done, s)
                for h in range(MH):
                    mm = nc.tensor.matmul(ps_u[:, h // 2, (h % 2) * W:(h % 2 + 1) * W], kk[d][:, h * P:(h + 1) * P],
                                          vw[:, h, :], start=True, stop=True)
                mm.then_inc(upd_done, 1)

            def states():
                for d in range(2):
                    pe.wait_ge(cn_done, 2)
                    for h in range(MH):
                        tr = nc.tensor.transpose(banks[d][:, h * P:(h + 1) * P], cn[d][:, h, 0:MD], ident[:])
                    tr.then_inc(cs_t, 1)
                pe.wait_ge(c0_in, 16)
                for d in range(2):
                    for h in range(MH):
                        tr = nc.tensor.transpose(banks[2 + d][:, h * P:(h + 1) * P], cs0[:, d * MH + h, :], ident[:])
                    tr.then_inc(c0_t, 1)
                pe.wait_ge(cs_out, 2)
                pe.wait_ge(c0_out, 6)

            spread(0, 0, 0)
            order(pe, cell, states)

        @block.scalar
        def _(act):
            act.wait_ge(abs_done, 1)
            nc.scalar.activation(tmp[:], log_f[:], ACT.Exp, scale=-1.0).then_inc(exp_done, 1)
            act.wait_ge(exp_done, 1)
            nc.scalar.activation(tmp[:], tmp[:], ACT.Ln, bias=1.0).then_inc(ln_done, 1)
            act.wait_ge(col_out, 3)
            act.wait_ge(diff_done, 1)
            for x in (w0, we0):
                nc.scalar.activation(x[:], x[:], ACT.Exp).then_inc(w_cols, 1)
            nc.scalar.activation(em[:], col[:, 2], ACT.Exp, scale=-1.0).then_inc(w_cols, 1)

            def cell(s, n, d, t, following):
                first = isinstance(s, int) and s == 0
                act.wait_ge(arg_done, s + 1)
                if not first:
                    act.wait_ge(vw_done, s)
                for h in range(MH):
                    bias = cols(col[:, 0, d].rearrange("p t h -> p (t h)"), t * MH + h, 1)
                    a = nc.scalar.activation(wt[:, h, :], arg[:, h * P:(h + 1) * P], ACT.Exp, bias=bias)
                a.then_inc(wt_done, 1)
                act.wait_ge(inter_done, s + 1)
                act.wait_ge(w_cols, 3)
                if not first:
                    act.wait_ge(tot_done, s)
                for h in range(MH):
                    scale = cols(w0[:, d].rearrange("p t h -> p (t h)"), t * MH + h, 1)
                    a = nc.scalar.activation(ic[:, h, :], ps_i[:, h // 2, (h % 2) * W:(h % 2 + 1) * W], ACT.Copy, scale=scale)
                a.then_inc(ic_done, 1)

            def states():
                for d in range(2):
                    act.wait_ge(cs_t, d + 1)
                    nc.scalar.copy(cs[:, d * MH:(d + 1) * MH, :].rearrange("p h n -> p (h n)"), banks[d]).then_inc(cs_out, 1)

            order(act, cell, states)

        @block.vector
        def _(dve):
            s_ = Steps(dve, step)
            nc.vector.scalar_tensor_tensor(out=log_f[:], in0=gates[:], scalar=-1.0, in1=gates[:], op0=ALU.mult, op1=ALU.max).then_inc(abs_done, 1)
            dve.wait_ge(ln_done, 1)
            s_.link(nc.vector.tensor_scalar(log_f[:], gates[:], 0.0, None, ALU.min))
            nc.vector.tensor_tensor(log_f[:], log_f[:], tmp[:], ALU.subtract).then_inc(f_done, 1)
            k = 0
            for kind in range(2):
                for d in range(2):
                    dve.wait_ge(rows_t, k + 1)
                    for j in range(3):
                        dst = (li if kind == 0 else lf)[:, d, j * 3 * P:(j + 1) * 3 * P]
                        c = nc.vector.tensor_copy(dst, banks[3 * (k % 2) + j][0:MH, 0:3 * P])
                    c.then_inc(rows_out, 1)
                    k += 1
            dve.wait_ge(rows_out, 4)
            dve.wait_ge(small_in, 48)
            flip = lambda ap: ap[:, ::-1]
            for d in range(2):
                way = (lambda ap: ap) if d == 0 else flip
                last = nc.vector.tensor_tensor_scan(way(b[:, d, :]), way(restart[:, d, :]), way(lf[:, d, :]), 0.0, ALU.mult, ALU.add)
            s_.link(last)
            s_.link(nc.vector.tensor_tensor(g[:], li[:], b[:], ALU.subtract))
            dve.wait_ge(zero_set, 1)
            dve.wait_ge(m0_in, 32)

            def scan(tiles, c_prev, c_next):
                for d in range(2):
                    way = (lambda ap: ap) if d == 0 else flip
                    row = cols(g[:, d, :], tiles[d] * P, P)
                    last = nc.vector.tensor_tensor_scan(way(cols(mx[:, d, :], tiles[d] * P, P)), way(row), way(row),
                                                        cols(prev[:, d, :], c_prev[d], 1), ALU.max, ALU.max)
                s_.link(last)
                for d in range(2):
                    e = tiles[d] * P + (P - 1 if d == 0 else 0)
                    last = nc.vector.tensor_tensor(cols(prev[:, d, :], c_next[d], 1), cols(mx[:, d, :], e, 1), cols(b[:, d, :], e, 1), ALU.add)
                s_.link(last)

            scan((0, 0), PREV0, (END0, END0))
            for i in range(LAT):
                scan((i + 1, LAT - i), (i + 1, LAT - i), (i + 2, LAT - i - 1))
            nc.vector.tensor_tensor(m[:], mx[:], b[:], ALU.add)
            for d in range(2):
                e = P - 1 if d == 0 else 0
                last = nc.vector.tensor_copy(end[:, d, :], mx[:, d, :].rearrange("h (t n) -> h t n", t=TILES)[:, :, e])
            s_.link(last)
            nc.vector.memset(prev[:, 1, 0:1], 0.0).then_inc(scan_done, 1)
            dve.wait_ge(col_t, 1)
            nc.vector.tensor_copy(col[:].rearrange("p k d t h -> p (k d t h)"), ps[0][:, 0:3 * 2 * TILES * MH]).then_inc(col_out, 1)
            nc.vector.tensor_copy(prevb[:].rearrange("p d h t -> p (d h t)"), ps[1][:, 0:2 * MH * NCOL]).then_inc(col_out, 1)
            nc.vector.tensor_copy(endb[:].rearrange("p d h t -> p (d h t)"), ps[1][:, 2 * MH * NCOL:2 * MH * (NCOL + TILES)]).then_inc(col_out, 1)
            dve.wait_ge(col_out, 3)
            for d in range(2):
                before = prevb[:, d, :, 0:TILES].rearrange("p h t -> p t h")
                nc.vector.tensor_tensor(w0[:, d], before, col[:, 1, d], ALU.subtract)
                last = nc.vector.tensor_tensor(we0[:, d], before, endb[:, d].rearrange("p h t -> p t h"), ALU.subtract)
            last.then_inc(diff_done, 1)
            dve.wait_ge(w_cols, 3)

            def exponent(s, d, t):
                dve.wait_ge(mb_done, s + 1)
                if not (isinstance(s, int) and s == 0):
                    dve.wait_ge(wt_done, s)
                nc.vector.scalar_tensor_tensor(out=arg[:].rearrange("p (h n) -> p h n", h=MH), in0=ps[0][:].rearrange("p (h n) -> p h n", h=MH),
                                               scalar=-1.0, in1=causal[:, d, :].unsqueeze(1).to_broadcast([P, MH, P]),
                                               op0=ALU.mult, op1=ALU.add).then_inc(arg_done, 1)

            def cell(s, n, d, t, following):
                first = isinstance(s, int) and s == 0
                dve.wait_ge(wt_done, s + 1)
                dve.wait_ge(st_done, s + 1)
                if not first:
                    dve.wait_ge(local_done, s)
                nc.vector.tensor_tensor(pw[:], ps[1][:], wt[:].rearrange("p h n -> p (h n)"), ALU.mult).then_inc(p_done, 1)
                dve.wait_ge(cell_in[d], 48 * n + 48)
                if not first:
                    dve.wait_ge(upd_done, s)
                e = P - 1 if d == 0 else 0
                nc.vector.tensor_tensor(vw[:], v1[d][:], wt[:, :, e:e + 1].to_broadcast([P, MH, W]), ALU.mult).then_inc(vw_done, 1)
                if following is not None:
                    exponent(*following)
                dve.wait_ge(ic_done, s + 1)
                dve.wait_ge(local_done, s + 1)
                for a in range(2):
                    last = nc.vector.tensor_tensor(tot[:, 2 * a:2 * a + 2, :].rearrange("p h n -> p (h n)"),
                                                   ic[:, 2 * a:2 * a + 2, :].rearrange("p h n -> p (h n)"), ps_l[:, a, 0:2 * W], ALU.add)
                last.then_inc(tot_done, 1)
                dve.wait_ge(tot_done, s + 1)
                raw = tot[:, :, MD:W].rearrange("p h a -> p (h a)")
                s_.link(nc.vector.scalar_tensor_tensor(out=den[:], in0=raw, scalar=-1.0, in1=raw, op0=ALU.mult, op1=ALU.max))
                s_.link(nc.vector.tensor_tensor(den[:], den[:], cols(em[:, d].rearrange("p t h -> p (t h)"), t * MH, MH), ALU.max))
                s_.link(nc.vector.reciprocal(den[:], den[:]))
                nc.vector.tensor_tensor(cols(hd[:, d], t * MIX, MIX).rearrange("p (h n) -> p h n", h=MH), tot[:, :, 0:MD],
                                        den[:].unsqueeze(2).to_broadcast([P, MH, MD]), ALU.mult)
                dve.wait_ge(upd_done, s + 1)
                for h in range(MH):
                    carry = cols(we0[:, d].rearrange("p t h -> p (t h)"), t * MH + h, 1)
                    last = nc.vector.scalar_tensor_tensor(out=cn[d][:, h, :], in0=cn[d][:, h, :], scalar=carry,
                                                          in1=ps_u[:, h // 2, (h % 2) * W:(h % 2 + 1) * W], op0=ALU.mult, op1=ALU.add)
                last.then_inc(cn_done, 1)

            def states():
                for d in range(2):
                    dve.wait_ge(c0_t, d + 1)
                    for a in range(2):
                        nc.vector.tensor_copy(cn[d][:, 2 * a:2 * a + 2, 0:MD], banks[2 + d][:, a * 256:(a + 1) * 256].rearrange(
                            "p (h n) -> p h n", h=2)).then_inc(c0_out, 1)
                dve.wait_ge(n0_in, 32)
                dve.wait_ge(n_stored, 32)
                for d in range(2):
                    nc.vector.tensor_copy(cn[d][:, :, MD:W].rearrange("p h a -> p (h a)"), ns0[:, d, :]).then_inc(c0_out, 1)
                dve.wait_ge(c0_out, 6)

            exponent(0, 0, 0)
            order(dve, cell, states, s_)


def attend(nc, T, keep):
    with nc.cleanup_on_exit(), ExitStack() as ctx:
        sb = lambda n, s, d=F32: ctx.enter_context(nc.sbuf_tensor(n, s, d))
        sem = nc.alloc_semaphore
        bank = lambda n: ctx.enter_context(nc.psum_tensor(n, [P, 512], F32))
        ident, kat, va, hd = keep.ident, keep.kat, keep.va, keep.hd
        ck = sb("at_ck", [P, AKV * AD])
        ckt = sb("at_ckt", [AD, AKV, P])
        cv = sb("at_cv", [P, AKV * AD])
        sink = sb("at_sink", [P, AH])
        gm = sb("at_gm", [P, MIX])
        half = sb("at_half", [P, MH])
        qat = [sb(f"at_qat{u}", [AD, AH * P]) for u in range(2)]
        win = [sb(f"at_win{u}", [P, 4 * P]) for u in range(2)]
        og = [sb(f"at_og{u}", [P, MIX]) for u in range(2)]
        sm = [sb(f"at_sm{u}", [P, 512]) for u in range(2)]
        pr = [sb(f"at_pr{u}", [P, 512]) for u in range(2)]
        pt = [sb(f"at_pt{u}", [P, 512]) for u in range(2)]
        top = sb("at_top", [P, AH])
        ntop = sb("at_ntop", [P, AH])
        total = sb("at_total", [P, AH])
        es = sb("at_es", [P, AH])
        rec = sb("at_rec", [P, AH])
        ya = sb("at_ya", [P, MIX])
        hs = sb("at_hs", [P, MIX])
        sq = sb("at_sq", [P, MIX])
        gain = sb("at_gain", [P, MIX])
        ms = sb("at_ms", [P, MH])
        rstd = sb("at_rstd", [P, MH])
        ym = sb("at_ym", [P, MIX])
        yt = sb("at_yt", [P, 2 * MIX])
        ps_s = [bank(f"at_ps_s{b}") for b in range(3)]
        ps_t = [bank(f"at_ps_t{b}") for b in range(2)]
        ps_o = bank("at_ps_o")
        ps_y = [bank(f"at_ps_y{b}") for b in range(2)]

        small_in, ckt_t, ckt_out, half_set = (sem(f"at_{n}") for n in ("small_in", "ckt_t", "ckt_out", "half_set"))
        tile_in = [sem(f"at_tile_in{u}") for u in range(2)]
        s_done, top_done, pr_done, pt_t, pt_done, o_done = (sem(f"at_{n}") for n in ("s", "top", "pr", "pt_t", "pt", "o"))
        diff_done, es_done, ya_done, ym_done = (sem(f"at_{n}") for n in ("diff", "es", "ya", "ym"))
        ms_done, rstd_done, y_t, y_out, stored = (sem(f"at_{n}") for n in ("ms", "rstd", "y_t", "y_out", "stored"))
        step, gain_done = sem("at_dve_step"), sem("at_gain_done")
        block = ctx.enter_context(nc.Block())
        SCALE = AD ** -0.5

        def order(eng, tile):
            tile(0, 1, 0)
            with eng.Fori(0, LAT // 2) as i:
                for u in range(2):
                    tile(2 * i + (1 + u), u, i + u)

        @block.sync
        def _(sp):
            sp.dma_start(ck[:], T["cache_k"][0, 0].rearrange("s k d -> s (k d)")).then_inc(small_in, 16)
            sp.dma_start(cv[:], T["cache_v"][0, 0].rearrange("s k d -> s (k d)")).then_inc(small_in, 16)
            sp.dma_start(sink[:], T["sink"].to_broadcast([P, AH])).then_inc(small_in, 16)
            sp.dma_start(gm[:], T["g_mlstm"].rearrange("a h n -> a (h n)").to_broadcast([P, MIX])).then_inc(small_in, 16)

            def load(t, u, n):
                if not isinstance(t, int) or t >= 2:
                    sp.wait_ge(ya_done, t - 1)
                    sp.wait_ge(ym_done, t - 1)
                sp.dma_start(qat[u][:], row(T["qat"], t)).then_inc(tile_in[u], 16)
                sp.dma_start(og[u][:], row(T["og"], t)).then_inc(tile_in[u], 16)
                if is_first(t):
                    sp.dma_start(win[u][:, 0:P], row(T["const_window"], 3)[:, 2 * P:3 * P]).then_inc(tile_in[u], 16)
                else:
                    sp.dma_start(win[u][:], row(T["const_window"], t - 1)).then_inc(tile_in[u], 16)

            def store(t):
                sp.wait_ge(y_out, 2 * t + 2)
                sp.dma_start(row(T["yt"], t), yt[:]).then_inc(stored, 16)

            load(0, 1, 0)
            load(1, 0, 0)
            for k in range(DC):
                sp.dma_start(keep.big[:, k, :], T["w_merge"][0, k * P:(k + 1) * P, :]).then_inc(keep.wm_in[k], 16)
            store(0)
            load(2, 1, 1)
            store(1)
            with sp.Fori(0, LAT // 2 - 1) as i:
                for u in range(2):
                    load(2 * i + (3 + u), u, i + 1 + u)
                    store(2 * i + (2 + u))
            store(LAT)
            sp.wait_ge(stored, 16 * TILES + 16)

        @block.gpsimd
        def _(pool):
            nc.gpsimd.memset(half[:], -0.5).then_inc(half_set, 1)
            pool.wait_ge(half_set, 1)

            pool.wait_ge(small_in, 64)

            def tile(t, u, n):
                pool.wait_ge(tile_in[u], 48 * n + 48)
                if not is_first(t):
                    pool.wait_ge(ym_done, t)
                nc.gpsimd.tensor_tensor(gain[:], gm[:], og[u][:], ALU.mult).then_inc(gain_done, 1)
                pool.wait_ge(ms_done, t + 1)
                nc.gpsimd.tensor_tensor(rstd[:], ms[:], half[:], ALU.pow).then_inc(rstd_done, 1)

            order(pool, tile)

        @block.tensor
        def _(pe):
            pe.wait_ge(small_in, 64)
            for k in range(AKV):
                tr = nc.tensor.transpose(ps_t[0][0:AD, k * P:(k + 1) * P], ck[:, k * AD:(k + 1) * AD], ident[:])
            tr.then_inc(ckt_t, 1)
            pe.wait_ge(ckt_out, 1)

            def tile(t, u, n):
                nb = 1 if is_first(t) else 4

                def scores(h):
                    if not is_first(t) or h >= 3:
                        pe.wait_ge(top_done, AH * t + h - 2)
                    q, kv = qat[u][:, h * P:(h + 1) * P], h // (AH // AKV)
                    if is_first(t):
                        mm = nc.tensor.matmul(ps_s[h % 3][:, 0:P], q, kat[:, kv, 0:P], start=True, stop=True)
                    else:
                        nc.tensor.matmul(ps_s[h % 3][:, 0:P], q, ckt[:, kv, :], start=True, stop=True)
                        mm = nc.tensor.matmul(ps_s[h % 3][:, P:4 * P], q, cols(kat[:, kv, :], (t - 1) * P, 3 * P), start=True, stop=True)
                    mm.then_inc(s_done, 1)

                def turn(h):
                    pe.wait_ge(pr_done, AH * t + h + 1)
                    if not is_first(t) or h >= 2:
                        pe.wait_ge(pt_done, AH * t + h - 1)
                    for b in range(nb):
                        tr = nc.tensor.transpose(ps_t[h % 2][:, b * P:(b + 1) * P], pr[h % 2][:, b * P:(b + 1) * P], ident[:])
                    tr.then_inc(pt_t, 1)

                def values(h):
                    pe.wait_ge(pt_done, AH * t + h + 1)
                    if h == 0 and not is_first(t):
                        pe.wait_ge(ya_done, t)
                    kv = h // (AH // AKV)
                    for b in range(nb):
                        if is_first(t):
                            v = va[:, 0, kv * AD:(kv + 1) * AD]
                        elif b == 0:
                            v = cv[:, kv * AD:(kv + 1) * AD]
                        else:
                            v = cols(va[:].rearrange("p t n -> p (t n)"), (t + (b - 2)) * P + kv * AD, AD)
                        mm = nc.tensor.matmul(ps_o[:, h * AD:(h + 1) * AD], pt[h % 2][:, b * P:(b + 1) * P], v, start=(b == 0), stop=(b == nb - 1))
                    mm.then_inc(o_done, 1)

                pe.wait_ge(tile_in[u], 48 * n + 48)
                scores(0)
                scores(1)
                if not is_first(t):
                    turn_y(t - 1)
                for h in range(AH):
                    if h + 2 < AH:
                        scores(h + 2)
                    turn(h)
                    if h >= 1:
                        values(h - 1)
                values(AH - 1)

            def turn_y(t):
                for k, (y, ready) in enumerate(((ym, ym_done), (ya, ya_done))):
                    pe.wait_ge(ready, t + 1)
                    for a in range(4):
                        tr = nc.tensor.transpose(ps_y[k][:, a * P:(a + 1) * P], y[:, a * P:(a + 1) * P], ident[:])
                    tr.then_inc(y_t, 1)

            order(pe, tile)
            turn_y(LAT)

        @block.scalar
        def _(act):
            act.wait_ge(ckt_t, 1)
            nc.scalar.copy(ckt[:].rearrange("p k n -> p (k n)"), ps_t[0][0:AD, 0:2 * P]).then_inc(ckt_out, 1)

            def tile(t, u, n):
                w = P if is_first(t) else 4 * P
                for h in range(AH):
                    act.wait_ge(top_done, AH * t + h + 1)
                    if not is_first(t) or h >= 2:
                        act.wait_ge(pt_t, AH * t + h - 1)
                    nc.scalar.activation(pr[h % 2][:, 0:w], sm[h % 2][:, 0:w], ACT.Exp, bias=ntop[:, h:h + 1], scale=SCALE,
                                         accum_out=total[:, h:h + 1]).then_inc(pr_done, 1)
                    if h == 0 and not is_first(t):
                        outs(t - 1)
                    if h % 2 == 1:
                        act.wait_ge(pt_t, AH * t + h)
                        if not is_first(t) or h >= 2:
                            act.wait_ge(o_done, AH * t + h - 2)
                        nc.scalar.copy(pt[0][:, 0:w], ps_t[0][:, 0:w]).then_inc(pt_done, 1)
                        act.wait_ge(pt_t, AH * t + h + 1)
                        if not is_first(t) or h >= 2:
                            act.wait_ge(o_done, AH * t + h - 1)
                        nc.scalar.copy(pt[1][:, 0:w], ps_t[1][:, 0:w]).then_inc(pt_done, 1)
                act.wait_ge(diff_done, t + 1)
                nc.scalar.activation(es[:], es[:], ACT.Exp).then_inc(es_done, 1)

            def outs(t):
                for k in range(2):
                    act.wait_ge(y_t, 2 * t + k + 1)
                    act.wait_ge(stored, 16 * t + 16)
                    nc.scalar.copy(yt[:, k * MIX:(k + 1) * MIX], ps_y[k][:]).then_inc(y_out, 1)

            order(act, tile)
            outs(LAT)

        @block.vector
        def _(dve):
            s_ = Steps(dve, step)
            nc.vector.memset(total[:], 0.0).then_inc(stored, 16)
            dve.wait_ge(small_in, 64)

            def tile(t, u, n):
                w = P if is_first(t) else 4 * P
                dve.wait_ge(tile_in[u], 48 * n + 48)
                for h in range(AH):
                    if not is_first(t) or h >= 2:
                        dve.wait_ge(pr_done, AH * t + h - 1)
                    dve.wait_ge(s_done, AH * t + h + 1)
                    s_.link(nc.vector.tensor_tensor(sm[h % 2][:, 0:w], ps_s[h % 3][:, 0:w], win[u][:, 0:w], ALU.add))
                    s_.link(nc.vector.tensor_reduce(top[:, h:h + 1], sm[h % 2][:, 0:w], AX_X, ALU.max))
                    s_.link(nc.vector.scalar_tensor_tensor(out=top[:, h:h + 1], in0=top[:, h:h + 1], scalar=SCALE, in1=sink[:, h:h + 1],
                                                           op0=ALU.mult, op1=ALU.max))
                    nc.vector.tensor_scalar(ntop[:, h:h + 1], top[:, h:h + 1], -1.0, None, ALU.mult).then_inc(top_done, 1)
                nc.vector.tensor_tensor(es[:], sink[:], top[:], ALU.subtract).then_inc(diff_done, 1)
                hf, hb = (cols(hd[:, d], t * MIX, MIX) for d in range(2))
                if not is_first(t):
                    dve.wait_ge(y_t, 2 * t)
                s_.link(nc.vector.tensor_tensor(hs[:], hf, hb, ALU.add))
                s_.link(nc.vector.tensor_tensor(sq[:], hs[:], hs[:], ALU.mult))
                s_.link(nc.vector.tensor_reduce(ms[:], sq[:].rearrange("p (h n) -> p h n", h=MH), AX_X, ALU.add))
                nc.vector.tensor_scalar(ms[:], ms[:], 1.0 / MD, EPS, ALU.mult, ALU.add).then_inc(ms_done, 1)
                dve.wait_ge(rstd_done, t + 1)
                s_.link(nc.vector.tensor_tensor(hs[:].rearrange("p (h n) -> p h n", h=MH), hs[:].rearrange("p (h n) -> p h n", h=MH),
                                                rstd[:].unsqueeze(2).to_broadcast([P, MH, MD]), ALU.mult))
                dve.wait_ge(gain_done, t + 1)
                nc.vector.tensor_tensor(ym[:], hs[:], gain[:], ALU.mult).then_inc(ym_done, 1)
                dve.wait_ge(es_done, t + 1)
                s_.link(nc.vector.tensor_tensor(rec[:], es[:], total[:], ALU.add))
                s_.link(nc.vector.reciprocal(rec[:], rec[:]))
                dve.wait_ge(o_done, AH * t + AH)
                nc.vector.tensor_tensor(ya[:].rearrange("p (h n) -> p h n", h=AH), ps_o[:].rearrange("p (h n) -> p h n", h=AH),
                                        rec[:].unsqueeze(2).to_broadcast([P, AH, AD]), ALU.mult).then_inc(ya_done, 1)

            tile(0, 1, 0)
            PER = 4 + 3 * AH + 2
            with dve.Fori(0, LAT // 2) as i:
                s_.enter(i, 2 * PER)
                for u in range(2):
                    tile(2 * i + (1 + u), u, i + u)
            s_.leave(LAT // 2)


def pairs(eng, tile):
    tile(0, 1, 0)
    with eng.Fori(0, LAT // 2) as i:
        for u in range(2):
            tile(2 * i + (1 + u), u, i + u)


def merge(nc, T, keep):
    NBR = 3
    NJ = 2 * NBR
    with nc.cleanup_on_exit(), ExitStack() as ctx:
        sb = lambda n, s, d=F32: ctx.enter_context(nc.sbuf_tensor(n, s, d))
        sem = nc.alloc_semaphore
        bank = lambda n: ctx.enter_context(nc.psum_tensor(n, [P, 512], F32))
        ident = keep.ident
        wm = keep.big
        wb = sb("mg_wb", [P, NBR, 4, D])
        bm = sb("mg_bm", [P, NBR * D])
        ht = [sb(f"mg_ht{u}", [P, DC, P]) for u in range(2)]
        yt = [sb(f"mg_yt{u}", [P, 3, 4, P]) for u in range(2)]
        gsum = [sb(f"mg_gsum{u}", [P, 512]) for u in range(2)]
        gate = [sb(f"mg_gate{u}", [P, 512]) for u in range(2)]
        merged = sb("mg_merged", [P, D])
        mt = sb("mg_mt", [P, D])
        ps_g = [bank(f"mg_ps_g{b}") for b in range(3)]
        ps_p = [bank(f"mg_ps_p{b}") for b in range(2)]
        ps_t = [bank(f"mg_ps_t{b}") for b in range(2)]
        wb_in = [sem(f"mg_wb_in{n}") for n in range(NBR)]
        bm_in = sem("mg_bm_in")
        tile_in = [sem(f"mg_tile_in{u}") for u in range(2)]
        g_done, p_done, sum_done, gate_done, prod_done = (sem(f"mg_{n}") for n in ("g", "p", "sum", "gate", "prod"))
        m_t, m_out, stored = (sem(f"mg_{n}") for n in ("m_t", "m_out", "stored"))
        step = sem("mg_dve_step")
        block = ctx.enter_context(nc.Block())

        @block.sync
        def _(sp):
            def load(t, u, n):
                if not isinstance(t, int) or t >= 2:
                    sp.wait_ge(p_done, NJ * (t - 1))
                sp.dma_start(ht[u][:].rearrange("p k n -> p (k n)"), row(T["ht"], t)).then_inc(tile_in[u], 16)
                flat = yt[u][:].rearrange("p b k n -> p b (k n)")
                sp.dma_start(flat[:, 0, :], row(T["yt"], t)[:, 0:MIX]).then_inc(tile_in[u], 16)
                sp.dma_start(flat[:, 1, :], row(T["yct"], t)).then_inc(tile_in[u], 16)
                sp.dma_start(flat[:, 2, :], row(T["yt"], t)[:, MIX:]).then_inc(tile_in[u], 16)

            def store(t):
                sp.wait_ge(m_out, 2 * t + 2)
                sp.dma_start(row(T["mt"], t), mt[:]).then_inc(stored, 16)

            load(0, 1, 0)
            sp.dma_start(bm[:], T["b_merge"].to_broadcast([P, NBR * D])).then_inc(bm_in, 16)
            for n in range(NBR):
                sp.dma_start(wb[:, n], T["w_branch"][0, n].rearrange("(k p) d -> p k d", p=P)).then_inc(wb_in[n], 16)
            load(1, 0, 0)
            load(2, 1, 1)
            store(0)
            with sp.Fori(0, LAT // 2 - 1) as i:
                for u in range(2):
                    load(2 * i + (3 + u), u, i + 1 + u)
                    store(2 * i + (1 + u))
            store(LAT - 1)
            sp.wait_ge(g_done, NJ * LAT + 2)
            sp.dma_start(wm[:, :, 0:D], T["w_out"][0].rearrange("(k p) n -> p k n", p=P)).then_inc(keep.wo_in, 16)
            sp.wait_ge(g_done, NJ * LAT + 4)
            sp.dma_start(wm[:, :, D:2 * D], T["w_peer_q"][0, :, 0:D].rearrange("(k p) n -> p k n", p=P)).then_inc(keep.wq_in, 16)
            store(LAT)
            sp.wait_ge(stored, 16 * TILES)

        @block.tensor
        def _(pe):
            def turn(t):
                pe.wait_ge(prod_done, NJ * t + NJ)
                if not is_first(t):
                    pe.wait_ge(m_out, 2 * t)
                for k in range(DC):
                    tr = nc.tensor.transpose(ps_t[k // 4][:, (k % 4) * P:(k % 4 + 1) * P], merged[:, k * P:(k + 1) * P], ident[:])
                    if k % 4 == 3:
                        tr.then_inc(m_t, 1)

            def tile(t, u, n):
                pe.wait_ge(tile_in[u], 64 * n + 64)
                for j in range(NJ):
                    br, half = j // 2, j % 2
                    if not is_first(t) or j >= 3:
                        pe.wait_ge(sum_done, NJ * t + j - 2)
                    for k in range(DC):
                        if is_first(t) and j == 0:
                            pe.wait_ge(keep.wm_in[k], 16)
                        mm = nc.tensor.matmul(ps_g[j % 3][:], ht[u][:, k, :], wm[:, k, j * 512:(j + 1) * 512], start=(k == 0), stop=(k == DC - 1))
                    mm.then_inc(g_done, 1)
                    if not is_first(t) or j >= 2:
                        pe.wait_ge(prod_done, NJ * t + j - 1)
                    if is_first(t) and half == 0:
                        pe.wait_ge(wb_in[br], 16)
                    for k in range(4):
                        mm = nc.tensor.matmul(ps_p[j % 2][:], yt[u][:, br, k, :], wb[:, br, k, half * 512:(half + 1) * 512], start=(k == 0), stop=(k == 3))
                    mm.then_inc(p_done, 1)
                    if j == 0 and not is_first(t):
                        turn(t - 1)

            pairs(pe, tile)
            turn(LAT)

        @block.scalar
        def _(act):
            def out(t):
                for b in range(2):
                    act.wait_ge(m_t, 2 * t + b + 1)
                    if b == 0 and not is_first(t):
                        act.wait_ge(stored, 16 * t)
                    nc.scalar.copy(mt[:, b * 512:(b + 1) * 512], ps_t[b][:]).then_inc(m_out, 1)

            def tile(t, u, n):
                for j in range(NJ):
                    act.wait_ge(sum_done, NJ * t + j + 1)
                    if not is_first(t) or j >= 2:
                        act.wait_ge(prod_done, NJ * t + j - 1)
                    nc.scalar.activation(gate[j % 2][:], gsum[j % 2][:], ACT.Sigmoid).then_inc(gate_done, 1)
                    if j == 0 and not is_first(t):
                        out(t - 1)

            pairs(act, tile)
            out(LAT)

        @block.vector
        def _(dve):
            s_ = Steps(dve, step)
            dve.wait_ge(bm_in, 16)

            def tile(t, u, n):
                def add_bias(j):
                    dve.wait_ge(g_done, NJ * t + j + 1)
                    if not is_first(t) or j >= 2:
                        dve.wait_ge(gate_done, NJ * t + j - 1)
                    nc.vector.tensor_tensor(gsum[j % 2][:], ps_g[j % 3][:], bm[:, j * 512:(j + 1) * 512], ALU.add).then_inc(sum_done, 1)

                def add_product(j):
                    dve.wait_ge(gate_done, NJ * t + j + 1)
                    dve.wait_ge(p_done, NJ * t + j + 1)
                    into = merged[:, (j % 2) * 512:(j % 2 + 1) * 512]
                    if j == 0 and not is_first(t):
                        dve.wait_ge(m_t, 2 * t)
                    if j < 2:
                        nc.vector.tensor_tensor(into, gate[j % 2][:], ps_p[j % 2][:], ALU.mult).then_inc(prod_done, 1)
                    else:
                        s_.link(nc.vector.tensor_tensor(gate[j % 2][:], gate[j % 2][:], ps_p[j % 2][:], ALU.mult))
                        nc.vector.tensor_tensor(into, into, gate[j % 2][:], ALU.add).then_inc(prod_done, 1)

                for j in range(NJ):
                    add_bias(j)
                    if j >= 1:
                        add_product(j - 1)
                add_product(NJ - 1)

            tile(0, 1, 0)
            with dve.Fori(0, LAT // 2) as i:
                s_.enter(i, 2 * (NJ - 2))
                for u in range(2):
                    tile(2 * i + (1 + u), u, i + u)
            s_.leave(LAT // 2)


TOP16 = 5
PICK = 2 * TOP16 + 6


class Picker:

    def __init__(self, nc, sb, name, iota):
        self.nc, self.iota = nc, iota
        self.hold = sb(f"{name}_hold", [P, 1])
        self.v16 = sb(f"{name}_v16", [P, 2, TOPK])
        self.i16 = sb(f"{name}_i16", [P, 2, TOPK], U32)
        self.i16f = sb(f"{name}_i16f", [P, 2, TOPK])
        self.cand = sb(f"{name}_cand", [P, TOPK, TOPK])
        self.vs = sb(f"{name}_vs", [P, TOPK])
        self.ic = sb(f"{name}_ic", [P, TOPK], U32)
        self.part = sb(f"{name}_part", [P, 2, TOPK], U32)
        self.partf = sb(f"{name}_partf", [P, 2, TOPK])
        self.oh = sb(f"{name}_oh", [P, 2, TOPK, TOPK])
        self.e12 = sb(f"{name}_e12", [P, 2, TOPK])

    def top16(self, link, rows, values, indices):
        nc = self.nc
        carry = lambda: nc.vector.memset(self.hold[:], 0.0)
        for r, v in zip(rows, values):
            last = nc.vector.max(v[:, 0:8], r)
        link(last)
        carry()
        for r, v, i in zip(rows, values, indices):
            last = nc.vector.max_index(i[:, 0:8], v[:, 0:8], r)
        link(last)
        carry()
        for r, v in zip(rows, values):
            last = nc.vector.match_replace(r, v[:, 0:8], r, BIG)
        link(last)
        carry()
        for r, v in zip(rows, values):
            last = nc.vector.max(v[:, 8:16], r)
        link(last)
        carry()
        for r, v, i in zip(rows, values, indices):
            last = nc.vector.max_index(i[:, 8:16], v[:, 8:16], r)
        link(last)

    def pick(self, dve, step, number, halves, shifted, ids, picked, picked_value):
        nc = self.nc
        count = [0]

        def link(ins):
            ins.then_inc(step, 1)
            count[0] += 1
            dve.wait_ge(step, number * PICK + count[0])

        nc.vector.memset(self.hold[:], 0.0)
        self.top16(link, halves, [self.v16[:, a, :] for a in range(2)], [self.i16[:, a, :] for a in range(2)])
        nc.vector.tensor_copy(self.i16f[:], self.i16[:])
        square = [P, TOPK, TOPK]
        link(nc.vector.tensor_tensor(self.cand[:], self.v16[:, 0, :].unsqueeze(2).to_broadcast(square),
                                     self.v16[:, 1, :].unsqueeze(1).to_broadcast(square), ALU.add))
        nc.vector.memset(self.hold[:], 0.0)
        self.top16(link, [self.cand[:].rearrange("p a b -> p (a b)")], [self.vs[:]], [self.ic[:]])
        nc.vector.tensor_tensor(shifted, self.vs[:], self.vs[:, 0:1].to_broadcast([P, TOPK]), ALU.subtract)
        nc.vector.tensor_scalar(self.part[:, 0, :], self.ic[:], 4, None, ALU.logical_shift_right)
        link(nc.vector.tensor_scalar(self.part[:, 1, :], self.ic[:], TOPK - 1, None, ALU.bitwise_and))
        link(nc.vector.tensor_copy(self.partf[:], self.part[:]))
        both = [P, 2, TOPK, TOPK]
        link(nc.vector.tensor_tensor(self.oh[:], self.partf[:].unsqueeze(3).to_broadcast(both),
                                     self.iota[:].unsqueeze(1).unsqueeze(1).to_broadcast(both), ALU.is_equal))
        link(nc.vector.tensor_tensor(self.oh[:], self.oh[:], self.i16f[:].unsqueeze(2).to_broadcast(both), ALU.mult))
        link(nc.vector.tensor_reduce(self.e12[:], self.oh[:], AX_X, ALU.add))
        assert count[0] == PICK, count
        nc.vector.scalar_tensor_tensor(out=ids, in0=self.e12[:, 0, :], scalar=float(P), in1=self.e12[:, 1, :],
                                       op0=ALU.mult, op1=ALU.add).then_inc(picked, 1)
        dve.wait_ge(picked, picked_value)
        nc.vector.memset(self.hold[:], 0.0)


def sum_to_one(nc, s_, ex, tot, gw):
    heads = ex.rearrange("p (h k) -> p h k", k=TOPK)
    s_.link(nc.vector.tensor_reduce(tot[:], heads, AX_X, ALU.add))
    s_.link(nc.vector.reciprocal(tot[:], tot[:]))
    s_.link(nc.vector.tensor_tensor(gw[:], heads, tot[:].unsqueeze(2).to_broadcast([P, PH, TOPK]), ALU.mult))


def route(nc, T, keep):
    with nc.cleanup_on_exit(), ExitStack() as ctx:
        sb = lambda n, s, d=F32: ctx.enter_context(nc.sbuf_tensor(n, s, d))
        sem = nc.alloc_semaphore
        bank = lambda n: ctx.enter_context(nc.psum_tensor(n, [P, 512], F32))
        ident = keep.ident
        wo, wq = keep.big[:, :, 0:D], keep.big[:, :, D:]
        keyt = sb("rt_keyt", [P, HP, P])
        gate1, scale2, shift2, gain2 = (sb(f"rt_{n}", [P, D]) for n in ("gate1", "scale2", "shift2", "gain2"))
        mt = sb("rt_mt", [P, DC, P])
        x = sb("rt_x", [P, D])
        x1 = sb("rt_x1", [P, D])
        h2 = sb("rt_h2", [P, D])
        h2p = sb("rt_h2p", [P, D])
        R = 8
        U_TURNS = PH // 2
        ring = sb("rt_ring", [P, R, D])
        idx = [sb(f"rt_idx{b}", [P, TOPK], U32) for b in range(2)]
        heads = sb("rt_heads", [P, 2, 2, P])
        dots, gelu, wts = (sb(f"rt_{n}", [P, PICKS]) for n in ("dots", "gelu", "wts"))
        tot, gw = sb("rt_tot", [P, PH]), sb("rt_gw", [P, PH, TOPK])
        picker = Picker(nc, sb, "rt_pk", keep.iota)
        h2t = sb("rt_h2t", [P, DC, P])
        qt = sb("rt_qt", [P, HP, P])
        sc = sb("rt_sc", [P, HP, P])
        ss = sb("rt_ss", [P, 3])
        half = sb("rt_half", [P, 1])
        ps_y = [bank(f"rt_ps_y{b}") for b in range(2)]
        ps_x = [bank(f"rt_ps_x{b}") for b in range(2)]
        ps_q = [bank(f"rt_ps_q{b}") for b in range(2)]
        ps_s = [bank(f"rt_ps_s{b}") for b in range(2)]
        keys_in, rows_in, rows2_in = (sem(f"rt_{n}") for n in ("keys_in", "rows_in", "rows2_in"))
        mt_in, x_in, half_set, key_t, key_out = (sem(f"rt_{n}") for n in ("mt_in", "x_in", "half_set", "key_t", "key_out"))
        y_done, x1_done, ms_done, rstd_done, h2_done = (sem(f"rt_{n}") for n in ("y", "x1", "ms", "rstd", "h2"))
        h2_t, h2t_done, q_done, qt_done, s_done, sc_done = (sem(f"rt_{n}") for n in ("h2_t", "h2t", "q", "qt", "sco", "sc"))
        st_x1, st_h2, st_sc, step = (sem(f"rt_{n}") for n in ("st_x1", "st_h2", "st_sc", "step"))
        iota_in, pick_step = sem("rt_iota_in"), sem("rt_pick_step")
        head_in = [sem(f"rt_head_in{b}") for b in range(2)]
        rows_at = [sem(f"rt_rows_at{k}") for k in range(R)]
        picked, copied, waited, used, dots_done, gelu_done, acc_set = (
            sem(f"rt_{n}") for n in ("picked", "copied", "waited", "used", "dots", "gelu", "acc_set"))
        block = ctx.enter_context(nc.Block())

        @block.sync
        def _(sp):
            sp.dma_start(mt[:].rearrange("p k n -> p (k n)"), row(T["mt"], 0)).then_inc(mt_in, 16)
            sp.dma_start(x[:], T["x_prompt"][0]).then_inc(x_in, 16)
            for dst, c in ((gate1, 2), (scale2, 4), (shift2, 3)):
                sp.dma_start(dst[:], T["mod"][0:1, c * D:(c + 1) * D].to_broadcast([P, D])).then_inc(rows_in, 16)
            sp.dma_start(gain2[:], T["g_norm2"].to_broadcast([P, D])).then_inc(rows_in, 16)
            sp.dma_start(qt[:], T["peer_keys"][0].rearrange("h a k d -> k (h a) d")).then_inc(keys_in, 16)
            sp.dma_start(keep.iota[:], T["const_iota"]).then_inc(iota_in, 16)

            sp.dma_start(keep.big[:, :, 2 * D:], T["w_peer_q"][0, :, D:].rearrange("(k p) n -> p k n", p=P)).then_inc(keep.wq_in, 16)
            x_lat = T["x_sample"][0].rearrange("(t p) d -> t p d", p=P)

            def norm_tile(t, h2):
                last = isinstance(t, int) and t == LAT
                if not last:
                    sp.wait_ge(y_done, 2 * t + 2)
                    sp.dma_start(mt[:].rearrange("p k n -> p (k n)"), row(T["mt"], t + 1)).then_inc(mt_in, 16)
                sp.wait_ge(x1_done, 2 * t + 2)
                sp.dma_start(row(T["x1"], t), x1[:]).then_inc(st_x1, 16)
                if not last:
                    sp.wait_ge(ms_done, t + 1)
                    sp.dma_start(x[:], row(x_lat, t)).then_inc(x_in, 16)
                sp.wait_ge(h2_done, t + 1)
                sp.dma_start(row(T["h2"], t), h2[:]).then_inc(st_h2, 16)

            norm_tile(0, h2p)
            for dst, c in ((gate1, 2), (scale2, 4), (shift2, 3)):
                sp.dma_start(dst[:], T["mod"][1:2, c * D:(c + 1) * D].to_broadcast([P, D])).then_inc(rows2_in, 16)
            with sp.Fori(0, LAT - 1) as i:
                norm_tile(i + 1, h2)
            norm_tile(LAT, h2)
            for s in (st_x1, st_h2):
                sp.wait_ge(s, 16 * TILES)

        @block.gpsimd
        def _(pool):
            nc.gpsimd.memset(half[:], -0.5).then_inc(half_set, 1)
            pool.wait_ge(half_set, 1)

            def rsqrt(t):
                pool.wait_ge(ms_done, t + 1)
                nc.gpsimd.tensor_tensor(ss[:, 2:3], ss[:, 1:2], half[:], ALU.pow).then_inc(rstd_done, 1)

            def load_head(s, b):
                if not isinstance(s, int) or s >= 2:
                    pool.wait_ge(picked, s - 1)
                    pool.sem_inc(waited, 1)
                pool.dma_start(heads[:, b].rearrange("p a n -> p (a n)"), row(T["sc"].rearrange("t h p n -> (t h) p n"), s)).then_inc(head_in[b], 16)

            def gather(table, g, b, q):
                pool.wait_ge(used, q * TOPK + 1)
                nc.gpsimd.tensor_copy(idx[b][:], cols(keep.ids, g * TOPK, TOPK)).then_inc(copied, 1)
                pool.wait_ge(copied, q + 1)
                pool.sem_inc(waited, 1)
                for k in range(TOPK):
                    if k > 0:
                        pool.wait_ge(used, q * TOPK + (k + 1))
                        pool.sem_inc(waited, 1)
                    nc.gpsimd.indirect_dma_start(ring[:, k % R, :], None, table[0], bass.IndirectOffsetOnAxis(
                        ap=idx[b][:, k:k + 1], axis=0)).then_inc(rows_at[k % R], 16)

            rsqrt(0)
            rsqrt(1)
            pool.wait_ge(st_sc, 16)
            load_head(0, 0)
            load_head(1, 1)
            with pool.Fori(0, U_TURNS) as i:
                rsqrt(i + 2)
                pool.wait_ge(st_sc, 16 * i + 32)
                for b in range(2):
                    load_head(2 * i + (b + 2), b)
                    gather(T["peer_u"], 2 * i + b, b, 2 * i + b)

            def v_group(g, b):
                if not isinstance(g, int) or g < PH - 2:
                    load_head(g + (PH + 2), b)
                gather(T["peer_v"], g, b, g + PH)

            def v_turn(t, g):
                rsqrt(t)
                for b in range(2):
                    v_group(g + b, b)

            first = U_TURNS + 2
            pool.wait_ge(st_sc, 128)
            with pool.Fori(0, LAT - first + 1) as i:
                v_turn(i + first, 2 * i)
            for b in range(2):
                v_group(PH - 2 + b, b)

        @block.tensor
        def _(pe):
            def project_out(t):
                pe.wait_ge(mt_in, 16 * t + 16)
                if is_first(t):
                    pe.wait_ge(keep.wo_in, 16)
                for b in range(2):
                    if not is_first(t):
                        pe.wait_ge(x1_done, 2 * t + b - 1)
                    for k in range(DC):
                        mm = nc.tensor.matmul(ps_y[b][:], mt[:, k, :], wo[:, k, b * 512:(b + 1) * 512], start=(k == 0), stop=(k == DC - 1))
                    mm.then_inc(y_done, 1)

            def queries(t, h2):
                pe.wait_ge(h2_done, t + 1)
                if not is_first(t):
                    pe.wait_ge(h2t_done, 2 * t)
                for k in range(DC):
                    tr = nc.tensor.transpose(ps_x[k // 4][:, (k % 4) * P:(k % 4 + 1) * P], h2[:, k * P:(k + 1) * P], ident[:])
                    if k % 4 == 3:
                        tr.then_inc(h2_t, 1)
                pe.wait_ge(h2t_done, 2 * t + 2)

                def query(b):
                    if not is_first(t) or b >= 2:
                        pe.wait_ge(qt_done, 4 * t + b - 1)
                    for a in range(4):
                        for k in range(DC):
                            mm = nc.tensor.matmul(ps_q[b % 2][:, a * P:(a + 1) * P], wq[:, k, (4 * b + a) * P:(4 * b + a + 1) * P],
                                                  h2t[:, k, :], start=(k == 0), stop=(k == DC - 1))
                    mm.then_inc(q_done, 1)

                def score(b):
                    pe.wait_ge(qt_done, 4 * t + b + 1)
                    if not is_first(t) or b >= 2:
                        pe.wait_ge(sc_done, 4 * t + b - 1)
                    for a in range(4):
                        mm = nc.tensor.matmul(ps_s[b % 2][:, a * P:(a + 1) * P], qt[:, 4 * b + a, :], keyt[:, 4 * b + a, :], start=True, stop=True)
                    mm.then_inc(s_done, 1)

                query(0)
                for b in range(1, 4):
                    query(b)
                    score(b - 1)
                score(3)

            project_out(0)
            pe.wait_ge(keys_in, 16)
            pe.wait_ge(half_set, 1)
            for b in range(4):
                if b >= 2:
                    pe.wait_ge(key_out, b - 1)
                for a in range(4):
                    tr = nc.tensor.transpose(ps_q[b % 2][:, a * P:(a + 1) * P], qt[:, 4 * b + a, :], ident[:])
                tr.then_inc(key_t, 1)
            project_out(1)
            pe.wait_ge(keep.wq_in, 32)
            pe.wait_ge(key_out, 4)
            queries(0, h2p)
            with pe.Fori(0, LAT - 1) as i:
                project_out(i + 2)
                queries(i + 1, h2)
            queries(LAT, h2)

        @block.scalar
        def _(act):
            for b in range(4):
                act.wait_ge(key_t, b + 1)
                nc.scalar.copy(keyt[:, 4 * b:4 * b + 4, :].rearrange("p a n -> p (a n)"), ps_q[b % 2][:]).then_inc(key_out, 1)

            def outs(t):
                for b in range(2):
                    act.wait_ge(h2_t, 2 * t + b + 1)
                    if not is_first(t) and b == 0:
                        act.wait_ge(q_done, 4 * t)
                    nc.scalar.copy(h2t[:, 4 * b:4 * b + 4, :].rearrange("p a n -> p (a n)"), ps_x[b][:]).then_inc(h2t_done, 1)

                def query(b):
                    act.wait_ge(q_done, 4 * t + b + 1)
                    if is_first(t):
                        act.wait_ge(key_t, 4)
                    else:
                        act.wait_ge(s_done, 4 * (t - 1) + b + 1)
                    nc.scalar.copy(qt[:, 4 * b:4 * b + 4, :].rearrange("p a n -> p (a n)"), ps_q[b % 2][:]).then_inc(qt_done, 1)

                def score(b):
                    act.wait_ge(s_done, 4 * t + b + 1)
                    nc.scalar.copy(sc[:, 4 * b:4 * b + 4, :].rearrange("p a n -> p (a n)"), ps_s[b % 2][:]).then_inc(sc_done, 1)
                    if not is_first(t) or b > 0:
                        act.wait_ge(st_sc, 64 * t + 16 * b)
                    act.wait_ge(sc_done, 4 * t + b + 1)
                    act.dma_start(T["sc"][bass.ds(t, 1), 2 * b:2 * b + 2].rearrange("a h p n -> p (a h) n"),
                                  sc[:, 4 * b:4 * b + 4, :].rearrange("p (h a) n -> p h (a n)", a=2)).then_inc(st_sc, 16)

                query(0)
                for b in range(1, 4):
                    query(b)
                    score(b - 1)
                score(3)

            outs(0)
            with act.Fori(1, U_TURNS + 2) as t:
                outs(t)
            act.wait_ge(dots_done, 1)
            nc.scalar.activation(keep.ex[:, 0:PICKS], keep.ex[:, 0:PICKS], ACT.Exp)
            nc.scalar.activation(gelu[:], dots[:], ACT.Gelu_apprx_tanh).then_inc(gelu_done, 1)
            with act.Fori(U_TURNS + 2, TILES) as t:
                outs(t)
            act.wait_ge(st_sc, 64 * TILES)

        @block.vector
        def _(dve):
            s_ = Steps(dve, step)

            def norm(t, h2):
                if not is_first(t):
                    dve.wait_ge(st_x1, 16 * t)
                dve.wait_ge(x_in, 16 * t + 16)
                for b in range(2):
                    half_ = slice(b * 512, (b + 1) * 512)
                    dve.wait_ge(y_done, 2 * t + b + 1)
                    s_.link(nc.vector.tensor_tensor(x1[:, half_], ps_y[b][:], gate1[:, half_], ALU.mult))
                    nc.vector.tensor_tensor(x1[:, half_], x1[:, half_], x[:, half_], ALU.add).then_inc(x1_done, 1)
                dve.wait_ge(x1_done, 2 * t + 2)
                s_.link(nc.vector.scalar_tensor_tensor(out=x[:], in0=x1[:], scalar=1.0, in1=x1[:], op0=ALU.mult, op1=ALU.mult,
                                                       accum_out=ss[:, 0:1]))
                nc.vector.tensor_scalar(ss[:, 1:2], ss[:, 0:1], 1.0 / D, EPS, ALU.mult, ALU.add).then_inc(ms_done, 1)
                dve.wait_ge(rstd_done, t + 1)
                if not is_first(t):
                    dve.wait_ge(h2_t, 2 * t)
                    dve.wait_ge(st_h2, 16 * t)
                s_.link(nc.vector.scalar_tensor_tensor(out=h2[:], in0=x1[:], scalar=ss[:, 2:3], in1=scale2[:], op0=ALU.mult, op1=ALU.mult))
                nc.vector.tensor_tensor(h2[:], h2[:], shift2[:], ALU.add).then_inc(h2_done, 1)

            NORM = 4

            def scale_rows():
                s_.link(nc.vector.scalar_tensor_tensor(out=scale2[:], in0=scale2[:], scalar=1.0, in1=gain2[:], op0=ALU.add, op1=ALU.mult))

            def pick(s, b, round_):
                dve.wait_ge(head_in[b], 16 * round_ + 16)
                picker.pick(dve, pick_step, s, [heads[:, b, a, :] for a in range(2)],
                            cols(keep.ex, s * TOPK, TOPK), cols(keep.ids, s * TOPK, TOPK), picked, s + 1)

            def u_group(g):
                for k in range(TOPK):
                    dve.wait_ge(rows_at[k % R], 16 * (2 * g) + 16 * (k // R + 1))
                    nc.vector.scalar_tensor_tensor(out=ring[:, k % R, :], in0=ring[:, k % R, :], scalar=1.0, in1=h2p[:], op0=ALU.mult, op1=ALU.mult,
                                                   accum_out=cols(dots, g * TOPK + k, 1)).then_inc(used, 1)

            def v_group(g):
                for k in range(TOPK):
                    dve.wait_ge(rows_at[k % R], 16 * (2 * g) + 16 * (2 * PH + k // R + 1))
                    dve.wait_ge(used, g * TOPK + (PICKS + R + k))
                    nc.vector.scalar_tensor_tensor(out=keep.acc[:], in0=ring[:, k % R, :], scalar=cols(wts, g * TOPK + k, 1),
                                                   in1=keep.acc[:], op0=ALU.mult, op1=ALU.add).then_inc(used, 1)

            nc.vector.memset(keep.acc[:], 0.0).then_inc(used, R)
            dve.wait_ge(rows_in, 64)
            scale_rows()
            norm(0, h2p)
            dve.wait_ge(rows2_in, 48)
            scale_rows()
            norm(1, h2)
            dve.wait_ge(iota_in, 16)
            pick(0, 0, 0)
            with dve.Fori(0, U_TURNS) as i:
                s_.enter(i, NORM)
                norm(i + 2, h2)
                for b in range(2):
                    pick(2 * i + (b + 1), (b + 1) % 2, i + b)
                    u_group(2 * i + b)
            s_.leave(U_TURNS)
            dve.wait_ge(used, PICKS + R)
            nc.vector.memset(tot[:], 0.0).then_inc(dots_done, 1)
            t, g = U_TURNS + 2, 0
            norm(t, h2)
            pick(PH + 1, 1, PH // 2)
            dve.wait_ge(dots_done, 1)
            dve.wait_ge(gelu_done, 1)
            sum_to_one(nc, s_, keep.ex[:, 0:PICKS], tot, gw)
            s_.link(nc.vector.tensor_tensor(wts[:], gelu[:], gw[:].rearrange("p h k -> p (h k)"), ALU.mult))
            v_group(0)
            pick(PH + 2, 0, PH // 2 + 1)
            v_group(1)
            turns = LAT - t
            with dve.Fori(0, turns) as i:
                s_.enter(i, NORM)
                norm(i + (t + 1), h2)
                for b in range(2):
                    pick(2 * i + (PH + 3 + b), (b + 1) % 2, i + (PH // 2 + 1 + b))
                    v_group(2 * i + (2 + b))
            s_.leave(turns)
            pick(2 * PH - 1, 1, PH - 1)
            for b in range(2):
                v_group(PH - 2 + b)


def experts(nc, T, keep):
    R = TOPK
    NG = PH
    ND = 10
    NPE = R - ND
    with nc.cleanup_on_exit(), ExitStack() as ctx:
        sb = lambda n, s, d=F32: ctx.enter_context(nc.sbuf_tensor(n, s, d))
        sem = nc.alloc_semaphore
        ident = keep.ident
        ring_u = sb("ex_ring_u", [P, R, D])
        ring_v = sb("ex_ring_v", [P, R, D])
        sc = sb("ex_sc", [P, HP * P])
        h2 = [sb(f"ex_h2{u}", [P, D]) for u in range(2)]
        x1 = [sb(f"ex_x1{u}", [P, D]) for u in range(2)]
        idx_u, idx_v = ([sb(f"ex_idx_{n}{b}", [P, R], U32) for b in range(2)] for n in "uv")
        hold = sb("ex_hold", [P, 4])
        zero = sb("ex_zero", [P, P])
        diag = sb("ex_diag", [P, NPE, P])
        gate2, gfin = sb("ex_gate2", [P, D]), sb("ex_gfin", [P, D])
        head = sb("ex_head", [P, 2, P])
        picker = Picker(nc, sb, "ex_pk", keep.iota)
        tot = sb("ex_tot", [P, PH])
        gw = sb("ex_gw", [P, PH, TOPK])
        dots = sb("ex_dots", [P, PICKS])
        gelu = sb("ex_gelu", [P, PICKS])
        wts = sb("ex_wts", [P, PICKS])
        acc = [sb(f"ex_acc{a}", [P, D]) for a in range(2)]
        x2 = sb("ex_x2", [P, D])
        square = sb("ex_square", [P, D])
        y = sb("ex_y", [P, D])
        ss = sb("ex_ss", [P, 5])
        ps = ctx.enter_context(nc.psum_tensor("ex_ps", [P, 2, 512], F32))
        rows_in, rows2_in = sem("ex_rows_in"), sem("ex_rows2_in")
        tile_in = [sem(f"ex_tile_in{u}") for u in range(2)]
        sc_in, picked, sc_used = sem("ex_sc_in"), sem("ex_picked"), sem("ex_sc_used")
        u_in, v_in = [sem(f"ex_u_in{k}") for k in range(R)], [sem(f"ex_v_in{k}") for k in range(R)]
        used_u, used_vd, used_vp, copied_u, copied_v, waited = (
            sem(f"ex_{n}") for n in ("used_u", "used_vd", "used_vp", "copied_u", "copied_v", "waited"))
        ex_in, ex_done, dots_done, gelu_done, wts_done, diag_done, pv_done, x2_done, ss_done, ms_done, root_done, y_done, stored, step = (
            sem(f"ex_{n}") for n in ("ex_in", "ex", "dots", "gelu", "wts", "diag", "pv", "x2", "ss", "ms", "root", "y", "stored", "step"))
        zero_set, step2 = sem("ex_zero_set"), sem("ex_step2")
        block = ctx.enter_context(nc.Block())

        def order(eng, tile):
            with eng.Fori(0, LAT // 2 - 1) as i:
                for u in range(2):
                    tile(2 * i + (1 + u), u, i + u)
            for u in range(2):
                tile(LAT - 1 + u, u, LAT // 2 - 1 + u)

        half_of = lambda u: (1 - u) * PICKS

        @block.sync
        def _(sp):
            def load(t, u):
                if not isinstance(t, int) or t >= 2:
                    sp.wait_ge(y_done, t - 1)
                sp.dma_start(h2[u][:], row(T["h2"], t)).then_inc(tile_in[u], 16)
                sp.dma_start(x1[u][:], row(T["x1"], t)).then_inc(tile_in[u], 16)

            def load_scores(t):
                if not isinstance(t, int) or t >= 3:
                    sp.wait_ge(sc_used, NG * (t - 2))
                sp.dma_start(sc[:].rearrange("p (h n) -> p h n", h=PH),
                             T["sc"][bass.ds(t, 1)].rearrange("a h p n -> p (a h) n")).then_inc(sc_in, 16)

            y_lat = T["y_sample"][0].rearrange("(t p) d -> t p d", p=P)

            def store(t):
                sp.wait_ge(y_done, t + 1)
                sp.dma_start(row(y_lat, t - 1), y[:]).then_inc(stored, 16)

            load(1, 0)
            load(0, 1)
            sp.dma_start(gate2[:], T["mod"][0:1, 5 * D:6 * D].to_broadcast([P, D])).then_inc(rows_in, 16)
            sp.dma_start(gfin[:], T["g_final"].rearrange("(a d) -> a d", a=1).to_broadcast([P, D])).then_inc(rows_in, 16)
            load_scores(2)
            sp.wait_ge(y_done, 1)
            sp.dma_start(T["y_prompt"][0], y[:]).then_inc(stored, 16)
            sp.dma_start(gate2[:], T["mod"][1:2, 5 * D:6 * D].to_broadcast([P, D])).then_inc(rows2_in, 16)
            load(2, 1)
            with sp.Fori(0, LAT // 2 - 1) as i:
                for u in range(2):
                    load_scores(2 * i + (3 + u))
                    store(2 * i + (1 + u))
                    load(2 * i + (3 + u), u)
            store(LAT - 1)
            store(LAT)
            sp.wait_ge(stored, 16 * TILES)

        @block.gpsimd
        def _(pool):
            nc.gpsimd.memset(zero[:], 0.0).then_inc(zero_set, 1)

            def tile(t, u, n):
                def group(g2, b, table, ring, idx, arrived, copied, waits):
                    q = (t - 1) * NG + g2 * 2 + b
                    for used, first, per in waits:
                        pool.wait_ge(used, q * per + 1)
                    nc.gpsimd.tensor_copy(idx[b][:], cols(keep.ids, g2 * (2 * R) + (half_of(u) + b * R), R)).then_inc(copied, 1)
                    pool.wait_ge(copied, q + 1)
                    pool.sem_inc(waited, 1)
                    for k in range(R):
                        used, first, per = [w for w in waits if k >= w[1]][-1]
                        if k > first:
                            pool.wait_ge(used, q * per + (k - first + 1))
                            pool.sem_inc(waited, 1)
                        nc.gpsimd.indirect_dma_start(ring[:, k, :], None, table[0], bass.IndirectOffsetOnAxis(
                            ap=idx[b][:, k:k + 1], axis=0)).then_inc(arrived[k], 16)

                with pool.Fori(0, NG // 2) as g2:
                    for b in range(2):
                        pool.wait_ge(picked, (t - 1) * NG + g2 * 2 + (b + 1))
                        group(g2, b, T["peer_u"], ring_u, idx_u, u_in, copied_u, ((used_u, 0, R),))
                with pool.Fori(0, NG // 2) as g2:
                    for b in range(2):
                        group(g2, b, T["peer_v"], ring_v, idx_v, v_in, copied_v, ((used_vd, 0, ND), (used_vp, ND, NPE)))

            order(pool, tile)

        @block.tensor
        def _(pe):
            pe.wait_ge(zero_set, 1)
            pe.wait_ge(rows_in, 32)

            def tile(t, u, n):
                pe.wait_ge(x2_done, t)
                for b in range(2):
                    nc.tensor.matmul(ps[:, b, :], zero[:], gfin[:, b * 512:(b + 1) * 512], start=True, stop=False)
                with pe.Fori(0, NG) as g:
                    q = (t - 1) * NG + g
                    for j in range(NPE):
                        pe.wait_ge(diag_done, q * NPE + (j + 1))
                        pe.wait_ge(v_in[ND + j], 16 * q + 16)
                        for b in range(2):
                            mm = nc.tensor.matmul(ps[:, b, :], diag[:, j, :], ring_v[:, ND + j, b * 512:(b + 1) * 512], start=False, stop=False)
                        mm.then_inc(used_vp, 1)
                for b in range(2):
                    mm = nc.tensor.matmul(ps[:, b, :], zero[:], gfin[:, b * 512:(b + 1) * 512], start=False, stop=True)
                mm.then_inc(pv_done, 1)

            order(pe, tile)

        @block.scalar
        def _(act):
            def exponentials(half):
                nc.scalar.activation(cols(keep.ex, half, PICKS), cols(keep.ex, half, PICKS), ACT.Exp).then_inc(ex_done, 1)

            def root(t):
                act.wait_ge(x2_done, t + 1)
                nc.scalar.activation(square[:], x2[:], ACT.Square, accum_out=ss[:, 0:1]).then_inc(ss_done, 1)
                act.wait_ge(ms_done, t + 1)
                nc.scalar.activation(ss[:, 2:3], ss[:, 1:2], ACT.Sqrt).then_inc(root_done, 1)

            exponentials(half_of(0))
            root(0)

            def tile(t, u, n):
                act.wait_ge(dots_done, t)
                nc.scalar.activation(gelu[:], dots[:], ACT.Gelu_apprx_tanh).then_inc(gelu_done, 1)
                act.wait_ge(wts_done, t)
                nc.scalar.copy(ss[:, 3:4], ss[:, 2:3])
                with act.Fori(0, NG) as g:
                    q = (t - 1) * NG + g
                    for j in range(NPE):
                        act.wait_ge(used_vp, q * NPE + (j + 1))
                        nc.scalar.activation(diag[:, j, :], ident[:], ACT.Copy, scale=cols(wts, g * R + (ND + j), 1)).then_inc(diag_done, 1)
                if not (isinstance(t, int) and t == LAT):
                    act.wait_ge(ex_in, t)
                    exponentials(half_of(1 - u))
                root(t)

            order(act, tile)

        @block.vector
        def _(dve):
            nc.vector.memset(hold[:, 0:1], 0.0).then_inc(used_u, R)
            nc.vector.memset(ss[:], 1.0).then_inc(used_vd, ND)
            nc.vector.memset(gw[:, 0, 0:1], 0.0).then_inc(used_vp, NPE)
            nc.vector.memset(hold[:, 1:2], 0.0).then_inc(picked, NG)

            def pick(t, u, g):
                done = (t - 2) * NG + g
                dve.wait_ge(sc_in, 16 * (t - 1))
                nc.vector.tensor_copy(head[:].rearrange("p a n -> p (a n)"), cols(sc, g * (2 * P), 2 * P)).then_inc(sc_used, 1)
                dve.wait_ge(sc_used, done + 1)
                picker.pick(dve, step, done, [head[:, a, :] for a in range(2)], cols(keep.ex, g * TOPK + half_of(u), TOPK),
                            cols(keep.ids, g * TOPK + half_of(u), TOPK), picked, done + (NG + 1))

            s_ = Steps(dve, step2)

            def finish(t, u, total):
                s_.link(nc.vector.tensor_tensor(total[:], total[:], gate2[:], ALU.mult))
                nc.vector.tensor_tensor(x2[:], total[:], x1[u][:], ALU.add).then_inc(x2_done, 1)
                dve.wait_ge(ss_done, t + 1)
                nc.vector.tensor_scalar(ss[:, 1:2], ss[:, 0:1], 1.0 / D, EPS, ALU.mult, ALU.add).then_inc(ms_done, 1)
                dve.wait_ge(root_done, t + 1)
                s_.link(nc.vector.reciprocal(ss[:, 3:4], ss[:, 2:3]))
                s_.link(nc.vector.scalar_tensor_tensor(out=ss[:, 4:5], in0=ss[:, 3:4], scalar=ss[:, 1:2], in1=ss[:, 3:4], op0=ALU.mult, op1=ALU.mult))
                s_.link(nc.vector.tensor_scalar(ss[:, 4:5], ss[:, 4:5], -0.5, 1.5, ALU.mult, ALU.add))
                s_.link(nc.vector.tensor_tensor(ss[:, 4:5], ss[:, 4:5], ss[:, 3:4], ALU.mult))
                if not is_first(t):
                    dve.wait_ge(stored, 16 * t)
                nc.vector.scalar_tensor_tensor(out=y[:], in0=x2[:], scalar=ss[:, 4:5], in1=gfin[:], op0=ALU.mult, op1=ALU.mult).then_inc(y_done, 1)

            def tile(t, u, n):
                last_tile = isinstance(t, int) and t == LAT
                dve.wait_ge(tile_in[u], 32 * n + 32)
                nc.vector.memset(hold[:, 2:3], 0.0)
                with dve.Fori(0, NG) as g:
                    q = (t - 1) * NG + g
                    for k in range(R):
                        dve.wait_ge(u_in[k], 16 * q + 16)
                        nc.vector.scalar_tensor_tensor(out=ring_u[:, k, :], in0=ring_u[:, k, :], scalar=1.0, in1=h2[u][:], op0=ALU.mult, op1=ALU.mult,
                                                       accum_out=cols(dots, g * R + k, 1)).then_inc(used_u, 1)
                dve.wait_ge(used_u, t * PICKS + R)
                nc.vector.memset(acc[0][:], 0.0).then_inc(dots_done, 1)
                s_.link(nc.vector.memset(acc[1][:], 0.0))
                dve.wait_ge(ex_done, t)
                sum_to_one(nc, s_, cols(keep.ex, half_of(u), PICKS), tot, gw)
                dve.wait_ge(gelu_done, t)
                nc.vector.tensor_tensor(wts[:], gelu[:], gw[:].rearrange("p h k -> p (h k)"), ALU.mult).then_inc(wts_done, 1)
                dve.wait_ge(wts_done, t)
                nc.vector.memset(hold[:, 3:4], 0.0)
                with dve.Fori(0, NG) as g:
                    q = (t - 1) * NG + g
                    for k in range(ND):
                        dve.wait_ge(v_in[k], 16 * q + 16)
                        dve.wait_ge(used_vd, q * ND + (k + ND - 1))
                        nc.vector.scalar_tensor_tensor(out=acc[k % 2][:], in0=ring_v[:, k, :], scalar=cols(wts, g * R + k, 1),
                                                       in1=acc[k % 2][:], op0=ALU.mult, op1=ALU.add).then_inc(used_vd, 1)
                    if not last_tile:
                        pick(t + 1, 1 - u, g)
                dve.wait_ge(used_vd, t * (NG * ND) + ND)
                if not last_tile:
                    nc.vector.memset(hold[:, 1:2], 0.0).then_inc(ex_in, 1)
                s_.link(nc.vector.tensor_tensor(acc[0][:], acc[0][:], acc[1][:], ALU.add))
                dve.wait_ge(pv_done, t)
                s_.link(nc.vector.tensor_tensor(acc[0][:], acc[0][:], ps[:].rearrange("p b n -> p (b n)"), ALU.add))
                finish(t, u, acc[0])

            dve.wait_ge(tile_in[1], 32)
            dve.wait_ge(rows_in, 32)
            finish(0, 1, keep.acc)
            dve.wait_ge(rows2_in, 16)
            PER = 11
            with dve.Fori(0, LAT // 2 - 1) as i:
                s_.enter(i, 2 * PER)
                for u in range(2):
                    tile(2 * i + (1 + u), u, i + u)
            s_.leave(LAT // 2 - 1)
            for u in range(2):
                tile(LAT - 1 + u, u, LAT // 2 - 1 + u)


SCRATCH = {"mod": [2, 6 * D], "ht": [TILES, P, D], "kv": [TILES, P, 2 * MIX], "og": [TILES, P, MIX],
           "qat": [TILES, AD, AH * P], "qkt": [TILES, P, 2 * MIX], "yct": [TILES, P, MIX],
           "yt": [TILES, P, 2 * MIX], "mt": [TILES, P, D], "x1": [TILES, P, D], "h2": [TILES, P, D],
           "sc": [TILES, PH, P, 2 * P]}


class Keep:
    pass


def trunk(nc, ins, outs, phases=99, debug=False):
    kind = {"kind": "ExternalOutput"} if debug else {}
    scratch = {name: nc.dram_tensor(f"s_{name}", shape, F32, **kind).ap() for name, shape in SCRATCH.items()}
    T = {**ins, **outs, **scratch}
    keep = Keep()
    with nc.cleanup_on_exit(), ExitStack() as ctx:
        keep.w_in, keep.wm_in = ([nc.alloc_semaphore(f"{n}{k}") for k in range(DC)] for n in ("w_in", "w_merge_in"))
        keep.wo_in, keep.wq_in = nc.alloc_semaphore("w_out_in"), nc.alloc_semaphore("w_peer_q_in")
        keep.ident = ctx.enter_context(nc.sbuf_tensor("ident", [P, P], F32))
        keep.iota = ctx.enter_context(nc.sbuf_tensor("iota", [P, TOPK], F32))
        keep.ids = ctx.enter_context(nc.sbuf_tensor("ids", [P, 2 * PICKS], U32))
        keep.ex = ctx.enter_context(nc.sbuf_tensor("ex", [P, 2 * PICKS], F32))
        keep.acc = ctx.enter_context(nc.sbuf_tensor("prompt_sum", [P, D], F32))
        with ExitStack() as weights:
            keep.big = weights.enter_context(nc.sbuf_tensor("big", [P, DC, 3 * D], F32))
            with ExitStack() as mixer:
                keep.gates = mixer.enter_context(nc.sbuf_tensor("gates", [P, TILES, 16], F32))
                keep.kat = mixer.enter_context(nc.sbuf_tensor("kat", [AD, AKV, (TILES + 1) * P], F32))
                keep.va = mixer.enter_context(nc.sbuf_tensor("va", [P, TILES + 1, P], F32))
                with ExitStack() as inner:
                    keep.w_us = inner.enter_context(nc.sbuf_tensor("w_us", [P, DC, 2 * MIX], F32))
                    modulate(nc, T, keep)
                    project(nc, T, keep)
                keep.hd = mixer.enter_context(nc.sbuf_tensor("hd", [P, 2, TILES * MIX], F32))
                mlstm(nc, T, keep)
                attend(nc, T, keep)
            merge(nc, T, keep)
            route(nc, T, keep)
        experts(nc, T, keep)


_INS = ['x_prompt', 'x_sample', 'cache_k', 'cache_v', 'state_C', 'state_n', 'state_m', 'c', 'c_ctx',
        'w_ada', 'b_ada', 'g_norm1', 'g_norm2', 'w_in', 'b_gates_m', 'g_mlstm', 'w_spatial', 'b_spatial', 'sink',
        'w_branch', 'w_merge', 'b_merge', 'w_out', 'w_peer_q', 'peer_keys', 'peer_u', 'peer_v', 'g_final']
_OUTS = [("y_prompt", (1, P, D)), ("y_sample", (1, LAT * P, D)), ("new_k", (1, 1, P, AKV, AD)), ("new_v", (1, 1, P, AKV, AD)),
         ("new_C", (1, 1, 2, MH, MD, MD)), ("new_n", (1, 1, 2, MH, MD)), ("new_m", (1, 1, 2, MH))]


def kernel(**inputs):
    import concourse.bacc as bacc
    from concourse.bass_utils import run_bass_kernel_spmd

    nc = bacc.Bacc("TRN2", target_bir_lowering=False, num_devices=1)
    arrays, ins, outs = {}, {}, {}
    given = {name: np.ascontiguousarray(inputs[name]) for name in _INS}
    for name, a in {**given, **host_constants()}.items():
        arrays[f"in_{name}"] = a
        ins[name] = nc.dram_tensor(f"in_{name}", a.shape, mybir.dt.from_np(a.dtype), kind="ExternalInput").ap()
    for name, shape in _OUTS:
        outs[name] = nc.dram_tensor(f"out_{name}", shape, F32, kind="ExternalOutput").ap()
    trunk(nc, ins, outs)
    r = run_bass_kernel_spmd(nc, [arrays], core_ids=[0])
    return tuple(r.results[0][f"out_{name}"] for name, _ in _OUTS)
```
